# Optimizing a Trainium2 kernel written in Bass

```python
import math
import jax
import jax.numpy as jnp
from jax import lax
import numpy as np

D_MODEL = 1024
BATCH = 1
SEQ = 512
DEPTH = 1

GRID_W = 64
CTX_LEN = 256
HY_WIDTH = 512
ML_HEADS = 4
ML_DK = 64
ML_DV = 128
ML_WIDTH = ML_HEADS * ML_DV
MIX_WIDTH = HY_WIDTH + ML_WIDTH
HY_COLS = 3 * HY_WIDTH
QK_COLS = ML_HEADS * ML_DK
N_GATES = 4 * ML_HEADS
ML_COLS = 2 * QK_COLS + 2 * ML_WIDTH + N_GATES
IN_COLS = HY_COLS + ML_COLS
SHORT_W = 3
FILTER_EMB = 33
FILTER_HIDDEN = 64
DECAY_TARGET = 1e-2
FAST_DECAY_PCT = 0.3
SLOW_DECAY_PCT = 1.5
CHUNK = 128
GATE_CAP = 15.0
N_EXPERTS = 16
EXPERT_FF = 2048
CAP_FACTOR = 2
EPS = 1e-6

kernel_name = 'hyena_mlstm_ec_moe_diffusion_block'

def rmsnorm(x, g):
    xf = x.astype(jnp.float32)
    y = xf * lax.rsqrt(jnp.mean(xf * xf, axis=-1, keepdims=True) + EPS)
    return (y * g.astype(jnp.float32)).astype(x.dtype)

def modulated_norm(x, g, shift, scale):
    return rmsnorm(x, g) * (1 + scale) + shift

def pos_embed_2d(rows, cols, dim):
    quarter = dim // 4
    omega = 1.0 / (10000.0 ** (jnp.arange(quarter, dtype=jnp.float32) / quarter))

    def emb1d(n):
        ang = jnp.arange(n, dtype=jnp.float32)[:, None] * omega[None, :]
        return jnp.concatenate([jnp.sin(ang), jnp.cos(ang)], axis=-1)

    er = emb1d(rows)
    ec = emb1d(cols)
    pe = jnp.concatenate([jnp.broadcast_to(er[:, None, :], (rows, cols, dim // 2)),
                          jnp.broadcast_to(ec[None, :, :], (rows, cols, dim // 2))], axis=-1)
    return pe.reshape(rows * cols, dim)

def short_conv(z, w, b):
    L = z.shape[1]
    zp = jnp.pad(z, ((0, 0), (1, 1), (0, 0)))
    return zp[:, :L] * w[0] + zp[:, 1:L + 1] * w[1] + zp[:, 2:] * w[2] + b

def hyena_filter(L, w1, b1, w2, b2, w3, b3, w4, freq):
    f32 = jnp.float32
    t = jnp.linspace(0.0, 1.0, L, dtype=f32)[:, None]
    bands = (FILTER_EMB - 1) // 2
    w = 2.0 * math.pi * jnp.arange(L, dtype=f32) / L
    f = jnp.linspace(1e-4, bands - 1, bands, dtype=f32)
    ang = w[:, None] * f[None, :]
    z = jnp.concatenate([t, jnp.cos(ang), -jnp.sin(ang)], axis=-1)
    h = jnp.sin(freq * (z @ w1 + b1))
    h = jnp.sin(freq * (h @ w2 + b2))
    h = jnp.sin(freq * (h @ w3 + b3))
    h = (h @ w4).astype(f32)
    min_decay = math.log(DECAY_TARGET) / SLOW_DECAY_PCT
    max_decay = math.log(DECAY_TARGET) / FAST_DECAY_PCT
    deltas = jnp.linspace(min_decay, max_decay, HY_WIDTH, dtype=f32)
    decay = jnp.exp(-t * jnp.abs(deltas)[None, :])
    h_fwd = h[:, :HY_WIDTH] * decay
    h_bwd = h[:, HY_WIDTH:] * decay
    return jnp.concatenate([h_fwd, jnp.zeros((1, HY_WIDTH), f32), h_bwd[:0:-1]], axis=0)

def long_conv(v, k_circ, bias):
    L = v.shape[1]
    vf = v.astype(jnp.float32)
    spec = jnp.fft.rfft(vf, n=2 * L, axis=1) * jnp.fft.rfft(k_circ, axis=0)[None]
    y = jnp.fft.irfft(spec, n=2 * L, axis=1)[:, :L]
    return (y + vf * bias.astype(jnp.float32)).astype(v.dtype)

def hyena_group(z_hy, conv_w, conv_b, fw1, fb1, fw2, fb2, fw3, fb3, fw4, ffreq, hy_bias):
    z = short_conv(z_hy, conv_w, conv_b)
    x0, x1, v = jnp.split(z, 3, axis=-1)
    k_circ = hyena_filter(z.shape[1], fw1, fb1, fw2, fb2, fw3, fb3, fw4, ffreq)
    return x0 * long_conv(v * x1, k_circ, hy_bias)

def mlstm_chunkwise(q, k, v, i_pre, logf, state):
    f32 = jnp.float32
    q, k, v = q.astype(f32), k.astype(f32), v.astype(f32)
    B, H, L, _ = q.shape
    nc = L // CHUNK

    def to_chunks(a):
        return jnp.moveaxis(a.reshape(a.shape[:2] + (nc, CHUNK) + a.shape[3:]), 2, 0)

    causal = jnp.tril(jnp.ones((CHUNK, CHUNK), dtype=bool))

    def step(carry, inp):
        C, n, m = carry
        qt, kt, vt, it, ft = inp
        b = jnp.cumsum(ft, axis=-1)
        dlog = jnp.where(causal, b[..., :, None] - b[..., None, :] + it[..., None, :], -jnp.inf)
        m_inter = b + m[..., None]
        m_t = jnp.maximum(m_inter, jnp.max(dlog, axis=-1))
        w_intra = jnp.exp(dlog - m_t[..., None])
        w_inter = jnp.exp(m_inter - m_t)
        s = jnp.einsum('bhtk,bhsk->bhts', qt, kt) * w_intra
        num = jnp.einsum('bhts,bhsv->bhtv', s, vt) + w_inter[..., None] * jnp.einsum('bhtk,bhkv->bhtv', qt, C)
        den = jnp.sum(s, axis=-1) + w_inter * jnp.einsum('bhtk,bhk->bht', qt, n)
        h = num / jnp.maximum(jnp.abs(den), jnp.exp(-m_t))[..., None]
        b_end = b[..., -1]
        g = b_end[..., None] - b + it
        m_new = jnp.maximum(b_end + m, jnp.max(g, axis=-1))
        w_s = jnp.exp(g - m_new[..., None])
        w_c = jnp.exp(b_end + m - m_new)
        C_new = w_c[..., None, None] * C + jnp.einsum('bhs,bhsk,bhsv->bhkv', w_s, kt, vt)
        n_new = w_c[..., None] * n + jnp.einsum('bhs,bhsk->bhk', w_s, kt)
        return (C_new, n_new, m_new), h

    state, hc = lax.scan(step, state, (to_chunks(q), to_chunks(k), to_chunks(v), to_chunks(i_pre), to_chunks(logf)))
    h = jnp.moveaxis(hc, 0, 2).reshape(B, H, L, v.shape[-1])
    return h, state

def mlstm_inputs(zm, gate_b):
    B, L, _ = zm.shape
    q, k, v, o, gates = jnp.split(
        zm, [QK_COLS, 2 * QK_COLS, 2 * QK_COLS + ML_WIDTH, 2 * QK_COLS + 2 * ML_WIDTH], axis=-1)

    def heads(a, d):
        return a.reshape(B, L, ML_HEADS, d).transpose(0, 2, 1, 3)

    q = heads(q, ML_DK) * (ML_DK ** -0.5)
    k = heads(k, ML_DK)
    v = heads(v, ML_DV)
    g = gates.astype(jnp.float32) + gate_b.astype(jnp.float32)
    g = GATE_CAP * jnp.tanh(g / GATE_CAP)
    g = g.reshape(B, L, 4, ML_HEADS).transpose(2, 0, 3, 1)
    return q, k, v, o, g[0], jax.nn.log_sigmoid(g[1]), g[2], jax.nn.log_sigmoid(g[3])

def mlstm_output(h, o, norm_g):
    B, H, L, dv = h.shape
    hn = h * lax.rsqrt(jnp.mean(h * h, axis=-1, keepdims=True) + EPS)
    hn = hn.transpose(0, 2, 1, 3).reshape(B, L, H * dv) * norm_g.astype(jnp.float32)
    return (hn * jax.nn.sigmoid(o.astype(jnp.float32))).astype(o.dtype)

def mlstm_group(z_lat, z_ctx, gate_b, norm_g):
    q, k, v, o, i_f, lf_f, i_b, lf_b = mlstm_inputs(z_lat, gate_b)
    qc, kc, vc, oc, ic_f, lfc_f, ic_b, lfc_b = mlstm_inputs(z_ctx, gate_b)
    B = z_lat.shape[0]
    zero = (jnp.zeros((B, ML_HEADS, ML_DK, ML_DV), jnp.float32),
            jnp.zeros((B, ML_HEADS, ML_DK), jnp.float32),
            jnp.zeros((B, ML_HEADS), jnp.float32))

    def rev(a):
        return jnp.flip(a, axis=2)

    hc_f, st_f = mlstm_chunkwise(qc, kc, vc, ic_f, lfc_f, zero)
    hc_b, st_b = mlstm_chunkwise(rev(qc), rev(kc), rev(vc), rev(ic_b), rev(lfc_b), zero)
    h_f, _ = mlstm_chunkwise(q, k, v, i_f, lf_f, st_f)
    h_b, _ = mlstm_chunkwise(rev(q), rev(k), rev(v), rev(i_b), rev(lf_b), st_b)
    y_lat = mlstm_output(h_f + rev(h_b), o, norm_g)
    return y_lat, hc_f + rev(hc_b), oc

def ec_moe(h, w_router, w_gate, w_up, w_down):
    B, L, D = h.shape
    cap = CAP_FACTOR * L // N_EXPERTS
    aff = jax.nn.softmax((h @ w_router).astype(jnp.float32), axis=-1)
    g, idx = lax.top_k(jnp.swapaxes(aff, 1, 2), cap)
    xs = jax.vmap(lambda hb, ib: hb[ib])(h, idx)
    a = jnp.einsum('becd,edf->becf', xs, w_gate)
    u = jnp.einsum('becd,edf->becf', xs, w_up)
    ye = jnp.einsum('becf,efd->becd', jax.nn.silu(a) * u, w_down) * g[..., None].astype(h.dtype)
    return jax.vmap(lambda ib, yb: jnp.zeros((L, D), yb.dtype).at[ib.reshape(-1)].add(yb.reshape(-1, D)))(idx, ye)

def setup_inputs(seed: int = 0) -> dict:
    key = jax.random.key(seed)
    ks = iter(jax.random.split(key, 40))

    def nrm(shape, scale):
        return scale * jax.random.normal(next(ks), shape, jnp.float32)

    D, E, F, H = D_MODEL, N_EXPERTS, EXPERT_FF, ML_HEADS
    f_bias = jnp.linspace(3.0, 6.0, H, dtype=jnp.float32)[None, :]
    ml_gate_b = jnp.concatenate([nrm((DEPTH, H), 0.1), f_bias + nrm((DEPTH, H), 0.1),
                                 nrm((DEPTH, H), 0.1), f_bias + nrm((DEPTH, H), 0.1)], axis=-1)
    return {
        'x': nrm((BATCH, SEQ, D), 1.0),
        'c': nrm((BATCH, D), 1.0),
        'ctx': nrm((BATCH, CTX_LEN, D), 1.0),
        'c_ctx': nrm((D,), 1.0),
        'w_mod': nrm((DEPTH, D, 6 * D), D ** -0.5),
        'b_mod': nrm((DEPTH, 6 * D), 0.01),
        'pre_norm1': 1.0 + nrm((DEPTH, D), 0.05),
        'post_norm1': 1.0 + nrm((DEPTH, D), 0.05),
        'pre_norm2': 1.0 + nrm((DEPTH, D), 0.05),
        'post_norm2': 1.0 + nrm((DEPTH, D), 0.05),
        'w_in': nrm((DEPTH, D, IN_COLS), D ** -0.5),
        'conv_w': nrm((DEPTH, SHORT_W, HY_COLS), SHORT_W ** -0.5),
        'conv_b': nrm((DEPTH, HY_COLS), 0.01),
        'filt_w1': nrm((DEPTH, FILTER_EMB, FILTER_HIDDEN), FILTER_EMB ** -0.5),
        'filt_b1': nrm((DEPTH, FILTER_HIDDEN), 0.1),
        'filt_w2': nrm((DEPTH, FILTER_HIDDEN, FILTER_HIDDEN), FILTER_HIDDEN ** -0.5),
        'filt_b2': nrm((DEPTH, FILTER_HIDDEN), 0.1),
        'filt_w3': nrm((DEPTH, FILTER_HIDDEN, FILTER_HIDDEN), FILTER_HIDDEN ** -0.5),
        'filt_b3': nrm((DEPTH, FILTER_HIDDEN), 0.1),
        'filt_w4': nrm((DEPTH, FILTER_HIDDEN, 2 * HY_WIDTH), 0.02),
        'filt_freq': 1.0 + nrm((DEPTH, FILTER_HIDDEN), 0.05),
        'hyena_bias': nrm((DEPTH, HY_WIDTH), 0.5),
        'ml_gate_b': ml_gate_b,
        'ml_norm': 1.0 + nrm((DEPTH, ML_WIDTH), 0.05),
        'w_out': nrm((DEPTH, MIX_WIDTH, D), MIX_WIDTH ** -0.5),
        'w_router': nrm((DEPTH, D, E), D ** -0.5),
        'w_exp_gate': nrm((DEPTH, E, D, F), D ** -0.5),
        'w_exp_up': nrm((DEPTH, E, D, F), D ** -0.5),
        'w_exp_down': nrm((DEPTH, E, F, D), F ** -0.5),
    }

def reference(x, c, ctx, c_ctx, w_mod, b_mod, pre_norm1, post_norm1, pre_norm2, post_norm2,
              w_in, conv_w, conv_b, filt_w1, filt_b1, filt_w2, filt_b2, filt_w3, filt_b3, filt_w4,
              filt_freq, hyena_bias, ml_gate_b, ml_norm, w_out, w_router, w_exp_gate, w_exp_up,
              w_exp_down):
    B, L, D = x.shape
    rows = L // GRID_W
    x = x + pos_embed_2d(rows, GRID_W, D).astype(x.dtype)[None]
    xc = ctx
    for li in range(DEPTH):
        update_ctx = li < DEPTH - 1
        mod = (jax.nn.silu(c) @ w_mod[li] + b_mod[li])[:, None, :]
        mod_c = (jax.nn.silu(c_ctx)[None] @ w_mod[li] + b_mod[li])[:, None, :]
        sh1, sc1, g1, sh2, sc2, g2 = jnp.split(mod, 6, axis=-1)
        csh1, csc1, cg1, csh2, csc2, cg2 = jnp.split(mod_c, 6, axis=-1)
        hyena_w = (conv_w[li], conv_b[li], filt_w1[li], filt_b1[li], filt_w2[li], filt_b2[li],
                   filt_w3[li], filt_b3[li], filt_w4[li], filt_freq[li], hyena_bias[li])

        h = modulated_norm(x, pre_norm1[li], sh1, sc1)
        hc = modulated_norm(xc, pre_norm1[li], csh1, csc1)
        z = h @ w_in[li]
        zc_ml = hc @ w_in[li][:, HY_COLS:]
        y_hy = hyena_group(z[..., :HY_COLS], *hyena_w)
        y_ml, hc_ml, oc = mlstm_group(z[..., HY_COLS:], zc_ml, ml_gate_b[li], ml_norm[li])
        y = jnp.concatenate([y_hy, y_ml], axis=-1) @ w_out[li]
        x = x + g1 * rmsnorm(y, post_norm1[li])

        if update_ctx:
            yc_hy = hyena_group(hc @ w_in[li][:, :HY_COLS], *hyena_w)
            yc_ml = mlstm_output(hc_ml, oc, ml_norm[li])
            yc = jnp.concatenate([yc_hy, yc_ml], axis=-1) @ w_out[li]
            xc = xc + cg1 * rmsnorm(yc, post_norm1[li])
            hc2 = modulated_norm(xc, pre_norm2[li], csh2, csc2)
            xc = xc + cg2 * rmsnorm(ec_moe(hc2, w_router[li], w_exp_gate[li], w_exp_up[li], w_exp_down[li]), post_norm2[li])

        h2 = modulated_norm(x, pre_norm2[li], sh2, sc2)
        y2 = ec_moe(h2, w_router[li], w_exp_gate[li], w_exp_up[li], w_exp_down[li])
        x = x + g2 * rmsnorm(y2, post_norm2[li])
    return x


_drawn_inputs = setup_inputs


def setup_inputs(seed=0):
    import zlib

    import numpy as np

    out = dict(_drawn_inputs(seed))
    spreads = {}
    factors = {'post_norm2': 2.71}
    for name, (base, spread) in spreads.items():
        noise = np.random.default_rng([zlib.crc32(name.encode()), seed]).standard_normal(out[name].shape)
        drawn = base * np.exp(spread * noise) if base else spread * noise
        out[name] = jnp.asarray(drawn.astype(out[name].dtype))
    for name, factor in factors.items():
        out[name] = (out[name] * factor).astype(out[name].dtype)
    return out
```

```python
import math
from contextlib import ExitStack

import numpy as np

import concourse.bass as bass
from concourse import mybir

F32 = mybir.dt.float32
ALU = mybir.AluOpType
ACT = mybir.ActivationFunctionType
AX = mybir.AxisListType

D, L, LC = 1024, 512, 256
P = 128
KD = D // P
NLT, NCT = L // P, LC // P
NTT = NLT + NCT
HY, DK, DV, NH = 512, 64, 128, 4
QK = NH * DK
GRID_W = 64
E, FF, CAP = 16, 2048, 64
BANDS, FEMB, FH = 16, 33, 64
EPS = 1e-6
GCAP = 15.0
NCH = HY // P
BIG = 1e30
NSLOT, SLOTF = 8, 4096
CH = 512
TWO_PI = 2.0 * math.pi
MAGIC = 12582912.0
PI_IN = 3.1415925

R_C, R_CC, R_PRE1, R_PRE2, R_BMOD = 0, 8, 16, 24, 32
R1_ROWS = 80
R_CW, R_CB, R_MLN, R_FB, R_FQ = 0, 36, 48, 52, 55
R2_ROWS = 56

C_ID, C_UP, C_LO, C_ONE, C_BF, C_BB, C_IO, C_TC = 0, 128, 256, 384, 512, 640, 768, 832
C_COLS = 836


def shape_constants():
    i = np.arange(P)
    cst = np.zeros((P, C_COLS), np.float32)
    cst[:, C_ID:C_ID + P] = np.eye(P)
    cst[:, C_UP:C_UP + P] = i[:, None] <= i[None, :]
    cst[:, C_LO:C_LO + P] = i[:, None] >= i[None, :]
    cst[:, C_ONE:C_ONE + P] = 1.0
    cst[:, C_BF:C_BF + P] = np.where(i[:, None] <= i[None, :], 0.0, BIG)
    cst[:, C_BB:C_BB + P] = np.where(i[:, None] >= i[None, :], 0.0, BIG)
    cst[:, C_IO:C_IO + CAP] = np.arange(CAP)[None, :]
    tpos = np.linspace(0.0, 1.0, L, dtype=np.float32)
    cst[:, C_TC:C_TC + NLT] = -tpos.reshape(NLT, P).T
    quarter = D // 4
    omega = 1.0 / (10000.0 ** (np.arange(quarter, dtype=np.float64) / quarter))

    def emb(n):
        ang = np.arange(n, dtype=np.float64)[:, None] * omega[None, :]
        return np.concatenate([np.sin(ang), np.cos(ang)], axis=-1)
    rows = L // GRID_W
    er, ec = emb(rows), emb(GRID_W)
    pe = np.concatenate([np.broadcast_to(er[:, None, :], (rows, GRID_W, D // 2)),
                         np.broadcast_to(ec[None, :, :], (rows, GRID_W, D // 2))], axis=-1)
    pe = np.ascontiguousarray(pe.reshape(L, D).astype(np.float32))
    w = 2.0 * np.pi * np.arange(L) / L
    f = np.linspace(1e-4, BANDS - 1, BANDS)
    ang = w[:, None] * f[None, :]
    zf = np.concatenate([tpos[:, None].astype(np.float64), np.cos(ang), -np.sin(ang)], axis=-1)
    zft = np.ascontiguousarray(zf.T.astype(np.float32))
    lo, hi = math.log(1e-2) / 1.5, math.log(1e-2) / 0.3
    deltas = np.abs(np.linspace(lo, hi, HY, dtype=np.float32))
    dl = np.ascontiguousarray(np.broadcast_to(deltas[None, :], (P, HY)).astype(np.float32))
    t = np.arange(L, dtype=np.float64)
    a = (np.pi / L) * (t[:, None] * (t[None, :] + 0.5))
    fwd = np.stack([np.cos(a), np.sin(a)])
    inv = np.stack([np.cos(a).T, np.sin(a).T]) / L

    def tiles(m):
        return np.ascontiguousarray(
            m.reshape(2, NLT, P, L).transpose(2, 0, 1, 3).reshape(P, 2 * NLT * L).astype(np.float32))
    return {"cst": cst, "pos": pe, "zft": zft, "dl": dl, "dft": tiles(fwd), "idft": tiles(inv)}


def step_of(d, tile):
    if d == 0:
        return tile
    return NCT - 1 - tile if tile < NCT else NTT - 1 - (tile - NCT)


def block_kernel(nc, A, out):
    ctx = ExitStack()
    with ctx:
        def sb(name, cols, rows=P):
            return ctx.enter_context(nc.sbuf_tensor(name, [rows, cols], F32))

        def sem(name):
            return ctx.enter_context(nc.semaphore(name))

        ring = sb("ring", NSLOT * SLOTF)

        def slot(n, a=0, b=SLOTF):
            return ring[:, n * SLOTF + a:n * SLOTF + b]

        xl = sb("xl", NLT * D)
        yacc = sb("yacc", NLT * D)
        moe = sb("moe", 6144)
        fr = sb("fr", 3584)
        g2p = sb("g2p", D)
        cst = sb("cst_sb", C_COLS)
        col = sb("col", 620)

        ident = cst[:, C_ID:C_ID + P]
        ones = cst[:, C_ONE:C_ONE + P]
        x3 = xl[:, :].rearrange("p (c n) -> p c n", c=NLT)

        v1t = col[:, 0:R1_ROWS]
        v2t = col[:, 80:80 + R2_ROWS]
        aff1 = col[:, 136:168].rearrange("p (v w k) -> p v w k", v=2, w=2)
        aff2 = col[:, 168:184].rearrange("p (w k) -> p w k", w=2)
        sst = col[:, 184:190]
        std = col[:, 190:196]
        rst = col[:, 196:202]
        epsc = col[:, 202:203]
        slotm = col[:, 204:268].rearrange("p (e c) -> p e c", e=E)
        affr = col[:, 268:332].rearrange("p (e c) -> p e c", e=E)
        ss2 = col[:, 332:336]
        sd2 = col[:, 336:340]
        rs2 = col[:, 340:344]
        mcur = col[:, 344:408]
        mprev = col[:, 408:472]
        mend = col[:, 472:536]
        wcp = col[:, 536:560]
        slp = col[:, 560:568]
        afp = col[:, 568:576]
        sy = col[:, 576:580]
        sdy = col[:, 580:584]
        ry = col[:, 584:588]
        gb = col[:, 588:604]
        nst = col[:, 604:612].rearrange("p (c h) -> p c h", c=NLT)

        ut = slot(2, 0, 2048).rearrange("p (i t) -> p i t", i=NCH)
        brow = slot(2, 2048, 2560)
        prow = slot(2, 2560, 3072)
        g1p = slot(2, 3072, 4096)
        ht = ring[:, 3 * SLOTF:3 * SLOTF + KD * (L + LC)].rearrange("p (k t) -> p k t", k=KD)
        usp = slot(3).rearrange("p (w k n) -> p w k n", w=2, k=NLT)
        hsum = slot(4, 0, 2048).rearrange("p (c n) -> p c n", c=NLT)
        x0t = slot(4, 2048, 4096).rearrange("p (i t) -> p i t", i=NCH)
        dft = slot(5).rearrange("p (w c k) -> p w c k", w=2, c=NLT)
        cstate = slot(5, 0, 2064).rearrange("p (d s n) -> p d s n", d=2, s=NLT)
        ebuf = slot(5, 2064, 3088).rearrange("p (b n) -> p b n", b=2)
        kwb = slot(5, 3088, 3600).rearrange("p (b n) -> p b n", b=2)
        xn = slot(6).rearrange("p (c n) -> p c n", c=NLT)
        idft = slot(6).rearrange("p (w k t) -> p w k t", w=2, k=NLT)
        ksp = slot(7).rearrange("p (w k n) -> p w k n", w=2, k=NLT)
        zft = slot(3, 0, 512)
        fw1 = slot(3, 512, 576)
        fw2 = slot(3, 576, 640)
        fw3 = slot(3, 640, 704)
        fw4 = slot(3, 704, 1728)
        fh = slot(3, 1728, 2240)
        fa = slot(3, 2240, 2752)
        ft = slot(3, 2752, 3264)
        dlb = slot(3, 3264, 3776)
        dcy = slot(4, 0, 512)
        fhf = slot(4, 512, 1024)
        fhb = slot(4, 1024, 1536)
        tmask = slot(4, 1536, 1537)
        hyb = slot(4, 1600, 2112)
        vr1 = slot(4, 2112, 2240)
        vr2 = slot(4, 2240, 2368)
        sq = slot(4, 2400, 3424)
        hpm = yacc[:, :].rearrange("p (w c n) -> p w c n", w=2, c=NLT)
        v1 = yacc[:, 0:NTT * NH * (DV + 1)].rearrange("p (t h n) -> p t h n", t=NTT, h=NH)
        g0 = NTT * NH * (DV + 1)
        atp = yacc[:, g0:g0 + 512].rearrange("p (b n) -> p b n", b=2)
        ew = yacc[:, g0 + 512:g0 + 768].rearrange("p (w n) -> p w n", w=4)
        th = yacc[:, g0 + 768:g0 + 864].rearrange("p (d s n) -> p d s n", d=2, s=NTT)
        lf = yacc[:, g0 + 864:g0 + 912].rearrange("p (d s n) -> p d s n", d=2, s=NTT)
        aco = yacc[:, g0 + 912:g0 + 976]
        cx = moe[:, 0:NCT * D].rearrange("p (c n) -> p c n", c=NCT)
        qt = moe[:, 0:1024].rearrange("p (h t) -> p h t", h=2)
        kt = moe[:, 1024:2048].rearrange("p (h t) -> p h t", h=2)
        kk = moe[:, 2048:3584].rearrange("p (t n) -> p t n", t=NTT)
        og = moe[:, 3584:5632].rearrange("p (c n) -> p c n", c=NLT)
        cpad = moe[:, 5632:5888].rearrange("p (k m) -> p k m", k=KD)
        mrow_t = moe[:, 5888:6016]
        wgate_sb = moe[:, 6016:6144].rearrange("p (k n) -> p k n", k=KD)
        us = fr[:, 0:2048].rearrange("p (c n) -> p c n", c=NLT)
        ymt = fr[:, 0:2048].rearrange("p (h t) -> p h t", h=NH)
        ctmp = fr[:, 2048:3072].rearrange("p (b n) -> p b n", b=2)
        tot = fr[:, 2048:2048 + 516].rearrange("p (b c n) -> p b c n", b=2, c=2)
        dab = fr[:, 2570:2578].rearrange("p (b c) -> p b c", b=4)
        ssq = fr[:, 2580:2596]
        mrow = fr[:, 3072:3584]
        gt = moe[:, 3584:4352]

        xst = moe[:, 0:1024].rearrange("p (k n) -> p k n", k=KD)
        sil = moe[:, 1024:2048].rearrange("p (b n) -> p b n", b=2)
        hid = moe[:, 2048:3072].rearrange("p (b n) -> p b n", b=2)
        hdt = moe[:, 3072:3584].rearrange("p (b n) -> p b n", b=2)
        ye = moe[:, 3584:4608]
        psel = moe[:, 4608:5120].rearrange("p (c n) -> p c n", c=NLT)
        pw = moe[:, 5120:5632].rearrange("p (c n) -> p c n", c=NLT)
        pwt = moe[:, 5632:6144].rearrange("p (c n) -> p c n", c=NLT)
        peq = fr[:, 0:512].rearrange("p (c n) -> p c n", c=NLT)
        y3 = yacc[:, :].rearrange("p (c n) -> p c n", c=NLT)

        B = [ctx.enter_context(nc.psum_tensor(f"B{i}", [P, 512], F32)) for i in range(8)]

        xn2 = slot(2, 0, 2048).rearrange("p (b n) -> p b n", b=2)
        wr = slot(2, 2048, 2176).rearrange("p (k e) -> p k e", k=KD)
        junk = slot(4, 0, 1024)
        h2t = yacc[:, :].rearrange("p (k t) -> p k t", k=KD)
        lgt = fr[:, 0:512]
        lg = fr[:, 512:576].rearrange("p (c e) -> p c e", c=NLT)
        mx4 = fr[:, 576:580]
        sm4 = fr[:, 580:584]
        rc4 = fr[:, 584:588]
        aft = fr[:, 592:656].rearrange("p (c e) -> p c e", c=NLT)
        wka = fr[:, 1024:1536]
        wkb = fr[:, 1536:2048]
        top8 = fr[:, 656:664]
        mkt = fr[:, 672:736].rearrange("p (c e) -> p c e", c=NLT)

        d_vec, d_cst, d_filt, d_dft, d_inv = map(sem, ["d_vec", "d_cst", "d_filt", "d_dft", "d_inv"])
        d_x, d_pos, d_ctx, d_row, d_gate, d_wr = map(sem, ["d_x", "d_pos", "d_ctx", "d_row", "d_gate", "d_wr"])
        d_w = [sem(f"d_w{i}") for i in range(2)]
        d_ring = [sem(f"d_ring{i}") for i in range(NSLOT)]
        d_out = sem("d_out")
        names = ["p_vt", "p_fil", "p_kf", "p_ksp", "p_w", "p_modt", "p_g1", "p_htl", "p_htc", "p_gt",
                 "p_gtr", "p_cs", "p_at", "p_cm", "p_mt", "p_hy", "p_utr", "p_qk", "p_kc", "p_ktr", "p_v",
                 "p_st", "p_o", "p_usp", "p_inv", "p_sc", "p_mb", "p_num", "p_ytr", "p_y", "p_h2", "p_lg",
                 "p_lgt", "p_aft", "p_mk", "p_rk", "p_xs", "p_gu", "p_pwt", "p_ht", "p_dn", "p_sca", "v_ch",
                 "v_vt", "v_arg", "v_hpm", "v_kf", "v_mrow", "v_aff", "v_grow", "v_xn", "v_htc", "v_cpad",
                 "v_gsum", "v_sel", "v_dec", "v_x", "v_ew", "v_ssq", "v_cs", "v_at", "v_cum", "v_m", "v_mt",
                 "v_conv", "v_kc", "v_st", "v_cx", "v_inv", "v_d", "v_sw", "v_tot", "v_hs", "v_hn", "v_x1",
                 "v_xn2", "v_h2", "v_lgt", "v_sub", "v_aft", "v_mk", "v_mkt", "v_slot", "v_xs", "v_hid",
                 "v_hdt", "v_yacc", "v_res", "v_cp", "a_ch", "a_th", "a_fil", "a_dec", "a_ksp", "a_ss",
                 "a_std", "a_htl", "a_gt", "a_lf", "a_ew", "a_us", "a_qk", "a_ktr", "a_v", "a_o", "a_usp",
                 "a_e", "a_n2", "a_sq", "a_yt", "a_sy", "a_sdy", "a_ss2", "a_h2", "a_exp", "a_xs", "a_sil",
                 "a_pwt", "a_ye", "a_fsd", "g_ms", "g_zero", "g_kw", "g_sel", "g_cp"]
        S = {n: sem(n) for n in names}

        SLOT_OF = [7, 6, 3, 5, 0, 1, 4, 2]
        NPAIR = E // 2
        TILES = [("g", 0), ("u", 0), ("g", 1), ("u", 1), ("d", 0)]
        for q in range(2, 8):
            TILES += [("g", q), ("u", q), ("d", q - 1)]
        TILES += [("d", 7)]
        NTI = len(TILES)
        WT = [("m", 0), ("m", 1), ("m", 2), ("m", 3), ("i", 0), ("m", 4), ("i", 1), ("m", 5), ("i", 2),
              ("m", 6), ("i", 3), ("m", 7), ("i", 4), ("m", 8), ("m", 9), ("i", 5), ("m", 10), ("m", 11),
              ("o", 0), ("o", 1)]
        w_mod, w_in, w_out = A["w_mod"][0], A["w_in"][0], A["w_out"][0]

        N_VEC, N_FILT = 12, 7
        hy_bank, qk_bank, kc_bank, v_bank, o_bank, usp_bank = {}, {}, {}, {}, {}, {}
        usq = moe[:, 0:2048].rearrange("p (m n) -> p m n", n=DV)

        block = ctx.enter_context(nc.Block())

        @block.sync
        def _(sp):
            def rows(dst, r, src, n):
                sp.dma_start(dst[r:r + n, :], src.rearrange("(a b) -> a b", b=P)).then_inc(d_vec, 16)
            rows(vr1, R_C, A["c"][0], 8)
            rows(vr1, R_CC, A["c_ctx"], 8)
            rows(vr1, R_PRE1, A["pre_norm1"][0], 8)
            rows(vr1, R_PRE2, A["pre_norm2"][0], 8)
            rows(vr1, R_BMOD, A["b_mod"][0], 48)
            sp.wait_ge(S["g_ms"], 1)
            sp.dma_start(vr2[R_CW:R_CW + 36, :],
                         A["conv_w"][0].rearrange("w (a b) -> (w a) b", b=P)).then_inc(d_vec, 16)
            rows(vr2, R_CB, A["conv_b"][0], 12)
            rows(vr2, R_MLN, A["ml_norm"][0], 4)
            for n, name in enumerate(("filt_b1", "filt_b2", "filt_b3", "filt_freq")):
                sp.dma_start(vr2[R_FB + n:R_FB + n + 1, 0:FH], A[name]).then_inc(d_vec, 16)
            sp.dma_start(cst[:, :], A["cst"]).then_inc(d_cst, 16)
            sp.dma_start(zft[0:FEMB, :], A["zft"]).then_inc(d_filt, 16)
            sp.dma_start(fw1[0:FEMB, :], A["filt_w1"][0]).then_inc(d_filt, 16)
            sp.dma_start(fw2[0:FH, :], A["filt_w2"][0]).then_inc(d_filt, 16)
            sp.dma_start(fw3[0:FH, :], A["filt_w3"][0]).then_inc(d_filt, 16)
            sp.dma_start(fw4[0:FH, :], A["filt_w4"][0]).then_inc(d_filt, 16)
            sp.dma_start(dlb, A["dl"]).then_inc(d_filt, 16)
            sp.dma_start(hyb[0:1, :], A["hyena_bias"]).then_inc(d_filt, 16)
            sp.dma_start(slot(5), A["dft"]).then_inc(d_dft, 16)

            def weight(n):
                kind, i = WT[n]
                if n >= 2:
                    sp.wait_ge(S["p_w"], n - 1)
                dst = slot(n % 2)
                if kind == "m":
                    r, kp = divmod(i, 4)
                    src = w_mod[kp * 2 * P:(kp + 1) * 2 * P, r * 2048:(r + 1) * 2048]
                    dst = dst.rearrange("p (k n) -> p k n", k=2)
                elif kind == "i":
                    src, dst = w_in[:, i * CH:(i + 1) * CH], dst.rearrange("p (k n) -> p k n", k=KD)
                else:
                    src, dst = w_out[:, i * CH:(i + 1) * CH], dst.rearrange("p (k n) -> p k n", k=KD)
                sp.dma_start(dst, src.rearrange("(k p) n -> p k n", p=P)).then_inc(d_w[n % 2], 16)

            for n in range(len(WT)):
                if n == 4:
                    sp.dma_start(wgate_sb, w_in[:, 6 * CH:6 * CH + 16].rearrange("(k p) n -> p k n", p=P))\
                        .then_inc(d_gate, 16)
                    sp.dma_start(gb, A["ml_gate_b"][0].partition_broadcast(P)).then_inc(d_gate, 16)
                if n == 6:
                    sp.wait_ge(S["p_htl"], KD)
                    sp.dma_start(slot(6), A["idft"]).then_inc(d_inv, 16)
                weight(n)

            def expert_tile(i, pair):
                kind, st = TILES[i]
                e2, q = divmod(st, 4)
                dst = slot(SLOT_OF[i % NSLOT])
                ex = 2 * pair + e2
                if kind == "d":
                    src = A["w_exp_down"][0, bass.ds(ex, 1), q * CH:(q + 1) * CH, :]
                    src = src.rearrange("o (k p) n -> p (o k) n", p=P)
                    dst = dst.rearrange("p (k n) -> p k n", k=4)
                else:
                    w = A["w_exp_gate" if kind == "g" else "w_exp_up"]
                    src = w[0, bass.ds(ex, 1), :, q * CH:(q + 1) * CH]
                    src = src.rearrange("o (k p) n -> p (o k) n", p=P)
                    dst = dst.rearrange("p (k n) -> p k n", k=KD)
                sp.dma_start(dst, src).then_inc(d_ring[i % NSLOT], 16)

            def used(i, pair):
                kind, st = TILES[i]
                sp.wait_ge(S["p_dn" if kind == "d" else "p_gu"], 8 * pair + st + 1)

            sp.wait_ge(S["v_cx"], NLT)
            expert_tile(0, 0)
            sp.wait_ge(S["v_grow"], 2)
            sp.dma_start(wr, A["w_router"][0].rearrange("(k p) e -> p k e", p=P)).then_inc(d_wr, 16)
            sp.wait_ge(S["p_inv"], NCH)
            expert_tile(1, 0)
            expert_tile(2, 0)
            sp.wait_ge(S["p_num"], 16)
            expert_tile(3, 0)
            sp.wait_ge(S["p_w"], len(WT))
            expert_tile(4, 0)
            expert_tile(5, 0)
            sp.wait_ge(S["a_ss2"], NLT)
            expert_tile(6, 0)
            sp.wait_ge(S["p_lg"], NLT)
            expert_tile(7, 0)
            with sp.Fori(0, NPAIR - 1) as j:
                for i in range(NTI):
                    used(i, j)
                    expert_tile((i + NSLOT) % NTI, j if i + NSLOT < NTI else j + 1)
            for i in range(NTI - NSLOT):
                used(i, NPAIR - 1)
                expert_tile(i + NSLOT, NPAIR - 1)
            for c in range(NLT):
                sp.wait_ge(S["v_res"], c + 1)
                sp.dma_start(out[0, c * P:(c + 1) * P, :], y3[:, c, :]).then_inc(d_out, 16)
            sp.wait_ge(d_out, 16 * NLT)

        @block.gpsimd
        def _(pool):
            g = nc.gpsimd
            g.memset(vr2, 0.0).then_inc(S["g_ms"], 1)
            g.memset(brow, 0.0).then_inc(S["g_zero"], 1)
            g.memset(prow, 0.0).then_inc(S["g_zero"], 1)
            g.memset(moe[:, 5632:5888], 0.0).then_inc(S["g_zero"], 1)
            g.memset(epsc, EPS).then_inc(S["g_zero"], 1)
            pool.wait_ge(S["a_ew"], 1)
            pool.wait_ge(S["v_kc"], NCT)
            pool.wait_ge(S["a_ktr"], 2)
            pool.wait_ge(S["p_usp"], 8)
            n = 0
            for st in range(NTT - 1):
                for d in range(2):
                    tile = [t for t in range(NTT) if step_of(d, t) == st][0]
                    if n >= 2:
                        pool.wait_ge(S["p_st"], n - 1)
                    r = 32 * d + 4 * st
                    src = kk[:, tile, :].rearrange("p (h n) -> p h n", h=NH)
                    wsb = ew[:, 2, r:r + NH].rearrange("p (h o) -> p h o", o=1).to_broadcast([P, NH, DK])
                    g.tensor_tensor(kwb[:, n % 2, :].rearrange("p (h n) -> p h n", h=NH), src, wsb,
                                    ALU.mult).then_inc(S["g_kw"], 1)
                    n += 1
            pool.wait_ge(S["v_slot"], 2)
            with pool.Fori(0, NPAIR) as j:
                pool.wait_ge(S["v_sel"], 4 * j + 1)
                g.tensor_copy(afp, affr[:, bass.ds(2 * j, 2), :]
                              .rearrange("p e c -> p (e c)")).then_inc(S["g_cp"], 1)
                pool.wait_ge(S["g_cp"], j + 1)
                pool.wait_ge(S["v_sel"], 4 * j + 3)
                for e2 in range(2):
                    af = afp[:, 4 * e2:4 * e2 + 4].rearrange("p (c o) -> p c o", o=1).to_broadcast([P, NLT, CAP])
                    g.tensor_tensor(pw[:, :, CAP * e2:CAP * e2 + CAP], peq[:, :, CAP * e2:CAP * e2 + CAP], af,
                                    ALU.mult).then_inc(S["g_sel"], 1)

        @block.tensor
        def _(pe):
            mm, tr = nc.tensor.matmul, nc.tensor.transpose
            idn = ident
            users = {}

            def take(b):
                if b in users:
                    pe.wait_ge(*users[b])

            def upper(m):
                return ident[0:m, 0:m]

            pe.wait_ge(d_cst, 16)
            pe.wait_ge(d_vec, 16 * N_VEC)
            tr(B[0][:, 0:R1_ROWS], vr1[0:R1_ROWS, :], upper(R1_ROWS)).then_inc(S["p_vt"], 1)
            tr(B[1][:, 0:R2_ROWS], vr2[0:R2_ROWS, :], upper(R2_ROWS)).then_inc(S["p_vt"], 1)
            users[0] = users[1] = (S["v_vt"], 2)
            pe.wait_ge(d_filt, 16 * N_FILT)
            mm(B[2][0:FH, :], fw1[0:FEMB, :], zft[0:FEMB, :], start=True, stop=True).then_inc(S["p_fil"], 1)
            pe.wait_ge(S["a_fil"], 1)
            mm(B[3][0:FH, :], fw2[0:FH, :], fh[0:FH, :], start=True, stop=True).then_inc(S["p_fil"], 1)
            pe.wait_ge(S["a_fil"], 2)
            mm(B[2][0:FH, :], fw3[0:FH, :], fh[0:FH, :], start=True, stop=True).then_inc(S["p_fil"], 1)
            pe.wait_ge(S["a_fil"], 3)
            for c in range(NLT):
                for w in range(2):
                    b = 4 + 2 * (c % 2) + w
                    if c >= 2:
                        pe.wait_ge(S["v_kf"], 2 * (c - 2) + w + 1)
                    mm(B[b][:, :], fh[0:FH, c * P:(c + 1) * P], fw4[0:FH, w * HY:(w + 1) * HY],
                       start=True, stop=True).then_inc(S["p_kf"], 1)
            pe.wait_ge(d_dft, 16)
            pe.wait_ge(S["v_vt"], 2)
            pe.wait_ge(S["v_hpm"], 1)
            for kc in range(NLT):
                for w in range(2):
                    b = 2 * kc + w
                    for c in range(NLT):
                        r = mm(B[b][:, :], dft[:, w, c, kc * P:(kc + 1) * P], hpm[:, w, c, :],
                               start=(c == 0), stop=(c == NLT - 1))
                    r.then_inc(S["p_ksp"], 1)
                    users[b] = (S["a_ksp"], b + 1)

            stream = [0]

            def weights(kind, i):
                n = stream[0]
                assert WT[n] == (kind, i)
                stream[0] += 1
                pe.wait_ge(d_w[n % 2], 16 * (n // 2 + 1))
                return slot(n % 2)

            def mod_tile(i):
                r, kp = divmod(i, 4)
                w = weights("m", i).rearrange("p (k n) -> p k n", k=2)
                if kp == 0:
                    take(2)
                for k in range(2):
                    for n in range(4):
                        x = mm(B[2][32 * n:32 * n + 32, :], cpad[:, 2 * kp + k, :], w[:, k, n * CH:(n + 1) * CH],
                               start=(kp == 0 and k == 0), stop=(kp == 3 and k == 1))
                x.then_inc(S["p_w"], 1)
                users[2] = (S["v_mrow"], r + 1)

            def mod_turn(r, b):
                pe.wait_ge(S["v_mrow"], r + 1)
                take(b)
                for q in range(4):
                    x = tr(B[b][:, q * P:(q + 1) * P], mrow[:, q * P:(q + 1) * P], idn)
                x.then_inc(S["p_modt"], 1)
                users[b] = (S["v_aff"], r + 1)

            def gate_rows(g, n0):
                pe.wait_ge(S["v_grow"], g + 1)
                for h in range(2):
                    take(h)
                    row = 32 * (n0 + h)
                    mm(B[h][:, :], ident[:, row:row + 1].to_broadcast([P, P]), mrow[:, :],
                       start=True, stop=True).then_inc(S["p_g1"], 1)
                    users[h] = (S["v_cp"], 2 * g + h + 1)

            pe.wait_ge(S["v_cpad"], 1)
            for i in range(4):
                mod_tile(i)
            mod_turn(0, 1)
            pe.wait_ge(S["v_xn"], NTT)
            for k in range(KD):
                for lat in (1, 0):
                    b = 3 + (2 * k + 1 - lat) % 5
                    take(b)
                    src = xn if lat else cx
                    for c in range(NLT if lat else NCT):
                        x = tr(B[b][:, c * P:(c + 1) * P], src[:, c, k * P:(k + 1) * P], idn)
                    x.then_inc(S["p_htl" if lat else "p_htc"], 1)
                    users[b] = (S["a_htl" if lat else "v_htc"], k + 1)
            pe.wait_ge(S["a_htl"], KD)
            pe.wait_ge(S["v_htc"], KD)
            pe.wait_ge(d_gate, 32)
            take(0)
            for k in range(KD):
                mm(B[0][0:16, :], wgate_sb[:, k, :], ht[:, k, LC:], start=(k == 0), stop=(k == KD - 1))
                x = mm(B[0][32:48, 0:LC], wgate_sb[:, k, :], ht[:, k, 0:LC], start=(k == 0), stop=(k == KD - 1))
            x.then_inc(S["p_gt"], 1)
            users[0] = (S["a_gt"], 2)
            rot = [0]

            def next_bank():
                b = 3 + rot[0] % 5
                rot[0] += 1
                take(b)
                return b

            def hyena_tile(i):
                w = weights("i", i).rearrange("p (k n) -> p k n", k=KD)
                for m in range(NCH):
                    b = next_bank()
                    for k in range(KD):
                        x = mm(B[b][:, :], w[:, k, m * P:(m + 1) * P], ht[:, k, LC:], start=(k == 0), stop=(k == KD - 1))
                    x.then_inc(S["p_hy" if m < NCH - 1 else "p_w"], 1)
                    n = i * NCH + m
                    hy_bank[n] = b
                    users[b] = (S["v_conv"], n + 1)

            hyena_tile(0)
            pe.wait_ge(S["a_gt"], 2)
            take(1)
            for d in range(2):
                for t in range(NTT):
                    o = (d * NTT + step_of(d, t)) * 16
                    x = tr(B[1][:, o:o + 16], gt[0:16, t * P:(t + 1) * P], upper(16))
            x.then_inc(S["p_gtr"], 1)
            users[1] = (S["v_gsum"], 2)
            mod_tile(4)
            hyena_tile(1)
            pe.wait_ge(S["a_lf"], 1)
            take(0)
            mm(B[0][:, 0:24], cst[:, C_UP:C_UP + P], lf[:, 0, :, :], start=True, stop=True)
            mm(B[0][:, 32:56], cst[:, C_LO:C_LO + P], lf[:, 1, :, :], start=True, stop=True)
            mm(B[0][:, 64:88], ones, lf[:, 0, :, :], start=True, stop=True)
            mm(B[0][:, 96:120], ones, lf[:, 1, :, :], start=True, stop=True).then_inc(S["p_cs"], 1)
            users[0] = (S["v_cs"], 1)
            mod_tile(5)
            pe.wait_ge(S["v_cs"], 1)
            take(1)
            tr(B[1][0:64, 0:P], aco, idn).then_inc(S["p_at"], 1)
            users[1] = (S["v_at"], 1)
            hyena_tile(2)
            pe.wait_ge(S["v_cum"], 1)
            take(0)
            tr(B[0][:, 0:64], atp[0:64, 1, 64:192], upper(64))
            mm(B[0][:, 64:128], mrow_t[0:64, 0:1].to_broadcast([64, P]), upper(64),
               start=True, stop=True).then_inc(S["p_cm"], 1)
            users[0] = (S["v_m"], 1)
            mod_tile(6)
            w = weights("i", 3).rearrange("p (k n) -> p k n", k=KD)
            for m in range(4):
                b = next_bank()
                for k in range(KD):
                    x = mm(B[b][:, :], w[:, k, m * P:(m + 1) * P], ht[:, k, LC:], start=(k == 0), stop=(k == KD - 1))
                x.then_inc(S["p_qk"], 1)
                qk_bank[m] = b
                users[b] = (S["a_qk"], m + 1)
                if m == 0:
                    pe.wait_ge(S["v_m"], 1)
                    take(1)
                    tr(B[1][0:64, 0:P], mcur, idn).then_inc(S["p_mt"], 1)
                    users[1] = (S["v_mt"], 1)
            for c in range(NCT):
                b = next_bank()
                for k in range(KD):
                    x = mm(B[b][:, 0:QK], ht[:, k, c * P:(c + 1) * P], w[:, k, QK:2 * QK], start=(k == 0), stop=(k == KD - 1))
                x.then_inc(S["p_kc"] if c < NCT - 1 else S["p_w"], 1)
                kc_bank[c] = b
                users[b] = (S["v_kc"], c + 1)
            for i in range(NCH):
                pe.wait_ge(S["v_conv"], 2 * NCH + i + 1)
                take(i % 2)
                for c in range(NLT):
                    x = tr(B[i % 2][:, c * P:(c + 1) * P], ut[:, i, c * P:(c + 1) * P], idn)
                x.then_inc(S["p_utr"], 1)
                users[i % 2] = (S["a_us"], i + 1)
            mod_tile(7)
            pe.wait_ge(S["a_qk"], 4)
            for g in range(2):
                take(g)
                for c in range(2):
                    for hp in range(2):
                        x = tr(B[g][:, c * QK + hp * P:c * QK + (hp + 1) * P],
                               kt[:, hp, (2 * g + c) * P:(2 * g + c + 1) * P], idn)
                x.then_inc(S["p_ktr"], 1)
                users[g] = (S["a_ktr"], g + 1)
            w = weights("i", 4).rearrange("p (k n) -> p k n", k=KD)
            for t in range(NTT):
                b = next_bank()
                for k in range(KD):
                    x = mm(B[b][:, :], ht[:, k, t * P:(t + 1) * P], w[:, k, :], start=(k == 0), stop=(k == KD - 1))
                x.then_inc(S["p_v"] if t < NTT - 1 else S["p_w"], 1)
                v_bank[t] = b
                users[b] = (S["a_v"], t + 1)
                if t == 1:
                    mod_turn(1, 1)
            gate_rows(0, 0)
            mod_tile(8)
            mod_tile(9)
            w = weights("i", 5).rearrange("p (k n) -> p k n", k=KD)
            for c in range(NLT):
                b = next_bank()
                for k in range(KD):
                    x = mm(B[b][:, :], ht[:, k, LC + c * P:LC + (c + 1) * P], w[:, k, :], start=(k == 0), stop=(k == KD - 1))
                x.then_inc(S["p_o"] if c < NLT - 1 else S["p_w"], 1)
                o_bank[c] = b
                users[b] = (S["a_o"], c + 1)
            mod_tile(10)
            mod_tile(11)
            pe.wait_ge(S["a_us"], NCH)
            for kc in range(NLT):
                for wv in range(2):
                    b = next_bank()
                    for c in range(NLT):
                        x = mm(B[b][:, :], dft[:, wv, c, kc * P:(kc + 1) * P], us[:, c, :], start=(c == 0), stop=(c == NLT - 1))
                    x.then_inc(S["p_usp"], 1)
                    usp_bank[2 * kc + wv] = b
                    users[b] = (S["a_usp"], 2 * kc + wv + 1)
            n = 0
            for st in range(NTT - 1):
                for d in range(2):
                    tile = [t for t in range(NTT) if step_of(d, t) == st][0]
                    pe.wait_ge(S["g_kw"], n + 1)
                    take(n % 2)
                    for h in range(NH):
                        po = DK * (h % 2)
                        x = mm(B[n % 2][po:po + DK, (h // 2) * (DV + 1):(h // 2 + 1) * (DV + 1)],
                               kwb[:, n % 2, h * DK:(h + 1) * DK], v1[:, tile, h, :], start=True, stop=True)
                    x.then_inc(S["p_st"], 1)
                    users[n % 2] = (S["v_st"], n + 1)
                    n += 1
            mod_turn(2, 2)
            gate_rows(1, 2)

            def prepare(h):
                po = DK * (h % 2)
                take(h % 2)
                for c in range(NLT):
                    x = mm(B[h % 2][:, c * P:(c + 1) * P], kt[po:po + DK, h // 2, c * P:(c + 1) * P],
                           qt[po:po + DK, h // 2, c * P:(c + 1) * P], start=True, stop=True)
                x.then_inc(S["p_sc"], 1)
                users[h % 2] = (S["v_sw"], 2 * h + 2)
                for d in range(2):
                    take(2 + d)
                    for c in range(NLT):
                        r = 32 * d + 4 * step_of(d, NCT + c) + h
                        x = mm(B[2 + d][:, c * P:(c + 1) * P], ident[0:64, r:r + 1].to_broadcast([64, P]),
                               mrow_t[0:64, :], start=True, stop=True)
                    x.then_inc(S["p_mb"], 1)
                    users[2 + d] = (S["v_d"], 2 * h + d + 1)

            def numerators(h):
                po = DK * (h % 2)
                for d in range(2):
                    pe.wait_ge(S["v_sw"], 2 * h + d + 1)
                    for cp in range(2):
                        n = 4 * h + 2 * d + cp
                        ba, bb = 4 + 2 * (n % 2), 5 + 2 * (n % 2)
                        take(ba)
                        take(bb)
                        for c in (2 * cp, 2 * cp + 1):
                            o = (c % 2) * (DV + 1)
                            st = step_of(d, NCT + c)
                            mm(B[bb][:, o:o + DV + 1], qt[po:po + DK, h // 2, c * P:(c + 1) * P],
                               cstate[po:po + DK, d, st - NCT, (h // 2) * (DV + 1):(h // 2 + 1) * (DV + 1)],
                               start=True, stop=True)
                            x = mm(B[ba][:, o:o + DV + 1], ebuf[:, d, c * P:(c + 1) * P], v1[:, NCT + c, h, :],
                                   start=True, stop=True)
                        x.then_inc(S["p_num"], 1)
                        users[ba] = users[bb] = (S["v_tot"], n + 1)

            def inverse(i):
                b = 4 + i
                take(b)
                for wv in range(2):
                    for k in range(NLT):
                        x = mm(B[b][:, :], usp[:, wv, k, i * P:(i + 1) * P], idft[:, wv, k, :],
                               start=(wv == 0 and k == 0), stop=(wv == 1 and k == NLT - 1))
                x.then_inc(S["p_inv"], 1)
                users[b] = (S["v_inv"], i + 1)

            pe.wait_ge(S["v_mt"], 1)
            pe.wait_ge(S["v_st"], n)
            prepare(0)
            pe.wait_ge(d_inv, 16)
            pe.wait_ge(S["v_cx"], NLT)
            for i in range(NCH):
                inverse(i)
            for h in range(NH):
                numerators(h)
                if h + 1 < NH:
                    prepare(h + 1)
            for i in range(NH):
                pe.wait_ge(S["v_hn"], i + 1)
                take(i % 2)
                for h in range(NH):
                    x = tr(B[i % 2][:, h * P:(h + 1) * P], hsum[:, i, h * P:(h + 1) * P], idn)
                x.then_inc(S["p_ytr"], 1)
                users[i % 2] = (S["a_yt"], i + 1)
            pe.wait_ge(S["v_inv"], NCH)
            wo = [weights("o", i).rearrange("p (k n) -> p k n", k=KD) for i in range(2)]
            for c in range(NLT):
                for half in range(2):
                    b = 2 * c + half
                    take(b)
                    for k in range(KD):
                        if k == NCH:
                            pe.wait_ge(S["a_yt"], c + 1)
                        lhs = x0t[:, k, c * P:(c + 1) * P] if k < NCH else ymt[:, k - NCH, c * P:(c + 1) * P]
                        x = mm(B[b][:, :], lhs, wo[half][:, k, :], start=(k == 0), stop=(k == KD - 1))
                    last = c == NLT - 1
                    x.then_inc(S["p_w"] if last else S["p_y"], 1)
                    users[b] = (S["v_x1"], b + 1)
            pe.wait_ge(d_wr, 16)
            for c in range(NLT):
                pe.wait_ge(S["v_xn2"], c + 1)
                for g in range(2):
                    b = 2 * (c % 2) + g
                    take(b)
                    for k in range(4):
                        x = tr(B[b][:, k * P:(k + 1) * P], xn2[:, c % 2, (4 * g + k) * P:(4 * g + k + 1) * P], idn)
                    x.then_inc(S["p_h2"], 1)
                    users[b] = (S["a_h2"] if g else S["v_h2"], c + 1)
                pe.wait_ge(S["a_h2"], c + 1)
                pe.wait_ge(S["v_h2"], c + 1)
                if c == 0:
                    take(4)
                for k in range(KD):
                    x = mm(B[4][0:E, c * P:(c + 1) * P], wr[:, k, :], h2t[:, k, c * P:(c + 1) * P],
                           start=(k == 0), stop=(k == KD - 1))
                x.then_inc(S["p_lg"], 1)
            pe.wait_ge(S["v_lgt"], 1)
            take(5)
            for c in range(NLT):
                x = tr(B[5][:, c * E:(c + 1) * E], lgt[0:E, c * P:(c + 1) * P], upper(E))
            x.then_inc(S["p_lgt"], 1)
            pe.wait_ge(S["v_aft"], 1)
            take(6)
            for c in range(NLT):
                x = tr(B[6][0:E, c * P:(c + 1) * P], aft[:, c, :], idn)
            x.then_inc(S["p_aft"], 1)
            pe.wait_ge(S["v_mk"], 1)
            take(7)
            for c in range(NLT):
                x = tr(B[7][:, c * E:(c + 1) * E], wka[0:E, c * P:(c + 1) * P], upper(E))
            x.then_inc(S["p_mk"], 1)
            pe.wait_ge(S["v_mkt"], 1)
            take(0)
            mm(B[0][:, 0:NLT * E], cst[:, C_UP:C_UP + P], mkt, start=True, stop=False)
            for s in range(1, NLT):
                x = mm(B[0][:, s * E:NLT * E], ones, mkt[:, 0:NLT - s, :], start=False, stop=(s == NLT - 1))
            x.then_inc(S["p_rk"], 1)
            pe.wait_ge(S["v_slot"], 2)

            with pe.Fori(0, NPAIR) as j:
                pe.wait_ge(S["v_sel"], 4 * j + 4)
                for g in range(2):
                    for k in range(4):
                        for c in range(NLT):
                            dk = 4 * g + k
                            x = mm(B[6 + g][:, k * P:(k + 1) * P], x3[:, c, dk * P:(dk + 1) * P], psel[:, c, :],
                                   start=(c == 0), stop=(c == NLT - 1))
                    x.then_inc(S["p_xs"], 1)

                def ring_tile(kind, st):
                    i = TILES.index((kind, st))
                    per = NTI // NSLOT
                    pe.wait_ge(d_ring[i % NSLOT], 16 * (per * j + i // NSLOT + 1))
                    return slot(SLOT_OF[i % NSLOT])

                def gate_up(st):
                    e2 = st // 4
                    wg = ring_tile("g", st).rearrange("p (k n) -> p k n", k=KD)
                    wu = ring_tile("u", st).rearrange("p (k n) -> p k n", k=KD)
                    if st == 0:
                        pe.wait_ge(S["v_xs"], 4 * j + 4)
                        pe.wait_ge(S["a_xs"], 4 * j + 4)
                    if st >= 2:
                        pe.wait_ge(S["v_hid"], 8 * j + st - 1)
                    for k in range(KD):
                        lhs = xst[:, k, CAP * e2:CAP * (e2 + 1)]
                        mm(B[st % 2][0:CAP, :], lhs, wg[:, k, :], start=(k == 0), stop=(k == KD - 1))
                        x = mm(B[st % 2][CAP:P, :], lhs, wu[:, k, :], start=(k == 0), stop=(k == KD - 1))
                    x.then_inc(S["p_gu"], 1)

                def down(st):
                    e2, q = divmod(st, 4)
                    pe.wait_ge(S["v_hid"], 8 * j + st + 1)
                    for k in range(4):
                        x = tr(B[2 + st % 2][:, k * P:(k + 1) * P], hid[:, st % 2, k * P:(k + 1) * P], idn)
                    x.then_inc(S["p_ht"], 1)
                    wd = ring_tile("d", st).rearrange("p (k n) -> p k n", k=4)
                    pe.wait_ge(S["v_hdt"], 8 * j + st + 1)
                    for k in range(4):
                        for half in range(2):
                            x = mm(B[4 + e2][CAP * half:CAP * (half + 1), :], hdt[:, st % 2, k * CAP:(k + 1) * CAP],
                                   wd[:, k, half * CH:(half + 1) * CH],
                                   start=(q == 0 and k == 0), stop=(q == 3 and k == 3))
                    x.then_inc(S["p_dn"], 1)

                gate_up(0)
                gate_up(1)
                pe.wait_ge(S["g_sel"], 2 * j + 2)
                for c in range(NLT):
                    x = tr(B[6][:, c * P:(c + 1) * P], pw[:, c, :], idn)
                x.then_inc(S["p_pwt"], 1)
                down(0)
                for st in range(2, 8):
                    gate_up(st)
                    down(st - 1)
                down(7)
                pe.wait_ge(S["a_pwt"], j + 1)
                pe.wait_ge(S["a_ye"], 4 * j + 4)
                for n in range(2 * NLT):
                    c, half = divmod(n, 2)
                    if n >= 2:
                        pe.wait_ge(S["v_yacc"], 8 * j + n - 1)
                    mm(B[6 + half][:, :], pwt[:, c, :], ye[:, half * CH:(half + 1) * CH],
                       start=True, stop=True).then_inc(S["p_sca"], 1)
                pe.wait_ge(S["v_yacc"], 8 * j + 8)

        @block.scalar
        def _(act):
            a = nc.scalar
            act.dma_start(cx, A["ctx"][0].rearrange("(c p) n -> p c n", p=P)).then_inc(d_ctx, 16)
            act.dma_start(x3, A["x"][0].rearrange("(c p) n -> p c n", p=P)).then_inc(d_x, 16)
            act.dma_start(xn, A["pos"].rearrange("(c p) n -> p c n", p=P)).then_inc(d_pos, 16)
            act.wait_ge(S["g_zero"], 2)
            for g, (o, norm) in enumerate(((2 * D, "post_norm1"), (5 * D, "post_norm2"))):
                r = 64 * g
                act.dma_start(brow[r:r + 33:32, :], A["b_mod"][0, o:o + D].rearrange("(a n) -> a n", a=2)).then_inc(d_row, 16)
                act.dma_start(prow[r:r + 33:32, :], A[norm][0].rearrange("(a n) -> a n", a=2)).then_inc(d_row, 16)
            done = [0]

            def link(ins):
                done[0] += 1
                ins.then_inc(S["a_ch"], 1)
                act.wait_ge(S["a_ch"], done[0])

            act.wait_ge(S["v_vt"], 1)
            a.activation(mcur[:, 0:16], v1t[:, R_C:R_C + 16], ACT.Tanh, scale=0.5).then_inc(S["a_th"], 1)
            for n in range(3):
                act.wait_ge(S["v_arg"], n + 1)
                if n:
                    act.wait_ge(S["p_fil"], n + 1)
                a.activation(fh[0:FH, :], fa[0:FH, :], ACT.Sin).then_inc(S["a_fil"], 1)
            act.wait_ge(d_filt, 16 * N_FILT)
            act.wait_ge(d_cst, 16)
            for c in range(NLT):
                if c:
                    act.wait_ge(S["v_dec"], c)
                a.activation(dcy, dlb, ACT.Exp, scale=cst[:, C_TC + c:C_TC + c + 1]).then_inc(S["a_dec"], 1)
            act.wait_ge(d_ctx, 16)
            for t in range(NTT):
                if t == NCT:
                    act.wait_ge(S["v_x"], 1)
                src = cx[:, t, :] if t < NCT else x3[:, t - NCT, :]
                if t:
                    act.wait_ge(S["a_ss"], t)
                a.activation(sq, src, ACT.Square, accum_out=sst[:, t:t + 1]).then_inc(S["a_ss"], 1)
            act.wait_ge(S["a_ss"], NTT)
            act.wait_ge(S["g_zero"], 4)
            a.activation(std, sst, ACT.Sqrt, scale=1.0 / D, bias=epsc).then_inc(S["a_std"], 1)
            for n in range(8):
                act.wait_ge(S["p_ksp"], n + 1)
                a.activation(ksp[:, n % 2, n // 2, :], B[n][:, :], ACT.Copy).then_inc(S["a_ksp"], 1)
            act.wait_ge(S["v_aff"], 1)
            act.wait_ge(S["v_dec"], NLT)
            for k in range(KD):
                act.wait_ge(S["p_htl"], k + 1)
                a.activation(ht[:, k, LC:], B[3 + 2 * k % 5][:, :], ACT.Identity, scale=aff1[:, 0, 0, k:k + 1],
                             bias=aff1[:, 0, 1, k:k + 1]).then_inc(S["a_htl"], 1)
            act.wait_ge(S["p_gt"], 1)
            a.activation(gt[0:16, LC:], B[0][0:16, :], ACT.Copy).then_inc(S["a_gt"], 1)
            a.activation(gt[0:16, 0:LC], B[0][32:48, 0:LC], ACT.Copy).then_inc(S["a_gt"], 1)
            act.wait_ge(S["v_gsum"], 2)
            link(a.activation(th, th, ACT.Tanh, scale=1.0 / GCAP))
            link(a.activation(lf, th[:, :, :, 4:8], ACT.Exp, scale=-GCAP))
            a.activation(lf, lf, ACT.Ln, bias=1.0).then_inc(S["a_lf"], 1)
            act.wait_ge(S["v_ew"], 1)
            a.activation(ew, ew, ACT.Exp).then_inc(S["a_ew"], 1)
            for m in range(4):
                act.wait_ge(S["p_qk"], m + 1)
                dst = (qt if m < 2 else kt)[:, m % 2, :]
                a.activation(dst, B[qk_bank[m]][:, :], ACT.Copy, scale=DK ** -0.5 if m < 2 else 1.0)\
                    .then_inc(S["a_qk"], 1)
            for i in range(NCH):
                act.wait_ge(S["p_utr"], i + 1)
                a.activation(us[:, :, i * P:(i + 1) * P], B[i % 2][:, :].rearrange("p (c n) -> p c n", c=NLT),
                             ACT.Copy).then_inc(S["a_us"], 1)
            for g in range(2):
                act.wait_ge(S["p_ktr"], g + 1)
                a.activation(kk[:, NCT + 2 * g:NCT + 2 * g + 2, :],
                             B[g][:, :].rearrange("p (c n) -> p c n", c=2), ACT.Copy).then_inc(S["a_ktr"], 1)
            for t in range(NTT):
                if t < NTT - 1:
                    act.wait_ge(S["p_v"], t + 1)
                else:
                    act.wait_ge(S["p_w"], WT.index(("i", 4)) + 1)
                a.activation(v1[:, t, :, 0:DV], B[v_bank[t]][:, :].rearrange("p (h n) -> p h n", h=NH),
                             ACT.Copy).then_inc(S["a_v"], 1)
            for c in range(NLT):
                if c < NLT - 1:
                    act.wait_ge(S["p_o"], c + 1)
                else:
                    act.wait_ge(S["p_w"], WT.index(("i", 5)) + 1)
                a.activation(og[:, c, :], B[o_bank[c]][:, :], ACT.Tanh, scale=0.5).then_inc(S["a_o"], 1)
            for n in range(8):
                act.wait_ge(S["p_usp"], n + 1)
                a.activation(usp[:, n % 2, n // 2, :], B[usp_bank[n]][:, :], ACT.Copy).then_inc(S["a_usp"], 1)
            for h in range(NH):
                for d in range(2):
                    act.wait_ge(S["v_d"], 2 * h + d + 1)
                    a.activation(ebuf[:, d, :], ebuf[:, d, :], ACT.Exp, scale=-1.0).then_inc(S["a_e"], 1)
                for d in range(2):
                    for cp in range(2):
                        n = 4 * h + 2 * d + cp
                        act.wait_ge(S["p_num"], n + 1)
                        if n >= 2:
                            act.wait_ge(S["v_hs"], n - 1)
                        for c in (2 * cp, 2 * cp + 1):
                            o = (c % 2) * (DV + 1)
                            r = 32 * d + 4 * step_of(d, NCT + c) + h
                            a.activation(tot[:, n % 2, c % 2, :], B[5 + 2 * (n % 2)][:, o:o + DV + 1], ACT.Copy,
                                         scale=ew[:, 0, r:r + 1]).then_inc(S["a_n2"], 1)
            act.wait_ge(S["v_ssq"], 1)
            a.activation(ssq, ssq, ACT.Sqrt, scale=1.0 / DV, bias=epsc).then_inc(S["a_sq"], 1)
            for c in range(NLT):
                act.wait_ge(S["p_ytr"], c + 1)
                for h in range(NH):
                    x = a.activation(ymt[:, h, c * P:(c + 1) * P], B[c % 2][:, h * P:(h + 1) * P], ACT.Copy,
                                     scale=v2t[:, R_MLN + h:R_MLN + h + 1])
                x.then_inc(S["a_yt"], 1)

            def h2_half(c):
                act.wait_ge(S["p_h2"], 2 * c + 2)
                act.wait_ge(S["v_aff"], 3)
                for k in range(4):
                    x = a.activation(h2t[:, 4 + k, c * P:(c + 1) * P], B[2 * (c % 2) + 1][:, k * P:(k + 1) * P],
                                     ACT.Identity, scale=aff2[:, 0, 4 + k:5 + k], bias=aff2[:, 1, 4 + k:5 + k])
                x.then_inc(S["a_h2"], 1)

            for c in range(NLT):
                for half in range(2):
                    if c < NLT - 1:
                        act.wait_ge(S["p_y"], 2 * c + half + 1)
                    else:
                        act.wait_ge(S["p_w"], len(WT) - 1 + half)
                    link(a.activation(junk[:, 0:CH], B[2 * c + half][:, :], ACT.Square,
                                      accum_out=(sy if half else sst)[:, c:c + 1]))
                a.activation(sy[:, c:c + 1], sy[:, c:c + 1], ACT.Identity, bias=sst[:, c:c + 1]).then_inc(S["a_sy"], 1)
                act.wait_ge(S["a_sy"], c + 1)
                a.activation(sdy[:, c:c + 1], sy[:, c:c + 1], ACT.Sqrt, scale=1.0 / D, bias=epsc).then_inc(S["a_sdy"], 1)
                act.wait_ge(S["v_x1"], 2 * c + 2)
                link(a.activation(junk, x3[:, c, :], ACT.Square, accum_out=ss2[:, c:c + 1]))
                a.activation(sd2[:, c:c + 1], ss2[:, c:c + 1], ACT.Sqrt, scale=1.0 / D, bias=epsc).then_inc(S["a_ss2"], 1)
                if c:
                    h2_half(c - 1)
            h2_half(NLT - 1)
            act.wait_ge(S["v_sub"], 1)
            a.activation(lg, lg, ACT.Exp).then_inc(S["a_exp"], 1)

            with act.Fori(0, NPAIR) as j:
                act.wait_ge(S["p_xs"], 2 * j + 2)
                for k in range(4):
                    a.activation(xst[:, 4 + k, :], B[7][:, k * P:(k + 1) * P], ACT.Identity,
                                 scale=aff2[:, 0, 4 + k:5 + k], bias=aff2[:, 1, 4 + k:5 + k]).then_inc(S["a_xs"], 1)

                def silu(st):
                    act.wait_ge(S["p_gu"], 8 * j + st + 1)
                    if st >= 2:
                        act.wait_ge(S["v_hid"], 8 * j + st - 1)
                    a.activation(sil[CAP:P, st % 2, :], B[st % 2][0:CAP, :], ACT.Silu).then_inc(S["a_sil"], 1)

                def results(e2):
                    act.wait_ge(S["p_dn"], 8 * j + 4 * e2 + 4)
                    for half in range(2):
                        a.activation(ye[CAP * e2:CAP * (e2 + 1), half * CH:(half + 1) * CH],
                                     B[4 + e2][CAP * half:CAP * (half + 1), :], ACT.Copy).then_inc(S["a_ye"], 1)

                silu(0)
                silu(1)
                act.wait_ge(S["p_pwt"], j + 1)
                a.activation(pwt, B[6][:, :].rearrange("p (c n) -> p c n", c=NLT), ACT.Copy).then_inc(S["a_pwt"], 1)
                for st in range(2, 5):
                    silu(st)
                results(0)
                for st in range(5, 8):
                    silu(st)
                results(1)
            for c in range(NLT):
                act.wait_ge(S["v_yacc"], 8 * NPAIR)
                link(a.activation(xst[:, :, :].rearrange("p k n -> p (k n)"), y3[:, c, :], ACT.Square,
                                  accum_out=ss2[:, c:c + 1]))
                a.activation(sd2[:, c:c + 1], ss2[:, c:c + 1], ACT.Sqrt, scale=1.0 / D, bias=epsc).then_inc(S["a_fsd"], 1)

        @block.vector
        def _(dve):
            v = nc.vector
            done = [0]

            def link(ins):
                done[0] += 1
                ins.then_inc(S["v_ch"], 1)
                dve.wait_ge(S["v_ch"], done[0])

            def stt(out_, in0, sc, in1, op0, op1):
                return v.scalar_tensor_tensor(out=out_, in0=in0, scalar=sc, in1=in1, op0=op0, op1=op1)

            dve.wait_ge(S["p_vt"], 2)
            v.tensor_copy(v1t, B[0][:, 0:R1_ROWS]).then_inc(S["v_vt"], 1)
            v.tensor_copy(v2t, B[1][:, 0:R2_ROWS]).then_inc(S["v_vt"], 1)
            dve.wait_ge(S["a_th"], 1)
            dve.wait_ge(S["g_zero"], 3)
            link(stt(mcur[:, 16:32], mcur[:, 0:16], 1.0, v1t[:, R_C:R_C + 16], ALU.add, ALU.mult))
            v.tensor_scalar(cpad[:, :, 0:2], mcur[:, 16:32].rearrange("p (w k) -> p k w", w=2), 0.5, None,
                            ALU.mult).then_inc(S["v_cpad"], 1)
            dve.wait_ge(S["v_vt"], 2)
            for n in range(3):
                dve.wait_ge(S["p_fil"], n + 1)
                src = B[2 + n % 2][0:FH, :]
                link(v.tensor_scalar(ft[0:FH, :], src, v2t[0:FH, R_FB + n:R_FB + n + 1], v2t[0:FH, R_FQ:R_FQ + 1],
                                     ALU.add, ALU.mult))
                link(v.tensor_scalar(fa[0:FH, :], ft[0:FH, :], 1.0 / TWO_PI, MAGIC, ALU.mult, ALU.add))
                link(v.tensor_scalar(fa[0:FH, :], fa[0:FH, :], MAGIC, None, ALU.subtract))
                link(stt(fa[0:FH, :], fa[0:FH, :], -TWO_PI, ft[0:FH, :], ALU.mult, ALU.add))
                v.tensor_scalar(fa[0:FH, :], fa[0:FH, :], PI_IN, -PI_IN, ALU.min, ALU.max).then_inc(S["v_arg"], 1)
                dve.wait_ge(S["a_fil"], n + 1)
            link(v.memset(tmask, 1.0))
            link(v.memset(tmask[0:1, :], 0.0))
            for c in range(NLT):
                dve.wait_ge(S["p_kf"], 2 * c + 2)
                dve.wait_ge(S["a_dec"], c + 1)
                b = 4 + 2 * (c % 2)
                v.tensor_tensor(fhf, B[b][:, :], dcy, ALU.mult).then_inc(S["v_kf"], 1)
                v.tensor_tensor(fhb, B[b + 1][:, :], dcy, ALU.mult).then_inc(S["v_kf"], 1)
                dve.wait_ge(S["v_kf"], 2 * c + 2)
                if c == 0:
                    link(v.tensor_scalar(fhb, fhb, tmask, None, ALU.mult))
                v.tensor_tensor(hpm[:, 0, c, :], fhf, fhb, ALU.add).then_inc(S["v_dec"], 1)
                link(v.tensor_tensor(hpm[:, 1, c, :], fhf, fhb, ALU.subtract))
            dve.wait_ge(d_filt, 16 * N_FILT)
            v.tensor_tensor(hpm[0:1, 0, 0, :], hpm[0:1, 0, 0, :], hyb[0:1, :], ALU.add).then_inc(S["v_hpm"], 1)
            dve.wait_ge(d_x, 16)
            dve.wait_ge(d_pos, 16)
            v.tensor_tensor(xl[:, :], xl[:, :], slot(6), ALU.add).then_inc(S["v_x"], 1)
            dve.wait_ge(S["a_std"], 1)
            link(v.reciprocal(rst, std))
            dve.wait_ge(S["v_x"], 1)
            for t in range(NTT):
                src = cx[:, t, :] if t < NCT else x3[:, t - NCT, :]
                dst = cx[:, t, :] if t < NCT else xn[:, t - NCT, :]
                v.tensor_scalar(dst, src, rst[:, t:t + 1], None, ALU.mult).then_inc(S["v_xn"], 1)

            def mod_rows(r):
                if r < 3:
                    dve.wait_ge(S["p_w"], WT.index(("m", 4 * r + 3)) + 1)
                    if r:
                        dve.wait_ge(S["p_modt"], r)
                    if r == 2:
                        dve.wait_ge(S["p_g1"], 2)
                    v.tensor_copy(mrow, B[2][:, :]).then_inc(S["v_mrow"], 1)

            def turned(b, i0, w):
                return B[b][:, :].rearrange("p (q i u) -> p i q u", q=4, i=4)[:, i0:i0 + 2, :, w]

            def two(apx):
                return apx.rearrange("p (i q) -> p i q", i=2)

            mod_rows(0)
            dve.wait_ge(S["p_modt"], 1)
            for w in range(2):
                link(v.tensor_tensor(two(aff1[:, w, 0, :]), turned(1, 2, w), two(v1t[:, R_BMOD + 8:R_BMOD + 16]), ALU.add))
                link(stt(aff1[:, w, 0, :], aff1[:, w, 0, :], 1.0, v1t[:, R_PRE1:R_PRE1 + 8], ALU.add, ALU.mult))
                x = v.tensor_tensor(two(aff1[:, w, 1, :]), turned(1, 0, w), two(v1t[:, R_BMOD:R_BMOD + 8]), ALU.add)
                link(x) if w == 0 else x.then_inc(S["v_aff"], 1)
            dve.wait_ge(S["v_aff"], 1)
            for k in range(KD):
                dve.wait_ge(S["p_htc"], k + 1)
                v.tensor_scalar(ht[:, k, 0:LC], B[3 + (2 * k + 1) % 5][:, 0:LC], aff1[:, 1, 0, k:k + 1],
                                aff1[:, 1, 1, k:k + 1], ALU.mult, ALU.add).then_inc(S["v_htc"], 1)

            dve.wait_ge(S["p_ksp"], 8)
            link(v.memset(v1[:, :, :, DV:DV + 1], 1.0))
            link(v.memset(ew, 0.0))
            link(v.memset(aco, 0.0))
            link(v.memset(atp, -BIG))
            link(v.memset(mprev, 0.0))
            link(v.memset(mend, 0.0))

            def conv(n):
                i, m = divmod(n, NCH)
                if m < NCH - 1:
                    dve.wait_ge(S["p_hy"], 3 * i + m + 1)
                else:
                    dve.wait_ge(S["p_w"], WT.index(("i", i)) + 1)
                src = B[hy_bank[n]]
                dst = (x0t[:, m, :], ut[:, m, :], ctmp[:, m % 2, :])[i]
                w = [v2t[:, R_CW + 12 * s + n:R_CW + 12 * s + n + 1] for s in range(3)]
                link(v.tensor_scalar(dst, src[:, :], w[1], v2t[:, R_CB + n:R_CB + n + 1], ALU.mult, ALU.add))
                link(stt(dst[:, 1:L], src[:, 0:L - 1], w[0], dst[:, 1:L], ALU.mult, ALU.add))
                x = stt(dst[:, 0:L - 1], src[:, 1:L], w[2], dst[:, 0:L - 1], ALU.mult, ALU.add)
                if i < 2:
                    x.then_inc(S["v_conv"], 1)
                else:
                    link(x)
                    v.tensor_tensor(ut[:, m, :], ut[:, m, :], dst, ALU.mult).then_inc(S["v_conv"], 1)

            for n in range(4):
                conv(n)
            dve.wait_ge(S["p_gtr"], 1)
            dve.wait_ge(d_gate, 32)
            for d in range(2):
                o = d * NTT * 16
                src = B[1][:, o:o + NTT * 16].rearrange("p (s n) -> p s n", s=NTT)[:, :, 8 * d:8 * d + 8]
                bias = gb[:, 8 * d:8 * d + 8].unsqueeze(1).broadcast_to([P, NTT, 8])
                v.tensor_tensor(th[:, d, :, :], src, bias, ALU.add).then_inc(S["v_gsum"], 1)
            for n in range(4, 8):
                conv(n)
            dve.wait_ge(S["p_cs"], 1)

            def packed(apx):
                return apx.rearrange("p (d n) -> p d n", d=2)[:, :, 0:24]
            link(v.tensor_copy(packed(ew[:, 1, :]), packed(B[0][:, 0:64])))
            link(v.tensor_copy(packed(ew[:, 3, :]), packed(B[0][:, 64:128])))
            for d in range(2):
                x = stt(aco[:, 32 * d:32 * d + 24], th[:, d, :, 0:4], GCAP, ew[:, 1, 32 * d:32 * d + 24]
                        .rearrange("p (s h) -> p s h", s=NTT), ALU.mult, ALU.add)
                link(x) if d == 0 else x.then_inc(S["v_cs"], 1)
            conv(8)
            dve.wait_ge(S["p_at"], 1)
            v.tensor_copy(atp[0:64, 0, 64:192], B[1][0:64, 0:P]).then_inc(S["v_at"], 1)
            dve.wait_ge(S["v_at"], 1)
            for n in range(7):
                s = 1 << n
                src, dst = atp[:, n % 2, :], atp[:, 1 - n % 2, :]
                link(v.tensor_tensor(dst[0:32, 64:192], src[0:32, 64:192], src[0:32, 64 - s:192 - s], ALU.max))
                link(v.tensor_tensor(dst[32:64, 64:192], src[32:64, 64:192], src[32:64, 64 + s:192 + s], ALU.max))
            link(v.tensor_copy(mrow_t[0:32, 0:1], atp[0:32, 1, 191:192]))
            v.tensor_copy(mrow_t[32:64, 0:1], atp[32:64, 1, 64:65]).then_inc(S["v_cum"], 1)
            for n in range(9, 12):
                conv(n)
            dve.wait_ge(S["p_cm"], 1)
            by_dir = lambda t, s: t.rearrange("p (d n) -> p d n", d=2)[:, :, 4 * s:4 * s + 4]
            for s in range(NTT):
                link(v.tensor_tensor(by_dir(mend, s), by_dir(mprev, s), by_dir(B[0][:, 64:128], s), ALU.max))
                if s + 1 < NTT:
                    link(v.tensor_tensor(by_dir(mprev, s + 1), by_dir(mend, s), by_dir(ew[:, 3, :], s), ALU.subtract))
            v.tensor_tensor(mcur, B[0][:, 0:64], mprev, ALU.max).then_inc(S["v_m"], 1)
            dve.wait_ge(S["v_m"], 1)
            link(v.tensor_tensor(ew[:, 0, :], mprev, mcur, ALU.subtract))
            link(v.tensor_tensor(ew[:, 1, :], ew[:, 1, :], mcur, ALU.subtract))
            link(v.tensor_tensor(ew[:, 2, :], aco, mend, ALU.subtract))
            v.tensor_tensor(ew[:, 3, :], mprev, mend, ALU.subtract).then_inc(S["v_ew"], 1)
            dve.wait_ge(S["p_mt"], 1)
            v.tensor_copy(mrow_t[0:64, :], B[1][0:64, 0:P]).then_inc(S["v_mt"], 1)
            dve.wait_ge(S["a_ew"], 1)
            for p in range(2):
                q = slice(64 * p, 64 * p + 64)
                src = ew[q, 3, :].rearrange("p (d n) -> p d n", d=2)[:, :, p:24:2]
                x = v.tensor_copy(wcp[q, :].rearrange("p (d n) -> p d n", d=2), src)
                link(x)
            for c in range(NCT):
                if c < NCT - 1:
                    dve.wait_ge(S["p_kc"], c + 1)
                else:
                    dve.wait_ge(S["p_w"], WT.index(("i", 3)) + 1)
                v.tensor_copy(kk[:, c, :], B[kc_bank[c]][:, 0:QK]).then_inc(S["v_kc"], 1)

            def gate_row(g):
                dve.wait_ge(S["p_modt"], g + 2)
                dve.wait_ge(d_row, 64)
                dve.wait_ge(S["v_mrow"], g + 2)
                link(v.tensor_tensor(mrow, mrow, brow, ALU.add))
                v.tensor_tensor(mrow, mrow, prow, ALU.mult).then_inc(S["v_grow"], 1)
                for h in range(2):
                    dve.wait_ge(S["p_g1"], 2 * g + h + 1)
                    v.tensor_copy((g1p, g2p)[g][:, h * CH:(h + 1) * CH], B[h][:, :]).then_inc(S["v_cp"], 1)

            mod_rows(1)
            dve.wait_ge(S["p_modt"], 2)
            v.tensor_tensor(two(aff2[:, 1, :]), turned(1, 2, 0), two(v1t[:, R_BMOD + 24:R_BMOD + 32]),
                            ALU.add).then_inc(S["v_aff"], 1)
            gate_row(0)
            mod_rows(2)
            for k in range(NLT):
                dve.wait_ge(S["a_usp"], 2 * k + 2)
                ur, ui, kr, ki = usp[:, 0, k, :], usp[:, 1, k, :], ksp[:, 0, k, :], ksp[:, 1, k, :]
                link(v.tensor_tensor(ctmp[:, 0, :], ur, kr, ALU.mult))
                link(v.tensor_tensor(ctmp[:, 1, :], ui, ki, ALU.mult))
                link(v.tensor_tensor(kr, ui, kr, ALU.mult))
                link(v.tensor_tensor(ki, ur, ki, ALU.mult))
                link(v.tensor_tensor(ur, ctmp[:, 0, :], ctmp[:, 1, :], ALU.subtract))
                v.tensor_tensor(ui, kr, ki, ALU.add).then_inc(S["v_cx"], 1)
            n = 0
            for st in range(NTT - 1):
                for d in range(2):
                    dve.wait_ge(S["p_st"], n + 1)
                    if n >= 2:
                        dve.wait_ge(S["v_st"], n - 1)
                    for p in range(2):
                        o = slice(p * (DV + 1), (p + 1) * (DV + 1))
                        src = B[n % 2][:, o]
                        if st == 0:
                            x = v.tensor_copy(cstate[:, d, 0, o], src)
                        else:
                            q = d * 12 + 2 * st + p
                            x = stt(cstate[:, d, st - 1, o], cstate[:, d, max(st - 2, 0), o], wcp[:, q:q + 1], src,
                                    ALU.mult, ALU.add)
                        link(x) if p == 0 else x.then_inc(S["v_st"], 1)
                    n += 1
            dve.wait_ge(S["p_modt"], 3)
            link(v.tensor_tensor(two(aff2[:, 0, :]), turned(2, 0, 0), two(v1t[:, R_BMOD + 32:R_BMOD + 40]), ALU.add))
            stt(aff2[:, 0, :], aff2[:, 0, :], 1.0, v1t[:, R_PRE2:R_PRE2 + 8], ALU.add, ALU.mult).then_inc(S["v_aff"], 1)
            gate_row(1)

            def h2_half(c):
                dve.wait_ge(S["p_h2"], 2 * c + 1)
                for k in range(4):
                    x = v.tensor_scalar(h2t[:, k, c * P:(c + 1) * P], B[2 * (c % 2)][:, k * P:(k + 1) * P],
                                        aff2[:, 0, k:k + 1], aff2[:, 1, k:k + 1], ALU.mult, ALU.add)
                x.then_inc(S["v_h2"], 1)

            def weights_of(h):
                for d in range(2):
                    dve.wait_ge(S["p_mb"], 2 * h + d + 1)
                    if h:
                        dve.wait_ge(S["p_num"], 4 * (h - 1) + 2 * d + 2)
                    for c in range(NLT):
                        r = 32 * d + 4 * step_of(d, NCT + c) + h
                        x = stt(ebuf[:, d, c * P:(c + 1) * P], B[2 + d][:, c * P:(c + 1) * P], aco[:, r:r + 1],
                                cst[:, (C_BF, C_BB)[d]:(C_BF, C_BB)[d] + P], ALU.subtract, ALU.max)
                    x.then_inc(S["v_d"], 1)

            def times_scores(h):
                dve.wait_ge(S["p_sc"], h + 1)
                for d in range(2):
                    dve.wait_ge(S["a_e"], 2 * h + d + 1)
                    v.tensor_tensor(ebuf[:, d, :], ebuf[:, d, :], B[h % 2][:, :], ALU.mult).then_inc(S["v_sw"], 1)

            weights_of(0)
            times_scores(0)
            for i in range(NCH):
                dve.wait_ge(S["p_inv"], i + 1)
                v.tensor_tensor(x0t[:, i, :], x0t[:, i, :], B[4 + i][:, :], ALU.mult).then_inc(S["v_inv"], 1)
            for h in range(NH):
                for d in range(2):
                    for cp in range(2):
                        n = 4 * h + 2 * d + cp
                        dve.wait_ge(S["a_n2"], 2 * n + 2)
                        t = tot[:, n % 2, :, :]
                        v.tensor_tensor(t, t, B[4 + 2 * (n % 2)][:, 0:2 * (DV + 1)].rearrange("p (c n) -> p c n", c=2),
                                        ALU.add).then_inc(S["v_tot"], 1)
                        dve.wait_ge(S["v_tot"], n + 1)
                        r = [32 * d + 4 * step_of(d, NCT + 2 * cp + c) + h for c in range(2)]
                        em = ew[:, 1, r[0]:r[0] + 5:4] if r[1] > r[0] else ew[:, 1, r[1]:r[1] + 5:4][:, ::-1]
                        dd = dab[:, n % 4, :].unsqueeze(2)
                        link(v.tensor_tensor(dd, t[:, :, DV:DV + 1], em.unsqueeze(2), ALU.max))
                        link(stt(dd, t[:, :, DV:DV + 1], -1.0, dd, ALU.mult, ALU.max))
                        link(v.reciprocal(dab[:, n % 4, :], dab[:, n % 4, :]))
                        rb = dab[:, n % 4, :].unsqueeze(2).broadcast_to([P, 2, DV])
                        dst = hsum[:, 2 * cp:2 * cp + 2, h * DV:(h + 1) * DV]
                        if d == 0:
                            v.tensor_tensor(dst, t[:, :, 0:DV], rb, ALU.mult).then_inc(S["v_hs"], 1)
                        else:
                            link(v.tensor_tensor(t[:, :, 0:DV], t[:, :, 0:DV], rb, ALU.mult))
                            v.tensor_tensor(dst, dst, t[:, :, 0:DV], ALU.add).then_inc(S["v_hs"], 1)
                if h + 1 < NH:
                    weights_of(h + 1)
                    times_scores(h + 1)
            dve.wait_ge(S["v_hs"], 16)
            hq = usq
            hs2 = hsum.rearrange("p c (h n) -> p (c h) n", h=NH)
            link(v.tensor_tensor(hq, hs2, hs2, ALU.mult))
            v.tensor_reduce(ssq, hq, AX.X, ALU.add).then_inc(S["v_ssq"], 1)
            link(v.tensor_scalar(v2t[:, R_MLN:R_MLN + NH], v2t[:, R_MLN:R_MLN + NH], 0.5, None, ALU.mult))
            dve.wait_ge(S["a_sq"], 1)
            link(v.reciprocal(ssq, ssq))
            for c in range(NLT):
                hc = hsum[:, c, :].rearrange("p (h n) -> p h n", h=NH)
                link(v.tensor_tensor(hc, hc, ssq[:, 4 * c:4 * c + 4].unsqueeze(2).broadcast_to([P, NH, DV]), ALU.mult))
                stt(hsum[:, c, :], og[:, c, :], 1.0, hsum[:, c, :], ALU.add, ALU.mult).then_inc(S["v_hn"], 1)
            for c in range(NLT):
                dve.wait_ge(S["a_sdy"], c + 1)
                link(v.reciprocal(ry[:, c:c + 1], sdy[:, c:c + 1]))
                for half in range(2):
                    h = slice(half * CH, (half + 1) * CH)
                    t = ctmp[:, half, :]
                    link(stt(t, B[2 * c + half][:, :], ry[:, c:c + 1], g1p[:, h], ALU.mult, ALU.mult))
                    v.tensor_tensor(x3[:, c, h], x3[:, c, h], t, ALU.add).then_inc(S["v_x1"], 1)
                dve.wait_ge(S["a_ss2"], c + 1)
                link(v.reciprocal(rs2[:, c:c + 1], sd2[:, c:c + 1]))
                if c >= 2:
                    dve.wait_ge(S["p_h2"], 2 * (c - 1))
                dve.wait_ge(S["v_x1"], 2 * c + 2)
                v.tensor_scalar(xn2[:, c % 2, :], x3[:, c, :], rs2[:, c:c + 1], None, ALU.mult).then_inc(S["v_xn2"], 1)
                if c:
                    h2_half(c - 1)
            h2_half(NLT - 1)
            dve.wait_ge(S["p_lg"], NLT)
            v.tensor_copy(lgt[0:E, :], B[4][0:E, :]).then_inc(S["v_lgt"], 1)
            dve.wait_ge(S["p_lgt"], 1)
            l5 = B[5][:, 0:NLT * E].rearrange("p (c e) -> p c e", c=NLT)
            link(v.tensor_reduce(mx4, l5, AX.X, ALU.max))
            v.tensor_tensor(lg, l5, mx4.unsqueeze(2).broadcast_to([P, NLT, E]), ALU.subtract).then_inc(S["v_sub"], 1)
            dve.wait_ge(S["a_exp"], 1)
            link(v.tensor_reduce(sm4, lg, AX.X, ALU.add))
            link(v.reciprocal(rc4, sm4))
            v.tensor_tensor(aft, lg, rc4.unsqueeze(2).broadcast_to([P, NLT, E]), ALU.mult).then_inc(S["v_aft"], 1)
            dve.wait_ge(S["v_aft"], 1)
            v.tensor_copy(affr, aft.rearrange("p c e -> p e c")).then_inc(S["v_slot"], 1)
            dve.wait_ge(S["p_aft"], 1)
            link(v.tensor_copy(lgt[0:E, :], B[6][0:E, :]))
            cur = lgt
            for r in range(CAP // 8):
                nxt = wka if r % 2 == 0 else wkb
                link(v.max(out=top8[0:E, :], in_=cur[0:E, :]))
                link(v.match_replace(out=nxt[0:E, :], in_to_replace=top8[0:E, :], in_values=cur[0:E, :], imm_value=-1.0))
                cur = nxt
            v.tensor_tensor(wka[0:E, :], cur[0:E, :], lgt[0:E, :], ALU.not_equal).then_inc(S["v_mk"], 1)
            dve.wait_ge(S["p_mk"], 1)
            v.tensor_copy(mkt, B[7][:, 0:NLT * E].rearrange("p (c e) -> p c e", c=NLT)).then_inc(S["v_mkt"], 1)
            link(v.memset(yacc[:, :], 0.0))
            link(v.memset(hid[0:CAP, :, :], 0.0))
            dve.wait_ge(S["p_rk"], 1)
            sl = slotm.rearrange("p e c -> p c e")
            link(v.tensor_tensor(sl, B[0][:, 0:NLT * E].rearrange("p (c e) -> p c e", c=NLT), mkt, ALU.mult))
            v.tensor_scalar(slotm, slotm, -1.0, None, ALU.add).then_inc(S["v_slot"], 1)

            dve.wait_ge(S["v_slot"], 2)

            with dve.Fori(0, NPAIR) as j:
                v.tensor_copy(slp, slotm[:, bass.ds(2 * j, 2), :].rearrange("p e c -> p (e c)")).then_inc(S["v_sel"], 1)
                dve.wait_ge(S["v_sel"], 4 * j + 1)
                for e2 in range(2):
                    io = cst[:, C_IO:C_IO + CAP].unsqueeze(1).broadcast_to([P, NLT, CAP])
                    sl = slp[:, 4 * e2:4 * e2 + 4].unsqueeze(2).broadcast_to([P, NLT, CAP])
                    v.tensor_tensor(peq[:, :, CAP * e2:CAP * e2 + CAP], io, sl, ALU.is_equal).then_inc(S["v_sel"], 1)
                dve.wait_ge(S["v_sel"], 4 * j + 3)
                v.tensor_tensor(psel, peq, rs2.unsqueeze(2).broadcast_to([P, NLT, P]), ALU.mult)\
                    .then_inc(S["v_sel"], 1)
                dve.wait_ge(S["p_xs"], 2 * j + 1)
                for k in range(4):
                    v.tensor_scalar(xst[:, k, :], B[6][:, k * P:(k + 1) * P], aff2[:, 0, k:k + 1], aff2[:, 1, k:k + 1],
                                    ALU.mult, ALU.add).then_inc(S["v_xs"], 1)

                def hidden(st):
                    dve.wait_ge(S["a_sil"], 8 * j + st + 1)
                    if st >= 2:
                        dve.wait_ge(S["p_ht"], 8 * j + st - 1)
                    v.tensor_tensor(hid[CAP:P, st % 2, :], sil[CAP:P, st % 2, :], B[st % 2][CAP:P, :],
                                    ALU.mult).then_inc(S["v_hid"], 1)

                def turned_hidden(st):
                    dve.wait_ge(S["p_ht"], 8 * j + st + 1)
                    if st >= 2:
                        dve.wait_ge(S["p_dn"], 8 * j + st - 1)
                    v.tensor_copy(hdt[:, st % 2, :].rearrange("p (k n) -> p k n", k=4),
                                  B[2 + st % 2][:, :].rearrange("p (k n) -> p k n", k=4)[:, :, CAP:P])\
                        .then_inc(S["v_hdt"], 1)

                hidden(0)
                hidden(1)
                turned_hidden(0)
                for st in range(2, 8):
                    hidden(st)
                    turned_hidden(st - 1)
                turned_hidden(7)
                for n in range(2 * NLT):
                    c, half = divmod(n, 2)
                    dve.wait_ge(S["p_sca"], 8 * j + n + 1)
                    dst = y3[:, c, half * CH:(half + 1) * CH]
                    v.tensor_tensor(dst, dst, B[6 + half][:, :], ALU.add).then_inc(S["v_yacc"], 1)
            for c in range(NLT):
                dve.wait_ge(S["a_fsd"], c + 1)
                link(v.reciprocal(ry[:, c:c + 1], sd2[:, c:c + 1]))
                dve.wait_ge(S["v_yacc"], 8 * NPAIR)
                link(stt(y3[:, c, :], y3[:, c, :], ry[:, c:c + 1], g2p[:, :], ALU.mult, ALU.mult))
                v.tensor_tensor(y3[:, c, :], y3[:, c, :], x3[:, c, :], ALU.add).then_inc(S["v_res"], 1)


NAMES = ["x", "c", "ctx", "c_ctx", "w_mod", "b_mod", "pre_norm1", "post_norm1", "pre_norm2", "post_norm2",
         "w_in", "conv_w", "conv_b", "filt_w1", "filt_b1", "filt_w2", "filt_b2", "filt_w3", "filt_b3", "filt_w4",
         "filt_freq", "hyena_bias", "ml_gate_b", "ml_norm", "w_out", "w_router", "w_exp_gate", "w_exp_up",
         "w_exp_down"]


def kernel(**inputs):
    import concourse.bacc as bacc
    from concourse.bass_utils import run_bass_kernel_spmd

    nc = bacc.Bacc("TRN2", target_bir_lowering=False, num_devices=1)
    arrays = {n: np.ascontiguousarray(inputs[n]) for n in NAMES}
    arrays.update(shape_constants())
    A = {n: nc.dram_tensor(f"in_{n}", a.shape, mybir.dt.from_np(a.dtype), kind="ExternalInput").ap()
         for n, a in arrays.items()}
    out = nc.dram_tensor("out", (1, L, D), F32, kind="ExternalOutput").ap()
    block_kernel(nc, A, out)
    r = run_bass_kernel_spmd(nc, [{f"in_{n}": a for n, a in arrays.items()}], core_ids=[0])
    return r.results[0]["out"]
```

```python
import math
from contextlib import ExitStack

import numpy as np

import concourse.bass as bass
from concourse import mybir

F32 = mybir.dt.float32
ALU = mybir.AluOpType
ACT = mybir.ActivationFunctionType
AX = mybir.AxisListType

D, L, LC = 1024, 512, 256
P = 128
KD = D // P
NLT, NCT = L // P, LC // P
NTT = NLT + NCT
HY, DK, DV, NH = 512, 64, 128, 4
QK = NH * DK
GRID_W = 64
E, FF, CAP = 16, 2048, 64
BANDS, FEMB, FH = 16, 33, 64
EPS = 1e-6
GCAP = 15.0
NCH = HY // P
BIG = 1e30
NSLOT, SLOTF = 8, 4096
CH = 512
NKW = 8
TWO_PI = 2.0 * math.pi
MAGIC = 12582912.0
TURN = 2 * 3.1415925

R_C, R_CC, R_PRE1, R_PRE2, R_BMOD = 0, 8, 16, 24, 32
R1_ROWS = 80
R_CW, R_CB, R_MLN, R_FB, R_FQ = 0, 36, 48, 52, 55
R2_ROWS = 56

C_ID, C_UP, C_LO, C_ONE, C_BF, C_BB, C_IO, C_TC = 0, 128, 256, 384, 512, 640, 768, 832
C_COLS = 836


def shape_constants():
    i = np.arange(P)
    cst = np.zeros((P, C_COLS), np.float32)
    cst[:, C_ID:C_ID + P] = np.eye(P)
    cst[:, C_UP:C_UP + P] = i[:, None] <= i[None, :]
    cst[:, C_LO:C_LO + P] = i[:, None] >= i[None, :]
    cst[:, C_ONE:C_ONE + P] = 1.0
    cst[:, C_BF:C_BF + P] = np.where(i[:, None] <= i[None, :], 0.0, BIG)
    cst[:, C_BB:C_BB + P] = np.where(i[:, None] >= i[None, :], 0.0, BIG)
    cst[:, C_IO:C_IO + CAP] = np.arange(CAP)[None, :]
    tpos = np.linspace(0.0, 1.0, L, dtype=np.float32)
    cst[:, C_TC:C_TC + NLT] = -tpos.reshape(NLT, P).T
    quarter = D // 4
    omega = 1.0 / (10000.0 ** (np.arange(quarter, dtype=np.float64) / quarter))

    def emb(n):
        ang = np.arange(n, dtype=np.float64)[:, None] * omega[None, :]
        return np.concatenate([np.sin(ang), np.cos(ang)], axis=-1)
    rows = L // GRID_W
    er, ec = emb(rows), emb(GRID_W)
    pe = np.concatenate([np.broadcast_to(er[:, None, :], (rows, GRID_W, D // 2)),
                         np.broadcast_to(ec[None, :, :], (rows, GRID_W, D // 2))], axis=-1)
    pe = np.ascontiguousarray(pe.reshape(L, D).astype(np.float32))
    w = 2.0 * np.pi * np.arange(L) / L
    f = np.linspace(1e-4, BANDS - 1, BANDS)
    ang = w[:, None] * f[None, :]
    zf = np.concatenate([tpos[:, None].astype(np.float64), np.cos(ang), -np.sin(ang)], axis=-1)
    zft = np.ascontiguousarray(zf.T.astype(np.float32))
    lo, hi = math.log(1e-2) / 1.5, math.log(1e-2) / 0.3
    deltas = np.abs(np.linspace(lo, hi, HY, dtype=np.float32))
    dl = np.ascontiguousarray(np.broadcast_to(deltas[None, :], (P, HY)).astype(np.float32))
    t = np.arange(L, dtype=np.float64)
    a = (np.pi / L) * (t[:, None] * (t[None, :] + 0.5))
    fwd = np.stack([np.cos(a), np.sin(a)])
    inv = np.stack([np.cos(a).T, np.sin(a).T]) / L

    def tiles(m):
        return np.ascontiguousarray(
            m.reshape(2, NLT, P, L).transpose(2, 0, 1, 3).reshape(P, 2 * NLT * L).astype(np.float32))
    return {"cst": cst, "pos": pe, "zft": zft, "dl": dl, "dft": tiles(fwd), "idft": tiles(inv)}


def step_of(d, tile):
    if d == 0:
        return tile
    return NCT - 1 - tile if tile < NCT else NTT - 1 - (tile - NCT)


def block_kernel(nc, A, out):
    ctx = ExitStack()
    with ctx:
        def sb(name, cols, rows=P):
            return ctx.enter_context(nc.sbuf_tensor(name, [rows, cols], F32))

        def sem(name):
            return ctx.enter_context(nc.semaphore(name))

        ring = sb("ring", NSLOT * SLOTF)

        def slot(n, a=0, b=SLOTF):
            return ring[:, n * SLOTF + a:n * SLOTF + b]

        xl = sb("xl", NLT * D)
        yacc = sb("yacc", NLT * D)
        moe = sb("moe", 6144)
        fr = sb("fr", 3584)
        g2p = sb("g2p", D)
        cst = sb("cst_sb", C_COLS)
        col = sb("col", 620)

        ident = cst[:, C_ID:C_ID + P]
        ones = cst[:, C_ONE:C_ONE + P]
        x3 = xl[:, :].rearrange("p (c n) -> p c n", c=NLT)

        v1t = col[:, 0:R1_ROWS]
        v2t = col[:, 80:80 + R2_ROWS]
        aff1 = col[:, 136:168].rearrange("p (v w k) -> p v w k", v=2, w=2)
        aff2 = col[:, 168:184].rearrange("p (w k) -> p w k", w=2)
        sst = col[:, 184:190]
        std = col[:, 190:196]
        rst = col[:, 196:202]
        epsc = col[:, 202:203]
        fqt = col[0:FH, 203:204]
        slotm = col[:, 204:268].rearrange("p (e c) -> p e c", e=E)
        affr = col[:, 268:332].rearrange("p (e c) -> p e c", e=E)
        ss2 = col[:, 332:336]
        sd2 = col[:, 336:340]
        rs2 = col[:, 340:344]
        mcur = col[:, 344:408]
        mprev = col[:, 408:472]
        mend = col[:, 472:536]
        wcp = col[:, 536:560]
        slp = col[:, 560:568]
        afp = col[:, 568:576]
        sy = col[:, 576:580]
        sdy = col[:, 580:584]
        ry = col[:, 584:588]
        gb = col[:, 588:604]
        nst = col[:, 604:612].rearrange("p (c h) -> p c h", c=NLT)

        ut = slot(2, 0, 2048).rearrange("p (i t) -> p i t", i=NCH)
        brow = slot(2, 2048, 2560)
        prow = slot(2, 2560, 3072)
        g1p = slot(2, 3072, 4096)
        ht = ring[:, 3 * SLOTF:3 * SLOTF + KD * (L + LC)].rearrange("p (k t) -> p k t", k=KD)
        usp = slot(3).rearrange("p (w k n) -> p w k n", w=2, k=NLT)
        hsum = slot(4, 0, 2048).rearrange("p (c n) -> p c n", c=NLT)
        x0t = slot(4, 2048, 4096).rearrange("p (i t) -> p i t", i=NCH)
        dft = slot(5).rearrange("p (w c k) -> p w c k", w=2, c=NLT)
        cstate = slot(5, 0, 2064).rearrange("p (d s n) -> p d s n", d=2, s=NLT)
        ebufs = [slot(5, 2064, 3088).rearrange("p (b n) -> p b n", b=2),
                 moe[:, 2048:3072].rearrange("p (b n) -> p b n", b=2)]
        kwb = slot(4, 0, 2048).rearrange("p (b n) -> p b n", b=NKW)
        xn = slot(6).rearrange("p (c n) -> p c n", c=NLT)
        idft = slot(6).rearrange("p (w k t) -> p w k t", w=2, k=NLT)
        ksp = slot(7).rearrange("p (w k n) -> p w k n", w=2, k=NLT)
        zft = slot(3, 0, 512)
        fw1 = slot(3, 512, 576)
        fw2 = slot(3, 576, 640)
        fw3 = slot(3, 640, 704)
        fw4 = slot(3, 704, 1728)
        fh = slot(3, 1728, 2240)
        fa = slot(3, 2240, 2752)
        ft = slot(3, 2752, 3264)
        dlb = slot(3, 3264, 3776)
        dcy = slot(4, 0, 2048).rearrange("p (c n) -> p c n", c=NLT)
        hyb = slot(4, 2048, 2560)
        vr1 = slot(4, 2560, 2688)
        vr2 = slot(4, 2688, 2816)
        sq = slot(4, 2816, 3840)
        fws = slot(7, 0, 1024).rearrange("p (w n) -> p w n", w=2)
        hpm = yacc[:, :].rearrange("p (w c n) -> p w c n", w=2, c=NLT)
        v1 = yacc[:, 0:NTT * NH * (DV + 1)].rearrange("p (t h n) -> p t h n", t=NTT, h=NH)
        g0 = NTT * NH * (DV + 1)
        atp = yacc[:, g0:g0 + 512].rearrange("p (b n) -> p b n", b=2)
        ew = yacc[:, g0 + 512:g0 + 768].rearrange("p (w n) -> p w n", w=4)
        th = yacc[:, g0 + 768:g0 + 864].rearrange("p (d s n) -> p d s n", d=2, s=NTT)
        lf = yacc[:, g0 + 864:g0 + 912].rearrange("p (d s n) -> p d s n", d=2, s=NTT)
        aco = yacc[:, g0 + 912:g0 + 976]
        cx = moe[:, 0:NCT * D].rearrange("p (c n) -> p c n", c=NCT)
        qt = moe[:, 0:1024].rearrange("p (h t) -> p h t", h=2)
        kt = moe[:, 1024:2048].rearrange("p (h t) -> p h t", h=2)
        kk = moe[:, 2048:3584].rearrange("p (t n) -> p t n", t=NTT)
        og = moe[:, 3584:5632].rearrange("p (c n) -> p c n", c=NLT)
        cpad = moe[:, 5632:5888].rearrange("p (k m) -> p k m", k=KD)
        mrow_t = moe[:, 5888:6016]
        wgate_sb = moe[:, 6016:6144].rearrange("p (k n) -> p k n", k=KD)
        us = fr[:, 0:2048].rearrange("p (c n) -> p c n", c=NLT)
        ymt = fr[:, 0:2048].rearrange("p (h t) -> p h t", h=NH)
        ctmp = fr[:, 2048:3072].rearrange("p (b n) -> p b n", b=2)
        tot = fr[:, 2048:2048 + 516].rearrange("p (b c n) -> p b c n", b=2, c=2)
        dab = fr[:, 2570:2578].rearrange("p (b c) -> p b c", b=4)
        ssq = fr[:, 2580:2596]
        mrow = fr[:, 3072:3584]
        gt = moe[:, 3584:4352]

        xst = moe[:, 0:1024].rearrange("p (k n) -> p k n", k=KD)
        sil = moe[:, 1024:2048].rearrange("p (b n) -> p b n", b=2)
        hid = moe[:, 2048:3072].rearrange("p (b n) -> p b n", b=2)
        hdt = moe[:, 3072:3584].rearrange("p (b n) -> p b n", b=2)
        ye = moe[:, 3584:4608]
        psel = moe[:, 4608:5120].rearrange("p (c n) -> p c n", c=NLT)
        pw = moe[:, 5120:5632].rearrange("p (c n) -> p c n", c=NLT)
        pwt = moe[:, 5632:6144].rearrange("p (c n) -> p c n", c=NLT)
        peq = fr[:, 0:512].rearrange("p (c n) -> p c n", c=NLT)
        y3 = yacc[:, :].rearrange("p (c n) -> p c n", c=NLT)

        B = [ctx.enter_context(nc.psum_tensor(f"B{i}", [P, 512], F32)) for i in range(8)]

        xn2 = slot(2, 0, 2048).rearrange("p (b n) -> p b n", b=2)
        wr = slot(2, 2048, 2176).rearrange("p (k e) -> p k e", k=KD)
        junk = slot(4, 0, 1024)
        h2t = yacc[:, :].rearrange("p (k t) -> p k t", k=KD)
        lgt = fr[:, 0:512]
        lg = fr[:, 512:576].rearrange("p (c e) -> p c e", c=NLT)
        mx4 = fr[:, 576:580]
        sm4 = fr[:, 580:584]
        rc4 = fr[:, 584:588]
        aft = fr[:, 592:656].rearrange("p (c e) -> p c e", c=NLT)
        wka = fr[:, 1024:1536]
        wkb = fr[:, 1536:2048]
        top8 = fr[:, 656:664]
        mkt = fr[:, 672:736].rearrange("p (c e) -> p c e", c=NLT)

        d_vec1, d_vec2, d_cst, d_filt = map(sem, ["d_vec1", "d_vec2", "d_cst", "d_filt"])
        d_taps, d_dft, d_inv = map(sem, ["d_taps", "d_dft", "d_inv"])
        d_x, d_pos, d_ctx, d_row, d_gate, d_wr = map(sem, ["d_x", "d_pos", "d_ctx", "d_row", "d_gate", "d_wr"])
        d_w = [sem(f"d_w{i}") for i in range(2)]
        d_ring = [sem(f"d_ring{i}") for i in range(NSLOT)]
        d_out = sem("d_out")
        names = ["p_vt", "p_fil", "p_kf", "p_ksp", "p_w", "p_modt", "p_g1", "p_htl", "p_htc", "p_gt",
                 "p_gtr", "p_cs", "p_at", "p_cm", "p_mt", "p_hy", "p_utr", "p_qk", "p_kc", "p_ktr", "p_v",
                 "p_st", "p_o", "p_usp", "p_inv", "p_sc", "p_mb", "p_num", "p_ytr", "p_y", "p_h2", "p_lg",
                 "p_lgt", "p_aft", "p_mk", "p_rk", "p_xs", "p_gu", "p_pwt", "p_ht", "p_dn", "p_sca", "v_ch",
                 "v_vt", "v_arg", "v_hpm", "v_kf", "v_mrow", "v_aff", "v_grow", "v_xn", "v_htc", "v_cpad",
                 "v_gsum", "v_sel", "v_x", "v_ew", "v_ssq", "v_cs", "v_at", "v_cum", "v_m", "v_mt",
                 "v_conv", "v_fws", "v_kc", "v_st", "v_cx", "v_inv", "v_d", "v_sw", "v_tot", "v_hs", "v_hn", "v_x1",
                 "v_xn2", "v_h2", "v_lgt", "v_sub", "v_aft", "v_mk", "v_mkt", "v_slot", "v_xs", "v_hid",
                 "v_hdt", "v_yacc", "v_res", "v_cp", "a_ch", "a_th", "a_fil", "a_dec", "a_ksp", "a_ss",
                 "a_std", "a_htl", "a_gt", "a_lf", "a_ew", "a_us", "a_qk", "a_ktr", "a_v", "a_o", "a_usp",
                 "a_e", "a_n2", "a_sq", "a_yt", "a_sy", "a_sdy", "a_ss2", "a_h2", "a_exp", "a_xs", "a_sil",
                 "a_pwt", "a_ye", "a_fsd", "g_ms", "g_zero", "g_kw", "g_sel", "g_cp"]
        S = {n: sem(n) for n in names}

        SLOT_OF = [7, 6, 3, 5, 0, 1, 4, 2]
        NPAIR = E // 2
        TILES = [("g", 0), ("u", 0), ("g", 1), ("u", 1), ("d", 0)]
        for q in range(2, 8):
            TILES += [("g", q), ("u", q), ("d", q - 1)]
        TILES += [("d", 7)]
        NTI = len(TILES)
        LOADS = [("m", 0, 0), ("m", 1, 1), ("m", 2, 0), ("m", 3, 1), ("i", 0, 0), ("m", 4, 1), ("i", 1, 1),
                 ("m", 5, 0), ("i", 2, 0), ("m", 6, 1), ("i", 3, 1), ("m", 7, 0), ("i", 4, 0), ("m", 8, 1),
                 ("i", 5, 1), ("m", 9, 0), ("m", 10, 0), ("m", 11, 1), ("o", 0, 0), ("o", 1, 1)]
        DONE = [("m", 0), ("m", 1), ("m", 2), ("m", 3), ("m", 4), ("i", 0), ("m", 5), ("i", 1), ("m", 6),
                ("i", 2), ("m", 7), ("i", 3), ("m", 8), ("i", 4), ("m", 9), ("i", 5), ("m", 10), ("m", 11),
                ("o", 0), ("o", 1)]

        def done_count(kind, i):
            return DONE.index((kind, i)) + 1

        w_mod, w_in, w_out = A["w_mod"][0], A["w_in"][0], A["w_out"][0]

        N_VEC1, N_VEC2 = 5, 7
        hy_bank, qk_bank, kc_bank, v_bank, o_bank, usp_bank = {}, {}, {}, {}, {}, {}
        ksp_bank, htl_bank, htc_bank = {}, {}, {}
        TAPS = [(1, 0), (0, 0), (0, 1), (0, 2), (0, 3), (1, 1), (1, 2), (1, 3)]
        usq = moe[:, 3072:3584].rearrange("p (c n) -> p c n", n=DV)

        block = ctx.enter_context(nc.Block())

        @block.sync
        def _(sp):
            def rows(dst, r, src, n):
                sp.dma_start(dst[r:r + n, :], src.rearrange("(a b) -> a b", b=P)).then_inc(d_vec2, 16)
            sp.dma_start(cst[:, :], A["cst"]).then_inc(d_cst, 16)
            sp.dma_start(dlb, A["dl"]).then_inc(d_cst, 16)
            sp.wait_ge(S["g_ms"], 1)
            sp.dma_start(vr2[R_CW:R_CW + 36, :],
                         A["conv_w"][0].rearrange("w (a b) -> (w a) b", b=P)).then_inc(d_vec2, 16)
            rows(vr2, R_CB, A["conv_b"][0], 12)
            rows(vr2, R_MLN, A["ml_norm"][0], 4)
            sp.dma_start(fw3[0:FH, :], A["filt_w3"][0]).then_inc(d_taps, 16)
            sp.dma_start(fw4[0:FH, :], A["filt_w4"][0]).then_inc(d_taps, 16)
            sp.dma_start(hyb[0:1, :], A["hyena_bias"]).then_inc(d_taps, 16)
            sp.dma_start(slot(5), A["dft"]).then_inc(d_dft, 16)

            def weight(n):
                kind, i, at = LOADS[n]
                before = [t[0:2] for t in LOADS[:n] if t[2] == at]
                if before:
                    sp.wait_ge(S["p_w"], done_count(*before[-1]))
                dst = slot(at)
                if kind == "m":
                    r, kp = divmod(i, 4)
                    src = w_mod[kp * 2 * P:(kp + 1) * 2 * P, r * 2048:(r + 1) * 2048]
                    dst = dst.rearrange("p (k n) -> p k n", k=2)
                elif kind == "i":
                    src, dst = w_in[:, i * CH:(i + 1) * CH], dst.rearrange("p (k n) -> p k n", k=KD)
                else:
                    src, dst = w_out[:, i * CH:(i + 1) * CH], dst.rearrange("p (k n) -> p k n", k=KD)
                sp.dma_start(dst, src.rearrange("(k p) n -> p k n", p=P)).then_inc(d_w[at], 16)

            for n in range(len(LOADS)):
                if n == 2:
                    sp.dma_start(cx, A["ctx"][0].rearrange("(c p) n -> p c n", p=P)).then_inc(d_ctx, 16)
                    sp.dma_start(x3, A["x"][0].rearrange("(c p) n -> p c n", p=P)).then_inc(d_x, 16)
                    sp.dma_start(xn, A["pos"].rearrange("(c p) n -> p c n", p=P)).then_inc(d_pos, 16)
                if n == 4:
                    sp.dma_start(wgate_sb, w_in[:, 6 * CH:6 * CH + 16].rearrange("(k p) n -> p k n", p=P))\
                        .then_inc(d_gate, 16)
                    sp.dma_start(gb, A["ml_gate_b"][0].partition_broadcast(P)).then_inc(d_gate, 16)
                if n == 6:
                    sp.wait_ge(S["p_htl"], KD)
                    sp.dma_start(slot(6), A["idft"]).then_inc(d_inv, 16)
                weight(n)

            def expert_tile(i, pair):
                kind, st = TILES[i]
                e2, q = divmod(st, 4)
                dst = slot(SLOT_OF[i % NSLOT])
                ex = 2 * pair + e2
                if kind == "d":
                    src = A["w_exp_down"][0, bass.ds(ex, 1), q * CH:(q + 1) * CH, :]
                    src = src.rearrange("o (k p) n -> p (o k) n", p=P)
                    dst = dst.rearrange("p (k n) -> p k n", k=4)
                else:
                    w = A["w_exp_gate" if kind == "g" else "w_exp_up"]
                    src = w[0, bass.ds(ex, 1), :, q * CH:(q + 1) * CH]
                    src = src.rearrange("o (k p) n -> p (o k) n", p=P)
                    dst = dst.rearrange("p (k n) -> p k n", k=KD)
                sp.dma_start(dst, src).then_inc(d_ring[i % NSLOT], 16)

            def used(i, pair):
                kind, st = TILES[i]
                sp.wait_ge(S["p_dn" if kind == "d" else "p_gu"], 8 * pair + st + 1)

            sp.wait_ge(S["v_cx"], NLT)
            expert_tile(0, 0)
            sp.wait_ge(S["p_inv"], NCH)
            expert_tile(1, 0)
            expert_tile(2, 0)
            sp.wait_ge(S["p_num"], 16)
            expert_tile(3, 0)
            sp.wait_ge(S["v_grow"], 2)
            sp.dma_start(wr, A["w_router"][0].rearrange("(k p) e -> p k e", p=P)).then_inc(d_wr, 16)
            sp.wait_ge(S["p_w"], len(DONE))
            expert_tile(4, 0)
            expert_tile(5, 0)
            sp.wait_ge(S["a_ss2"], NLT)
            expert_tile(6, 0)
            sp.wait_ge(S["p_lg"], NLT)
            expert_tile(7, 0)
            with sp.Fori(0, NPAIR - 1) as j:
                for i in range(NTI):
                    used(i, j)
                    expert_tile((i + NSLOT) % NTI, j if i + NSLOT < NTI else j + 1)
            for i in range(NTI - NSLOT):
                used(i, NPAIR - 1)
                expert_tile(i + NSLOT, NPAIR - 1)
            for c in range(NLT):
                sp.wait_ge(S["v_res"], c + 1)
                sp.dma_start(out[0, c * P:(c + 1) * P, :], y3[:, c, :]).then_inc(d_out, 16)
            sp.wait_ge(d_out, 16 * NLT)

        @block.gpsimd
        def _(pool):
            g = nc.gpsimd
            g.memset(vr2, 0.0).then_inc(S["g_ms"], 1)
            g.memset(brow, 0.0).then_inc(S["g_zero"], 1)
            g.memset(prow, 0.0).then_inc(S["g_zero"], 1)
            g.memset(moe[:, 5632:5888], 0.0).then_inc(S["g_zero"], 1)
            g.memset(epsc, EPS).then_inc(S["g_zero"], 1)
            for r, n, src in ((R_C, 8, A["c"][0]), (R_CC, 8, A["c_ctx"]), (R_PRE1, 8, A["pre_norm1"][0]),
                              (R_PRE2, 8, A["pre_norm2"][0]), (R_BMOD, 48, A["b_mod"][0])):
                pool.dma_start(vr1[r:r + n, :], src.rearrange("(a b) -> a b", b=P)).then_inc(d_vec1, 16)
            pool.wait_ge(S["g_zero"], 2)
            for i, (o, norm) in enumerate(((2 * D, "post_norm1"), (5 * D, "post_norm2"))):
                r = 64 * i
                pool.dma_start(brow[r:r + 33:32, :], A["b_mod"][0, o:o + D].rearrange("(a n) -> a n", a=2)).then_inc(d_row, 16)
                pool.dma_start(prow[r:r + 33:32, :], A[norm][0].rearrange("(a n) -> a n", a=2)).then_inc(d_row, 16)
            pool.wait_ge(S["a_ew"], 1)
            pool.wait_ge(S["v_kc"], NCT)
            pool.wait_ge(S["a_ktr"], 2)
            pool.wait_ge(S["p_w"], done_count("i", 5))
            n = 0
            for st in range(NTT - 1):
                for d in range(2):
                    tile = [t for t in range(NTT) if step_of(d, t) == st][0]
                    if n >= NKW:
                        pool.wait_ge(S["p_st"], n - NKW + 1)
                    r = 32 * d + 4 * st
                    src = kk[:, tile, :].rearrange("p (h n) -> p h n", h=NH)
                    wsb = ew[:, 2, r:r + NH].rearrange("p (h o) -> p h o", o=1).to_broadcast([P, NH, DK])
                    g.tensor_tensor(kwb[:, n % NKW, :].rearrange("p (h n) -> p h n", h=NH), src, wsb,
                                    ALU.mult).then_inc(S["g_kw"], 1)
                    n += 1
            pool.wait_ge(S["v_hn"], NLT)
            g.memset(hid[0:CAP, :, :], 0.0).then_inc(S["g_ms"], 1)
            pool.wait_ge(S["p_lg"], NLT)
            g.memset(yacc[:, :], 0.0).then_inc(S["g_ms"], 1)
            pool.wait_ge(S["v_slot"], 2)
            with pool.Fori(0, NPAIR) as j:
                pool.wait_ge(S["v_sel"], 4 * j + 1)
                g.tensor_copy(afp, affr[:, bass.ds(2 * j, 2), :]
                              .rearrange("p e c -> p (e c)")).then_inc(S["g_cp"], 1)
                pool.wait_ge(S["g_cp"], j + 1)
                pool.wait_ge(S["v_sel"], 4 * j + 3)
                for e2 in range(2):
                    af = afp[:, 4 * e2:4 * e2 + 4].rearrange("p (c o) -> p c o", o=1).to_broadcast([P, NLT, CAP])
                    g.tensor_tensor(pw[:, :, CAP * e2:CAP * e2 + CAP], peq[:, :, CAP * e2:CAP * e2 + CAP], af,
                                    ALU.mult).then_inc(S["g_sel"], 1)

        @block.tensor
        def _(pe):
            mm, tr = nc.tensor.matmul, nc.tensor.transpose
            idn = ident
            users = {}

            def take(b):
                if b in users:
                    pe.wait_ge(*users[b])

            def upper(m):
                return ident[0:m, 0:m]

            pe.wait_ge(d_cst, 32)
            pe.wait_ge(d_vec2, 16 * N_VEC2)
            tr(B[1][:, 0:R2_ROWS], vr2[0:R2_ROWS, :], upper(R2_ROWS)).then_inc(S["p_vt"], 1)
            for n, w in enumerate((fw1[0:FEMB, :], fw2[0:FH, :], fw3[0:FH, :])):
                if n == 0:
                    pe.wait_ge(d_filt, 48)
                if n == 2:
                    pe.wait_ge(d_taps, 48)
                for half in range(2):
                    if n:
                        pe.wait_ge(S["a_fil"], 2 * n + half - 1)
                    src = fh[0:FH, half * LC:(half + 1) * LC] if n else zft[0:FEMB, half * LC:(half + 1) * LC]
                    mm(B[2 + half][0:FH, (n % 2) * LC:(n % 2 + 1) * LC], w, src, start=True, stop=True).then_inc(S["p_fil"], 1)
                if n == 0:
                    pe.wait_ge(d_vec1, 16 * N_VEC1)
                    tr(B[0][:, 0:R1_ROWS], vr1[0:R1_ROWS, :], upper(R1_ROWS)).then_inc(S["p_vt"], 1)
            users[0] = users[1] = (S["v_vt"], 2)
            pe.wait_ge(S["v_fws"], 2)
            pe.wait_ge(S["a_fil"], 6)
            for n, (w, c) in enumerate(TAPS):
                b = 4 + n % 4
                if n >= 4:
                    pe.wait_ge(S["v_kf"], n - 3)
                mm(B[b][:, :], fh[0:FH, c * P:(c + 1) * P], fws[0:FH, w, :], start=True, stop=True)\
                    .then_inc(S["p_kf"], 1)
                users[b] = (S["v_kf"], n + 1)
            users[2] = users[3] = (S["a_fil"], 6)
            def weights(kind, i):
                n = [t[0:2] for t in LOADS].index((kind, i))
                at = LOADS[n][2]
                pe.wait_ge(d_w[at], 16 * sum(t[2] == at for t in LOADS[:n + 1]))
                return slot(at)

            def mod_tile(i):
                r, kp = divmod(i, 4)
                w = weights("m", i).rearrange("p (k n) -> p k n", k=2)
                if kp == 0:
                    take(2)
                for k in range(2):
                    for n in range(4):
                        x = mm(B[2][32 * n:32 * n + 32, :], cpad[:, 2 * kp + k, :], w[:, k, n * CH:(n + 1) * CH],
                               start=(kp == 0 and k == 0), stop=(kp == 3 and k == 1))
                x.then_inc(S["p_w"], 1)
                users[2] = (S["v_mrow"], r + 1)

            def mod_turn(r, b):
                pe.wait_ge(S["v_mrow"], r + 1)
                take(b)
                for q in range(4):
                    x = tr(B[b][:, q * P:(q + 1) * P], mrow[:, q * P:(q + 1) * P], idn)
                x.then_inc(S["p_modt"], 1)
                users[b] = (S["v_aff"], r + 1)

            def gate_rows(g, n0, b0):
                pe.wait_ge(S["v_grow"], g + 1)
                for h in range(2):
                    take(b0 + h)
                    row = 32 * (n0 + h)
                    mm(B[b0 + h][:, :], ident[:, row:row + 1].to_broadcast([P, P]), mrow[:, :],
                       start=True, stop=True).then_inc(S["p_g1"], 1)
                    users[b0 + h] = (S["v_cp"], 2 * g + h + 1)

            rot = [0]

            def next_bank():
                b = 3 + rot[0] % 5
                rot[0] += 1
                take(b)
                return b

            pe.wait_ge(S["v_cpad"], 1)
            mod_tile(0)
            mod_tile(1)

            def filter_spectrum(n):
                kc, w = divmod(n, 2)
                b = next_bank()
                if n == 0:
                    pe.wait_ge(d_dft, 16)
                    pe.wait_ge(S["v_hpm"], 1)
                if n == 1:
                    pe.wait_ge(S["v_kf"], len(TAPS))
                for c in range(NLT):
                    if n == 0 and c:
                        pe.wait_ge(S["v_kf"], TAPS.index((w, c)) + 1)
                    r = mm(B[b][:, :], dft[:, w, c, kc * P:(kc + 1) * P], hpm[:, w, c, :],
                           start=(c == 0), stop=(c == NLT - 1))
                r.then_inc(S["p_ksp"], 1)
                ksp_bank[n] = b
                users[b] = (S["a_ksp"], n + 1)

            for n in range(4):
                filter_spectrum(n)
            mod_tile(2)
            filter_spectrum(4)
            filter_spectrum(5)
            mod_tile(3)
            filter_spectrum(6)
            mod_turn(0, 1)
            filter_spectrum(7)
            pe.wait_ge(S["v_xn"], NTT)
            for k in range(KD):
                for lat in (1, 0):
                    b = next_bank()
                    (htl_bank if lat else htc_bank)[k] = b
                    src = xn if lat else cx
                    for c in range(NLT if lat else NCT):
                        x = tr(B[b][:, c * P:(c + 1) * P], src[:, c, k * P:(k + 1) * P], idn)
                    x.then_inc(S["p_htl" if lat else "p_htc"], 1)
                    users[b] = (S["a_htl" if lat else "v_htc"], k + 1)
            pe.wait_ge(S["a_htl"], KD)
            pe.wait_ge(S["v_htc"], KD)
            pe.wait_ge(d_gate, 32)
            take(0)
            for k in range(KD):
                mm(B[0][0:16, :], wgate_sb[:, k, :], ht[:, k, LC:], start=(k == 0), stop=(k == KD - 1))
                x = mm(B[0][32:48, 0:LC], wgate_sb[:, k, :], ht[:, k, 0:LC], start=(k == 0), stop=(k == KD - 1))
            x.then_inc(S["p_gt"], 1)
            users[0] = (S["a_gt"], 2)
            def hyena_tile(i):
                w = weights("i", i).rearrange("p (k n) -> p k n", k=KD)
                for m in range(NCH):
                    b = next_bank()
                    for k in range(KD):
                        x = mm(B[b][:, :], w[:, k, m * P:(m + 1) * P], ht[:, k, LC:], start=(k == 0), stop=(k == KD - 1))
                    x.then_inc(S["p_hy" if m < NCH - 1 else "p_w"], 1)
                    n = i * NCH + m
                    hy_bank[n] = b
                    users[b] = (S["v_conv"], n + 1)
                    if m == 1:
                        mod_tile(4 + i)

            hyena_tile(0)
            pe.wait_ge(S["a_gt"], 2)
            take(1)
            for d in range(2):
                for t in range(NTT):
                    o = (d * NTT + step_of(d, t)) * 16
                    x = tr(B[1][:, o:o + 16], gt[0:16, t * P:(t + 1) * P], upper(16))
            x.then_inc(S["p_gtr"], 1)
            users[1] = (S["v_gsum"], 2)
            hyena_tile(1)
            pe.wait_ge(S["a_lf"], 1)
            take(0)
            mm(B[0][:, 0:24], cst[:, C_UP:C_UP + P], lf[:, 0, :, :], start=True, stop=True)
            mm(B[0][:, 32:56], cst[:, C_LO:C_LO + P], lf[:, 1, :, :], start=True, stop=True)
            mm(B[0][:, 64:88], ones, lf[:, 0, :, :], start=True, stop=True)
            mm(B[0][:, 96:120], ones, lf[:, 1, :, :], start=True, stop=True).then_inc(S["p_cs"], 1)
            users[0] = (S["v_cs"], 1)
            pe.wait_ge(S["v_cs"], 1)
            take(1)
            tr(B[1][0:64, 0:P], aco, idn).then_inc(S["p_at"], 1)
            users[1] = (S["v_at"], 1)
            hyena_tile(2)
            pe.wait_ge(S["v_cum"], 1)
            take(0)
            tr(B[0][:, 0:64], atp[0:64, 1, 64:192], upper(64))
            mm(B[0][:, 64:128], mrow_t[0:64, 0:1].to_broadcast([64, P]), upper(64),
               start=True, stop=True).then_inc(S["p_cm"], 1)
            users[0] = (S["v_m"], 1)
            w = weights("i", 3).rearrange("p (k n) -> p k n", k=KD)
            for m in range(4):
                b = next_bank()
                for k in range(KD):
                    x = mm(B[b][:, :], w[:, k, m * P:(m + 1) * P], ht[:, k, LC:], start=(k == 0), stop=(k == KD - 1))
                x.then_inc(S["p_qk"], 1)
                qk_bank[m] = b
                users[b] = (S["a_qk"], m + 1)
                if m == 0:
                    pe.wait_ge(S["v_m"], 1)
                    take(1)
                    tr(B[1][0:64, 0:P], mcur, idn).then_inc(S["p_mt"], 1)
                    users[1] = (S["v_mt"], 1)
                if m == 1:
                    mod_tile(7)
            for c in range(NCT):
                b = next_bank()
                for k in range(KD):
                    x = mm(B[b][:, 0:QK], ht[:, k, c * P:(c + 1) * P], w[:, k, QK:2 * QK], start=(k == 0), stop=(k == KD - 1))
                x.then_inc(S["p_kc"] if c < NCT - 1 else S["p_w"], 1)
                kc_bank[c] = b
                users[b] = (S["v_kc"], c + 1)
            for i in range(NCH):
                pe.wait_ge(S["v_conv"], 2 * NCH + i + 1)
                take(i % 2)
                for c in range(NLT):
                    x = tr(B[i % 2][:, c * P:(c + 1) * P], ut[:, i, c * P:(c + 1) * P], idn)
                x.then_inc(S["p_utr"], 1)
                users[i % 2] = (S["a_us"], i + 1)
            pe.wait_ge(S["a_qk"], 4)
            for g in range(2):
                take(g)
                for c in range(2):
                    for hp in range(2):
                        x = tr(B[g][:, c * QK + hp * P:c * QK + (hp + 1) * P],
                               kt[:, hp, (2 * g + c) * P:(2 * g + c + 1) * P], idn)
                x.then_inc(S["p_ktr"], 1)
                users[g] = (S["a_ktr"], g + 1)
            w = weights("i", 4).rearrange("p (k n) -> p k n", k=KD)
            for t in range(NTT):
                b = next_bank()
                for k in range(KD):
                    x = mm(B[b][:, :], ht[:, k, t * P:(t + 1) * P], w[:, k, :], start=(k == 0), stop=(k == KD - 1))
                x.then_inc(S["p_v"] if t < NTT - 1 else S["p_w"], 1)
                v_bank[t] = b
                users[b] = (S["a_v"], t + 1)
                if t == 1:
                    mod_turn(1, 1)
                if t == 3:
                    mod_tile(8)
            gate_rows(0, 0, 0)
            w = weights("i", 5).rearrange("p (k n) -> p k n", k=KD)
            for c in range(NLT):
                b = next_bank()
                for k in range(KD):
                    x = mm(B[b][:, :], ht[:, k, LC + c * P:LC + (c + 1) * P], w[:, k, :], start=(k == 0), stop=(k == KD - 1))
                x.then_inc(S["p_o"] if c < NLT - 1 else S["p_w"], 1)
                o_bank[c] = b
                users[b] = (S["a_o"], c + 1)
                if c == 1:
                    mod_tile(9)
            pe.wait_ge(S["a_us"], NCH)
            for kc in range(NLT):
                for wv in range(2):
                    b = next_bank()
                    for c in range(NLT):
                        x = mm(B[b][:, :], dft[:, wv, c, kc * P:(kc + 1) * P], us[:, c, :], start=(c == 0), stop=(c == NLT - 1))
                    x.then_inc(S["p_usp"], 1)
                    usp_bank[2 * kc + wv] = b
                    users[b] = (S["a_usp"], 2 * kc + wv + 1)
            mod_tile(10)
            mod_tile(11)
            n = 0
            for st in range(NTT - 1):
                for d in range(2):
                    tile = [t for t in range(NTT) if step_of(d, t) == st][0]
                    pe.wait_ge(S["g_kw"], n + 1)
                    take(n % 2)
                    for h in range(NH):
                        po = DK * (h % 2)
                        x = mm(B[n % 2][po:po + DK, (h // 2) * (DV + 1):(h // 2 + 1) * (DV + 1)],
                               kwb[:, n % NKW, h * DK:(h + 1) * DK], v1[:, tile, h, :], start=True, stop=True)
                    x.then_inc(S["p_st"], 1)
                    users[n % 2] = (S["v_st"], n + 1)
                    n += 1
            def prepare(h):
                po = DK * (h % 2)
                take(h % 2)
                for c in range(NLT):
                    x = mm(B[h % 2][:, c * P:(c + 1) * P], kt[po:po + DK, h // 2, c * P:(c + 1) * P],
                           qt[po:po + DK, h // 2, c * P:(c + 1) * P], start=True, stop=True)
                x.then_inc(S["p_sc"], 1)
                users[h % 2] = (S["v_sw"], 2 * h + 2)
                for d in range(2):
                    take(2 + d)
                    for c in range(NLT):
                        r = 32 * d + 4 * step_of(d, NCT + c) + h
                        x = mm(B[2 + d][:, c * P:(c + 1) * P], ident[0:64, r:r + 1].to_broadcast([64, P]),
                               mrow_t[0:64, :], start=True, stop=True)
                    x.then_inc(S["p_mb"], 1)
                    users[2 + d] = (S["v_d"], 2 * h + d + 1)

            def numerators(h):
                po = DK * (h % 2)
                for d in range(2):
                    pe.wait_ge(S["v_sw"], 2 * h + d + 1)
                    for cp in range(2):
                        n = 4 * h + 2 * d + cp
                        ba, bb = 4 + 2 * (n % 2), 5 + 2 * (n % 2)
                        take(ba)
                        take(bb)
                        for c in (2 * cp, 2 * cp + 1):
                            o = (c % 2) * (DV + 1)
                            st = step_of(d, NCT + c)
                            mm(B[bb][:, o:o + DV + 1], qt[po:po + DK, h // 2, c * P:(c + 1) * P],
                               cstate[po:po + DK, d, st - NCT, (h // 2) * (DV + 1):(h // 2 + 1) * (DV + 1)],
                               start=True, stop=True)
                            x = mm(B[ba][:, o:o + DV + 1], ebufs[h % 2][:, d, c * P:(c + 1) * P], v1[:, NCT + c, h, :],
                                   start=True, stop=True)
                        x.then_inc(S["p_num"], 1)
                        users[ba] = users[bb] = (S["v_tot"], n + 1)

            def inverse(i):
                b = 4 + i
                take(b)
                for wv in range(2):
                    for k in range(NLT):
                        x = mm(B[b][:, :], usp[:, wv, k, i * P:(i + 1) * P], idft[:, wv, k, :],
                               start=(wv == 0 and k == 0), stop=(wv == 1 and k == NLT - 1))
                x.then_inc(S["p_inv"], 1)
                users[b] = (S["v_inv"], i + 1)

            pe.wait_ge(S["v_mt"], 1)
            pe.wait_ge(S["v_st"], n)
            pe.wait_ge(d_inv, 16)
            pe.wait_ge(S["v_cx"], NLT)
            prepare(0)
            inverse(0)
            prepare(1)
            inverse(1)
            numerators(0)
            prepare(2)
            inverse(2)
            numerators(1)
            prepare(3)
            inverse(3)
            numerators(2)
            numerators(3)

            def project(c, ks, halves=(0, 1)):
                for half in halves:
                    b = 2 * c + half
                    if ks[0] == 0:
                        take(b)
                    for k in ks:
                        lhs = x0t[:, k, c * P:(c + 1) * P] if k < NCH else ymt[:, k - NCH, c * P:(c + 1) * P]
                        x = mm(B[b][:, :], lhs, wo[half][:, k, :], start=(k == 0), stop=(k == KD - 1))
                    if ks[-1] == KD - 1:
                        x.then_inc(S["p_w" if c == NLT - 1 else "p_y"], 1)
                        users[b] = (S["v_x1"], b + 1)

            pe.wait_ge(S["v_inv"], NCH)
            wo = [weights("o", i).rearrange("p (k n) -> p k n", k=KD) for i in range(2)]
            hy_ks, ml_ks = range(NCH), range(NCH, KD)
            for c in range(NLT - 1):
                project(c, hy_ks)
            for i in range(NLT):
                pe.wait_ge(S["v_hn"], i + 1)
                b = 6 + i % 2
                take(b)
                for h in range(NH):
                    x = tr(B[b][:, h * P:(h + 1) * P], hsum[:, i, h * P:(h + 1) * P], idn)
                x.then_inc(S["p_ytr"], 1)
                users[b] = (S["a_yt"], i + 1)
            mod_turn(2, 6)
            pe.wait_ge(S["a_yt"], NLT)
            project(0, ml_ks)
            gate_rows(1, 2, 6)
            project(1, ml_ks)
            project(2, ml_ks)

            def rows_turned(c):
                pe.wait_ge(S["v_xn2"], c + 1)
                for g in range(2):
                    b = 2 * (c % 2) + g
                    take(b)
                    for k in range(4):
                        x = tr(B[b][:, k * P:(k + 1) * P], xn2[:, c % 2, (4 * g + k) * P:(4 * g + k + 1) * P], idn)
                    x.then_inc(S["p_h2"], 1)
                    users[b] = (S["a_h2"] if g else S["v_h2"], c + 1)

            def logits(c):
                pe.wait_ge(S["a_h2"], c + 1)
                pe.wait_ge(S["v_h2"], c + 1)
                if c == 0:
                    take(4)
                for k in range(KD):
                    x = mm(B[4][0:E, c * P:(c + 1) * P], wr[:, k, :], h2t[:, k, c * P:(c + 1) * P],
                           start=(k == 0), stop=(k == KD - 1))
                x.then_inc(S["p_lg"], 1)

            rows_turned(0)
            rows_turned(1)
            project(3, range(KD), (0,))
            rows_turned(2)
            pe.wait_ge(d_wr, 16)
            logits(0)
            logits(1)
            project(3, range(KD), (1,))
            logits(2)
            rows_turned(3)
            logits(3)
            pe.wait_ge(S["v_lgt"], 1)
            take(5)
            for c in range(NLT):
                x = tr(B[5][:, c * E:(c + 1) * E], lgt[0:E, c * P:(c + 1) * P], upper(E))
            x.then_inc(S["p_lgt"], 1)
            pe.wait_ge(S["v_aft"], 1)
            take(6)
            for c in range(NLT):
                x = tr(B[6][0:E, c * P:(c + 1) * P], aft[:, c, :], idn)
            x.then_inc(S["p_aft"], 1)
            pe.wait_ge(S["v_mk"], 1)
            take(7)
            for c in range(NLT):
                x = tr(B[7][:, c * E:(c + 1) * E], wka[0:E, c * P:(c + 1) * P], upper(E))
            x.then_inc(S["p_mk"], 1)
            pe.wait_ge(S["v_mkt"], 1)
            take(0)
            mm(B[0][:, 0:NLT * E], cst[:, C_UP:C_UP + P], mkt, start=True, stop=False)
            for s in range(1, NLT):
                x = mm(B[0][:, s * E:NLT * E], ones, mkt[:, 0:NLT - s, :], start=False, stop=(s == NLT - 1))
            x.then_inc(S["p_rk"], 1)
            pe.wait_ge(S["v_slot"], 2)

            pe.wait_ge(S["g_ms"], 2)
            with pe.Fori(0, NPAIR) as j:
                pe.wait_ge(S["v_sel"], 4 * j + 4)
                for g in range(2):
                    for k in range(4):
                        for c in range(NLT):
                            dk = 4 * g + k
                            x = mm(B[6 + g][:, k * P:(k + 1) * P], x3[:, c, dk * P:(dk + 1) * P], psel[:, c, :],
                                   start=(c == 0), stop=(c == NLT - 1))
                    x.then_inc(S["p_xs"], 1)

                def ring_tile(kind, st):
                    i = TILES.index((kind, st))
                    per = NTI // NSLOT
                    pe.wait_ge(d_ring[i % NSLOT], 16 * (per * j + i // NSLOT + 1))
                    return slot(SLOT_OF[i % NSLOT])

                def gate_up(st):
                    e2 = st // 4
                    wg = ring_tile("g", st).rearrange("p (k n) -> p k n", k=KD)
                    wu = ring_tile("u", st).rearrange("p (k n) -> p k n", k=KD)
                    if st == 0:
                        pe.wait_ge(S["v_xs"], 4 * j + 4)
                    if st >= 2:
                        pe.wait_ge(S["v_hid"], 8 * j + st - 1)
                    for k in range(KD):
                        if st == 0 and k == 4:
                            pe.wait_ge(S["a_xs"], 4 * j + 4)
                        lhs = xst[:, k, CAP * e2:CAP * (e2 + 1)]
                        mm(B[st % 2][0:CAP, :], lhs, wg[:, k, :], start=(k == 0), stop=(k == KD - 1))
                        x = mm(B[st % 2][CAP:P, :], lhs, wu[:, k, :], start=(k == 0), stop=(k == KD - 1))
                    x.then_inc(S["p_gu"], 1)

                def down(st):
                    e2, q = divmod(st, 4)
                    pe.wait_ge(S["v_hid"], 8 * j + st + 1)
                    for k in range(4):
                        x = tr(B[2 + st % 2][:, k * P:(k + 1) * P], hid[:, st % 2, k * P:(k + 1) * P], idn)
                    x.then_inc(S["p_ht"], 1)
                    wd = ring_tile("d", st).rearrange("p (k n) -> p k n", k=4)
                    pe.wait_ge(S["v_hdt"], 8 * j + st + 1)
                    for k in range(4):
                        for half in range(2):
                            x = mm(B[4 + e2][CAP * half:CAP * (half + 1), :], hdt[:, st % 2, k * CAP:(k + 1) * CAP],
                                   wd[:, k, half * CH:(half + 1) * CH],
                                   start=(q == 0 and k == 0), stop=(q == 3 and k == 3))
                    x.then_inc(S["p_dn"], 1)

                gate_up(0)
                gate_up(1)
                pe.wait_ge(S["g_sel"], 2 * j + 2)
                for c in range(NLT):
                    x = tr(B[6][:, c * P:(c + 1) * P], pw[:, c, :], idn)
                x.then_inc(S["p_pwt"], 1)
                down(0)
                for st in range(2, 8):
                    gate_up(st)
                    down(st - 1)
                down(7)
                pe.wait_ge(S["a_pwt"], j + 1)
                pe.wait_ge(S["a_ye"], 4 * j + 4)
                for n in range(2 * NLT):
                    c, half = divmod(n, 2)
                    if n >= 2:
                        pe.wait_ge(S["v_yacc"], 8 * j + n - 1)
                    mm(B[6 + half][:, :], pwt[:, c, :], ye[:, half * CH:(half + 1) * CH],
                       start=True, stop=True).then_inc(S["p_sca"], 1)
                pe.wait_ge(S["v_yacc"], 8 * j + 8)

        @block.scalar
        def _(act):
            a = nc.scalar
            act.dma_start(zft[0:FEMB, :], A["zft"]).then_inc(d_filt, 16)
            act.dma_start(fw1[0:FEMB, :], A["filt_w1"][0]).then_inc(d_filt, 16)
            act.wait_ge(S["g_ms"], 1)
            for n, name in enumerate(("filt_b1", "filt_b2", "filt_b3", "filt_freq")):
                act.dma_start(vr2[R_FB + n:R_FB + n + 1, 0:FH], A[name]).then_inc(d_vec2, 16)
            act.dma_start(fw2[0:FH, :], A["filt_w2"][0]).then_inc(d_filt, 16)
            done = [0]

            def link(ins):
                done[0] += 1
                ins.then_inc(S["a_ch"], 1)
                act.wait_ge(S["a_ch"], done[0])

            act.wait_ge(d_cst, 32)
            for c in range(NLT):
                a.activation(dcy[:, c, :], dlb, ACT.Exp, scale=cst[:, C_TC + c:C_TC + c + 1]).then_inc(S["a_dec"], 1)
            for n in range(6):
                act.wait_ge(S["v_arg"], n + 1)
                h = slice((n % 2) * LC, (n % 2 + 1) * LC)
                if n >= 2:
                    act.wait_ge(S["p_fil"], n + 1)
                a.activation(fh[0:FH, h], fa[0:FH, h], ACT.Sin, scale=TURN).then_inc(S["a_fil"], 1)
            act.wait_ge(S["v_vt"], 2)
            a.activation(mcur[:, 0:16], v1t[:, R_C:R_C + 16], ACT.Tanh, scale=0.5).then_inc(S["a_th"], 1)

            def spectrum_out(n):
                act.wait_ge(S["p_ksp"], n + 1)
                a.activation(ksp[:, n % 2, n // 2, :], B[ksp_bank[n]][:, :], ACT.Copy).then_inc(S["a_ksp"], 1)

            def squares(t):
                if t >= NCT:
                    act.wait_ge(S["v_x"], t - NCT + 1)
                src = cx[:, t, :] if t < NCT else x3[:, t - NCT, :]
                if t:
                    act.wait_ge(S["a_ss"], t)
                a.activation(sq, src, ACT.Square, accum_out=sst[:, t:t + 1]).then_inc(S["a_ss"], 1)

            for n in range(3):
                spectrum_out(n)
            act.wait_ge(d_ctx, 16)
            squares(0)
            squares(1)
            spectrum_out(3)
            for t in range(NCT, NTT):
                squares(t)
            act.wait_ge(S["a_ss"], NTT)
            act.wait_ge(S["g_zero"], 4)
            a.activation(std, sst, ACT.Sqrt, scale=1.0 / D, bias=epsc).then_inc(S["a_std"], 1)
            for n in range(4, 8):
                spectrum_out(n)
            act.wait_ge(S["v_aff"], 1)
            act.wait_ge(S["v_kf"], len(TAPS))
            for k in range(KD):
                act.wait_ge(S["p_htl"], k + 1)
                a.activation(ht[:, k, LC:], B[htl_bank[k]][:, :], ACT.Identity, scale=aff1[:, 0, 0, k:k + 1],
                             bias=aff1[:, 0, 1, k:k + 1]).then_inc(S["a_htl"], 1)
            act.wait_ge(S["p_gt"], 1)
            a.activation(gt[0:16, LC:], B[0][0:16, :], ACT.Copy).then_inc(S["a_gt"], 1)
            a.activation(gt[0:16, 0:LC], B[0][32:48, 0:LC], ACT.Copy).then_inc(S["a_gt"], 1)
            act.wait_ge(S["v_gsum"], 2)
            link(a.activation(th, th, ACT.Tanh, scale=1.0 / GCAP))
            link(a.activation(lf, th[:, :, :, 4:8], ACT.Exp, scale=-GCAP))
            a.activation(lf, lf, ACT.Ln, bias=1.0).then_inc(S["a_lf"], 1)
            act.wait_ge(S["v_ew"], 1)
            a.activation(ew, ew, ACT.Exp).then_inc(S["a_ew"], 1)
            for m in range(4):
                act.wait_ge(S["p_qk"], m + 1)
                dst = (qt if m < 2 else kt)[:, m % 2, :]
                a.activation(dst, B[qk_bank[m]][:, :], ACT.Copy, scale=DK ** -0.5 if m < 2 else 1.0)\
                    .then_inc(S["a_qk"], 1)
            for i in range(NCH):
                act.wait_ge(S["p_utr"], i + 1)
                a.activation(us[:, :, i * P:(i + 1) * P], B[i % 2][:, :].rearrange("p (c n) -> p c n", c=NLT),
                             ACT.Copy).then_inc(S["a_us"], 1)
            for g in range(2):
                act.wait_ge(S["p_ktr"], g + 1)
                a.activation(kk[:, NCT + 2 * g:NCT + 2 * g + 2, :],
                             B[g][:, :].rearrange("p (c n) -> p c n", c=2), ACT.Copy).then_inc(S["a_ktr"], 1)
            for t in range(NTT):
                if t < NTT - 1:
                    act.wait_ge(S["p_v"], t + 1)
                else:
                    act.wait_ge(S["p_w"], done_count("i", 4))
                a.activation(v1[:, t, :, 0:DV], B[v_bank[t]][:, :].rearrange("p (h n) -> p h n", h=NH),
                             ACT.Copy).then_inc(S["a_v"], 1)
            for c in range(NLT):
                if c < NLT - 1:
                    act.wait_ge(S["p_o"], c + 1)
                else:
                    act.wait_ge(S["p_w"], done_count("i", 5))
                a.activation(og[:, c, :], B[o_bank[c]][:, :], ACT.Tanh, scale=0.5).then_inc(S["a_o"], 1)
            for n in range(8):
                act.wait_ge(S["p_usp"], n + 1)
                a.activation(usp[:, n % 2, n // 2, :], B[usp_bank[n]][:, :], ACT.Copy).then_inc(S["a_usp"], 1)
            def decays(h):
                for d in range(2):
                    act.wait_ge(S["v_d"], 2 * h + d + 1)
                    a.activation(ebufs[h % 2][:, d, :], ebufs[h % 2][:, d, :], ACT.Exp, scale=-1.0)\
                        .then_inc(S["a_e"], 1)

            def carried(h):
                for n in range(4 * h, 4 * h + 4):
                    d, cp = divmod(n % 4, 2)
                    act.wait_ge(S["p_num"], n + 1)
                    if n >= 2:
                        act.wait_ge(S["v_hs"], n - 1)
                    for c in (2 * cp, 2 * cp + 1):
                        o = (c % 2) * (DV + 1)
                        r = 32 * d + 4 * step_of(d, NCT + c) + h
                        a.activation(tot[:, n % 2, c % 2, :], B[5 + 2 * (n % 2)][:, o:o + DV + 1], ACT.Copy,
                                     scale=ew[:, 0, r:r + 1]).then_inc(S["a_n2"], 1)

            decays(0)
            decays(1)
            for h in range(NH):
                carried(h)
                if h + 2 < NH:
                    decays(h + 2)
            act.wait_ge(S["v_ssq"], NH)
            a.activation(ssq, ssq, ACT.Sqrt, scale=1.0 / DV, bias=epsc).then_inc(S["a_sq"], 1)
            for c in range(NLT):
                act.wait_ge(S["p_ytr"], c + 1)
                for h in range(NH):
                    x = a.activation(ymt[:, h, c * P:(c + 1) * P], B[6 + c % 2][:, h * P:(h + 1) * P], ACT.Copy,
                                     scale=v2t[:, R_MLN + h:R_MLN + h + 1])
                x.then_inc(S["a_yt"], 1)

            def h2_half(c):
                act.wait_ge(S["p_h2"], 2 * c + 2)
                act.wait_ge(S["v_aff"], 3)
                for k in range(4):
                    x = a.activation(h2t[:, 4 + k, c * P:(c + 1) * P], B[2 * (c % 2) + 1][:, k * P:(k + 1) * P],
                                     ACT.Identity, scale=aff2[:, 0, 4 + k:5 + k], bias=aff2[:, 1, 4 + k:5 + k])
                x.then_inc(S["a_h2"], 1)

            for c in range(NLT):
                for half in range(2):
                    if c < NLT - 1:
                        act.wait_ge(S["p_y"], 2 * c + half + 1)
                    else:
                        act.wait_ge(S["p_w"], len(DONE) - 1 + half)
                    link(a.activation(junk[:, 0:CH], B[2 * c + half][:, :], ACT.Square,
                                      accum_out=(sy if half else sst)[:, c:c + 1]))
                a.activation(sy[:, c:c + 1], sy[:, c:c + 1], ACT.Identity, bias=sst[:, c:c + 1]).then_inc(S["a_sy"], 1)
                act.wait_ge(S["a_sy"], c + 1)
                a.activation(sdy[:, c:c + 1], sy[:, c:c + 1], ACT.Sqrt, scale=1.0 / D, bias=epsc).then_inc(S["a_sdy"], 1)
                act.wait_ge(S["v_x1"], 2 * c + 2)
                link(a.activation(junk, x3[:, c, :], ACT.Square, accum_out=ss2[:, c:c + 1]))
                a.activation(sd2[:, c:c + 1], ss2[:, c:c + 1], ACT.Sqrt, scale=1.0 / D, bias=epsc).then_inc(S["a_ss2"], 1)
                if 1 <= c < 3:
                    h2_half(c - 1)
                if c == 2:
                    h2_half(2)
            h2_half(NLT - 1)
            act.wait_ge(S["v_sub"], 1)
            a.activation(lg, lg, ACT.Exp).then_inc(S["a_exp"], 1)

            with act.Fori(0, NPAIR) as j:
                act.wait_ge(S["p_xs"], 2 * j + 2)
                for k in range(4):
                    a.activation(xst[:, 4 + k, :], B[7][:, k * P:(k + 1) * P], ACT.Identity,
                                 scale=aff2[:, 0, 4 + k:5 + k], bias=aff2[:, 1, 4 + k:5 + k]).then_inc(S["a_xs"], 1)

                def silu(st):
                    act.wait_ge(S["p_gu"], 8 * j + st + 1)
                    if st >= 2:
                        act.wait_ge(S["v_hid"], 8 * j + st - 1)
                    a.activation(sil[CAP:P, st % 2, :], B[st % 2][0:CAP, :], ACT.Silu).then_inc(S["a_sil"], 1)

                def results(e2):
                    act.wait_ge(S["p_dn"], 8 * j + 4 * e2 + 4)
                    for half in range(2):
                        a.activation(ye[CAP * e2:CAP * (e2 + 1), half * CH:(half + 1) * CH],
                                     B[4 + e2][CAP * half:CAP * (half + 1), :], ACT.Copy).then_inc(S["a_ye"], 1)

                silu(0)
                silu(1)
                act.wait_ge(S["p_pwt"], j + 1)
                a.activation(pwt, B[6][:, :].rearrange("p (c n) -> p c n", c=NLT), ACT.Copy).then_inc(S["a_pwt"], 1)
                for st in range(2, 5):
                    silu(st)
                results(0)
                for st in range(5, 8):
                    silu(st)
                results(1)
            for c in range(NLT):
                act.wait_ge(S["v_yacc"], 8 * (NPAIR - 1) + 2 * c + 2)
                link(a.activation(xst[:, :, :].rearrange("p k n -> p (k n)"), y3[:, c, :], ACT.Square,
                                  accum_out=ss2[:, c:c + 1]))
                a.activation(sd2[:, c:c + 1], ss2[:, c:c + 1], ACT.Sqrt, scale=1.0 / D, bias=epsc).then_inc(S["a_fsd"], 1)

        @block.vector
        def _(dve):
            v = nc.vector
            done = [0]

            def link(ins):
                done[0] += 1
                ins.then_inc(S["v_ch"], 1)
                dve.wait_ge(S["v_ch"], done[0])

            def stt(out_, in0, sc, in1, op0, op1):
                return v.scalar_tensor_tensor(out=out_, in0=in0, scalar=sc, in1=in1, op0=op0, op1=op1)

            dve.wait_ge(d_taps, 48)
            v.tensor_tensor(fws[0:FH, 0, :], fw4[0:FH, 0:HY], fw4[0:FH, HY:2 * HY], ALU.add).then_inc(S["v_fws"], 1)
            v.tensor_tensor(fws[0:FH, 1, :], fw4[0:FH, 0:HY], fw4[0:FH, HY:2 * HY], ALU.subtract).then_inc(S["v_fws"], 1)
            dve.wait_ge(S["p_vt"], 1)
            v.tensor_copy(v2t, B[1][:, 0:R2_ROWS]).then_inc(S["v_vt"], 1)
            dve.wait_ge(S["v_vt"], 1)
            link(v.tensor_scalar(fqt, v2t[0:FH, R_FQ:R_FQ + 1], 1.0 / TWO_PI, None, ALU.mult))
            for n in range(6):
                h = slice((n % 2) * LC, (n % 2 + 1) * LC)
                dve.wait_ge(S["p_fil"], n + 1)
                src = B[2 + n % 2][0:FH, (n // 2 % 2) * LC:(n // 2 % 2 + 1) * LC]
                if n >= 2:
                    dve.wait_ge(S["a_fil"], n - 1)
                link(v.tensor_scalar(ft[0:FH, h], src, v2t[0:FH, R_FB + n // 2:R_FB + n // 2 + 1], fqt, ALU.add, ALU.mult))
                link(v.tensor_scalar(fa[0:FH, h], ft[0:FH, h], MAGIC, MAGIC, ALU.add, ALU.subtract))
                v.tensor_tensor(fa[0:FH, h], ft[0:FH, h], fa[0:FH, h], ALU.subtract).then_inc(S["v_arg"], 1)
                if n == 1:
                    dve.wait_ge(S["p_vt"], 2)
                    v.tensor_copy(v1t, B[0][:, 0:R1_ROWS]).then_inc(S["v_vt"], 1)
            dve.wait_ge(S["a_dec"], NLT)
            for n, (w, c) in enumerate(TAPS):
                dve.wait_ge(S["p_kf"], n + 1)
                v.tensor_tensor(hpm[:, w, c, :], B[4 + n % 4][:, :], dcy[:, c, :], ALU.mult).then_inc(S["v_kf"], 1)
                if n == 1:
                    dve.wait_ge(S["v_kf"], 2)
                    z = hpm[0:1, 0, 0, :]
                    link(v.tensor_tensor(z, z, hpm[0:1, 1, 0, :], ALU.add))
                    stt(z, z, 0.5, hyb[0:1, :], ALU.mult, ALU.add).then_inc(S["v_hpm"], 1)
            dve.wait_ge(S["a_th"], 1)
            dve.wait_ge(S["g_zero"], 3)
            link(stt(mcur[:, 16:32], mcur[:, 0:16], 1.0, v1t[:, R_C:R_C + 16], ALU.add, ALU.mult))
            v.tensor_scalar(cpad[:, :, 0:2], mcur[:, 16:32].rearrange("p (w k) -> p k w", w=2), 0.5, None,
                            ALU.mult).then_inc(S["v_cpad"], 1)
            dve.wait_ge(d_x, 16)
            dve.wait_ge(d_pos, 16)
            for c in range(NLT):
                v.tensor_tensor(x3[:, c, :], x3[:, c, :], xn[:, c, :], ALU.add).then_inc(S["v_x"], 1)
            dve.wait_ge(S["a_std"], 1)
            link(v.reciprocal(rst, std))
            dve.wait_ge(S["v_x"], NLT)
            for t in range(NTT):
                src = cx[:, t, :] if t < NCT else x3[:, t - NCT, :]
                dst = cx[:, t, :] if t < NCT else xn[:, t - NCT, :]
                v.tensor_scalar(dst, src, rst[:, t:t + 1], None, ALU.mult).then_inc(S["v_xn"], 1)

            def mod_rows(r):
                if r < 3:
                    dve.wait_ge(S["p_w"], done_count("m", 4 * r + 3))
                    if r:
                        dve.wait_ge(S["p_modt"], r)
                    if r == 2:
                        dve.wait_ge(S["p_g1"], 2)
                    v.tensor_copy(mrow, B[2][:, :]).then_inc(S["v_mrow"], 1)

            def turned(b, i0, w):
                return B[b][:, :].rearrange("p (q i u) -> p i q u", q=4, i=4)[:, i0:i0 + 2, :, w]

            def two(apx):
                return apx.rearrange("p (i q) -> p i q", i=2)

            mod_rows(0)
            dve.wait_ge(S["p_modt"], 1)
            for w in range(2):
                link(v.tensor_tensor(two(aff1[:, w, 0, :]), turned(1, 2, w), two(v1t[:, R_BMOD + 8:R_BMOD + 16]), ALU.add))
                link(stt(aff1[:, w, 0, :], aff1[:, w, 0, :], 1.0, v1t[:, R_PRE1:R_PRE1 + 8], ALU.add, ALU.mult))
                x = v.tensor_tensor(two(aff1[:, w, 1, :]), turned(1, 0, w), two(v1t[:, R_BMOD:R_BMOD + 8]), ALU.add)
                link(x) if w == 0 else x.then_inc(S["v_aff"], 1)
            dve.wait_ge(S["v_aff"], 1)
            for k in range(KD):
                dve.wait_ge(S["p_htc"], k + 1)
                v.tensor_scalar(ht[:, k, 0:LC], B[htc_bank[k]][:, 0:LC], aff1[:, 1, 0, k:k + 1],
                                aff1[:, 1, 1, k:k + 1], ALU.mult, ALU.add).then_inc(S["v_htc"], 1)

            dve.wait_ge(S["p_ksp"], 8)
            link(v.memset(v1[:, :, :, DV:DV + 1], 1.0))
            link(v.memset(ew, 0.0))
            link(v.memset(aco, 0.0))
            link(v.memset(atp, -BIG))
            link(v.memset(mprev, 0.0))
            link(v.memset(mend, 0.0))

            def conv(n):
                i, m = divmod(n, NCH)
                if m < NCH - 1:
                    dve.wait_ge(S["p_hy"], 3 * i + m + 1)
                else:
                    dve.wait_ge(S["p_w"], done_count("i", i))
                src = B[hy_bank[n]]
                dst = (x0t[:, m, :], ut[:, m, :], ctmp[:, m % 2, :])[i]
                w = [v2t[:, R_CW + 12 * s + n:R_CW + 12 * s + n + 1] for s in range(3)]
                link(v.tensor_scalar(dst, src[:, :], w[1], v2t[:, R_CB + n:R_CB + n + 1], ALU.mult, ALU.add))
                link(stt(dst[:, 1:L], src[:, 0:L - 1], w[0], dst[:, 1:L], ALU.mult, ALU.add))
                x = stt(dst[:, 0:L - 1], src[:, 1:L], w[2], dst[:, 0:L - 1], ALU.mult, ALU.add)
                if i < 2:
                    x.then_inc(S["v_conv"], 1)
                else:
                    link(x)
                    v.tensor_tensor(ut[:, m, :], ut[:, m, :], dst, ALU.mult).then_inc(S["v_conv"], 1)

            for n in range(4):
                conv(n)
            dve.wait_ge(S["p_gtr"], 1)
            dve.wait_ge(d_gate, 32)
            for d in range(2):
                o = d * NTT * 16
                src = B[1][:, o:o + NTT * 16].rearrange("p (s n) -> p s n", s=NTT)[:, :, 8 * d:8 * d + 8]
                bias = gb[:, 8 * d:8 * d + 8].unsqueeze(1).broadcast_to([P, NTT, 8])
                v.tensor_tensor(th[:, d, :, :], src, bias, ALU.add).then_inc(S["v_gsum"], 1)
            for n in range(4, 8):
                conv(n)
            dve.wait_ge(S["p_cs"], 1)

            def packed(apx):
                return apx.rearrange("p (d n) -> p d n", d=2)[:, :, 0:24]
            link(v.tensor_copy(packed(ew[:, 1, :]), packed(B[0][:, 0:64])))
            link(v.tensor_copy(packed(ew[:, 3, :]), packed(B[0][:, 64:128])))
            for d in range(2):
                x = stt(aco[:, 32 * d:32 * d + 24], th[:, d, :, 0:4], GCAP, ew[:, 1, 32 * d:32 * d + 24]
                        .rearrange("p (s h) -> p s h", s=NTT), ALU.mult, ALU.add)
                link(x) if d == 0 else x.then_inc(S["v_cs"], 1)
            conv(8)
            dve.wait_ge(S["p_at"], 1)
            v.tensor_copy(atp[0:64, 0, 64:192], B[1][0:64, 0:P]).then_inc(S["v_at"], 1)
            dve.wait_ge(S["v_at"], 1)
            for n in range(7):
                s = 1 << n
                src, dst = atp[:, n % 2, :], atp[:, 1 - n % 2, :]
                link(v.tensor_tensor(dst[0:32, 64:192], src[0:32, 64:192], src[0:32, 64 - s:192 - s], ALU.max))
                link(v.tensor_tensor(dst[32:64, 64:192], src[32:64, 64:192], src[32:64, 64 + s:192 + s], ALU.max))
            link(v.tensor_copy(mrow_t[0:32, 0:1], atp[0:32, 1, 191:192]))
            v.tensor_copy(mrow_t[32:64, 0:1], atp[32:64, 1, 64:65]).then_inc(S["v_cum"], 1)
            for n in range(9, 12):
                conv(n)
            dve.wait_ge(S["p_cm"], 1)
            by_dir = lambda t, s: t.rearrange("p (d n) -> p d n", d=2)[:, :, 4 * s:4 * s + 4]
            for s in range(NTT):
                link(v.tensor_tensor(by_dir(mend, s), by_dir(mprev, s), by_dir(B[0][:, 64:128], s), ALU.max))
                if s + 1 < NTT:
                    link(v.tensor_tensor(by_dir(mprev, s + 1), by_dir(mend, s), by_dir(ew[:, 3, :], s), ALU.subtract))
            v.tensor_tensor(mcur, B[0][:, 0:64], mprev, ALU.max).then_inc(S["v_m"], 1)
            dve.wait_ge(S["v_m"], 1)
            link(v.tensor_tensor(ew[:, 0, :], mprev, mcur, ALU.subtract))
            link(v.tensor_tensor(ew[:, 1, :], ew[:, 1, :], mcur, ALU.subtract))
            link(v.tensor_tensor(ew[:, 2, :], aco, mend, ALU.subtract))
            v.tensor_tensor(ew[:, 3, :], mprev, mend, ALU.subtract).then_inc(S["v_ew"], 1)
            dve.wait_ge(S["p_mt"], 1)
            v.tensor_copy(mrow_t[0:64, :], B[1][0:64, 0:P]).then_inc(S["v_mt"], 1)
            dve.wait_ge(S["a_ew"], 1)
            for p in range(2):
                q = slice(64 * p, 64 * p + 64)
                src = ew[q, 3, :].rearrange("p (d n) -> p d n", d=2)[:, :, p:24:2]
                x = v.tensor_copy(wcp[q, :].rearrange("p (d n) -> p d n", d=2), src)
                link(x)
            for c in range(NCT):
                if c < NCT - 1:
                    dve.wait_ge(S["p_kc"], c + 1)
                else:
                    dve.wait_ge(S["p_w"], done_count("i", 3))
                v.tensor_copy(kk[:, c, :], B[kc_bank[c]][:, 0:QK]).then_inc(S["v_kc"], 1)

            def gate_row(g):
                dve.wait_ge(S["p_modt"], g + 2)
                dve.wait_ge(d_row, 64)
                dve.wait_ge(S["v_mrow"], g + 2)
                link(v.tensor_tensor(mrow, mrow, brow, ALU.add))
                v.tensor_tensor(mrow, mrow, prow, ALU.mult).then_inc(S["v_grow"], 1)
                for h in range(2):
                    dve.wait_ge(S["p_g1"], 2 * g + h + 1)
                    v.tensor_copy((g1p, g2p)[g][:, h * CH:(h + 1) * CH], B[6 * g + h][:, :]).then_inc(S["v_cp"], 1)

            mod_rows(1)
            dve.wait_ge(S["p_modt"], 2)
            v.tensor_tensor(two(aff2[:, 1, :]), turned(1, 2, 0), two(v1t[:, R_BMOD + 24:R_BMOD + 32]),
                            ALU.add).then_inc(S["v_aff"], 1)
            gate_row(0)
            for k in range(NLT):
                dve.wait_ge(S["a_usp"], 2 * k + 2)
                ur, ui, kr, ki = usp[:, 0, k, :], usp[:, 1, k, :], ksp[:, 0, k, :], ksp[:, 1, k, :]
                link(v.tensor_tensor(ctmp[:, 0, :], ur, kr, ALU.mult))
                link(v.tensor_tensor(ctmp[:, 1, :], ui, ki, ALU.mult))
                link(v.tensor_tensor(kr, ui, kr, ALU.mult))
                link(v.tensor_tensor(ki, ur, ki, ALU.mult))
                link(v.tensor_tensor(ur, ctmp[:, 0, :], ctmp[:, 1, :], ALU.subtract))
                v.tensor_tensor(ui, kr, ki, ALU.add).then_inc(S["v_cx"], 1)
            mod_rows(2)
            n = 0
            for st in range(NTT - 1):
                for d in range(2):
                    dve.wait_ge(S["p_st"], n + 1)
                    if n >= 2:
                        dve.wait_ge(S["v_st"], n - 1)
                    for p in range(2):
                        o = slice(p * (DV + 1), (p + 1) * (DV + 1))
                        src = B[n % 2][:, o]
                        if st == 0:
                            x = v.tensor_copy(cstate[:, d, 0, o], src)
                        else:
                            q = d * 12 + 2 * st + p
                            x = stt(cstate[:, d, st - 1, o], cstate[:, d, max(st - 2, 0), o], wcp[:, q:q + 1], src,
                                    ALU.mult, ALU.add)
                        link(x) if p == 0 else x.then_inc(S["v_st"], 1)
                    n += 1
            def h2_half(c):
                dve.wait_ge(S["p_h2"], 2 * c + 1)
                for k in range(4):
                    x = v.tensor_scalar(h2t[:, k, c * P:(c + 1) * P], B[2 * (c % 2)][:, k * P:(k + 1) * P],
                                        aff2[:, 0, k:k + 1], aff2[:, 1, k:k + 1], ALU.mult, ALU.add)
                x.then_inc(S["v_h2"], 1)

            def weights_of(h):
                for d in range(2):
                    dve.wait_ge(S["p_mb"], 2 * h + d + 1)
                    if h >= 2:
                        dve.wait_ge(S["p_num"], 4 * (h - 2) + 2 * d + 2)
                    for c in range(NLT):
                        r = 32 * d + 4 * step_of(d, NCT + c) + h
                        x = stt(ebufs[h % 2][:, d, c * P:(c + 1) * P], B[2 + d][:, c * P:(c + 1) * P], aco[:, r:r + 1],
                                cst[:, (C_BF, C_BB)[d]:(C_BF, C_BB)[d] + P], ALU.subtract, ALU.max)
                    x.then_inc(S["v_d"], 1)

            def times_scores(h):
                dve.wait_ge(S["p_sc"], h + 1)
                for d in range(2):
                    dve.wait_ge(S["a_e"], 2 * h + d + 1)
                    v.tensor_tensor(ebufs[h % 2][:, d, :], ebufs[h % 2][:, d, :], B[h % 2][:, :], ALU.mult).then_inc(S["v_sw"], 1)

            def hyena_out(i):
                dve.wait_ge(S["p_inv"], i + 1)
                v.tensor_tensor(x0t[:, i, :], x0t[:, i, :], B[4 + i][:, :], ALU.mult).then_inc(S["v_inv"], 1)

            hs4 = hsum.rearrange("p c (h n) -> p h c n", h=NH)
            sq4 = ssq.rearrange("p (c h) -> p h c", h=NH)

            def head(h):
                for n in range(4 * h, 4 * h + 4):
                    d, cp = divmod(n % 4, 2)
                    dve.wait_ge(S["a_n2"], 2 * n + 2)
                    t = tot[:, n % 2, :, :]
                    v.tensor_tensor(t, t, B[4 + 2 * (n % 2)][:, 0:2 * (DV + 1)].rearrange("p (c n) -> p c n", c=2),
                                    ALU.add).then_inc(S["v_tot"], 1)
                    dve.wait_ge(S["v_tot"], n + 1)
                    r = [32 * d + 4 * step_of(d, NCT + 2 * cp + c) + h for c in range(2)]
                    em = ew[:, 1, r[0]:r[0] + 5:4] if r[1] > r[0] else ew[:, 1, r[1]:r[1] + 5:4][:, ::-1]
                    dd = dab[:, n % 4, :].unsqueeze(2)
                    link(v.tensor_tensor(dd, t[:, :, DV:DV + 1], em.unsqueeze(2), ALU.max))
                    link(stt(dd, t[:, :, DV:DV + 1], -1.0, dd, ALU.mult, ALU.max))
                    link(v.reciprocal(dab[:, n % 4, :], dab[:, n % 4, :]))
                    rb = dab[:, n % 4, :].unsqueeze(2).broadcast_to([P, 2, DV])
                    dst = hsum[:, 2 * cp:2 * cp + 2, h * DV:(h + 1) * DV]
                    if d == 0:
                        v.tensor_tensor(dst, t[:, :, 0:DV], rb, ALU.mult).then_inc(S["v_hs"], 1)
                    else:
                        link(v.tensor_tensor(t[:, :, 0:DV], t[:, :, 0:DV], rb, ALU.mult))
                        v.tensor_tensor(dst, dst, t[:, :, 0:DV], ALU.add).then_inc(S["v_hs"], 1)
                dve.wait_ge(S["v_hs"], 4 * h + 4)
                if h:
                    dve.wait_ge(S["v_ssq"], h)
                link(v.tensor_tensor(usq, hs4[:, h, :, :], hs4[:, h, :, :], ALU.mult))
                v.tensor_reduce(sq4[:, h, :], usq, AX.X, ALU.add).then_inc(S["v_ssq"], 1)

            for h in range(2):
                weights_of(h)
                times_scores(h)
                hyena_out(h)
            for h in range(NH):
                head(h)
                if h + 2 < NH:
                    weights_of(h + 2)
                    times_scores(h + 2)
                    hyena_out(h + 2)
            link(v.tensor_scalar(v2t[:, R_MLN:R_MLN + NH], v2t[:, R_MLN:R_MLN + NH], 0.5, None, ALU.mult))
            dve.wait_ge(S["a_sq"], 1)
            link(v.reciprocal(ssq, ssq))
            for c in range(NLT):
                hc = hsum[:, c, :].rearrange("p (h n) -> p h n", h=NH)
                link(v.tensor_tensor(hc, hc, ssq[:, 4 * c:4 * c + 4].unsqueeze(2).broadcast_to([P, NH, DV]), ALU.mult))
                stt(hsum[:, c, :], og[:, c, :], 1.0, hsum[:, c, :], ALU.add, ALU.mult).then_inc(S["v_hn"], 1)
            dve.wait_ge(S["p_modt"], 3)
            link(v.tensor_tensor(two(aff2[:, 0, :]), turned(6, 0, 0), two(v1t[:, R_BMOD + 32:R_BMOD + 40]), ALU.add))
            stt(aff2[:, 0, :], aff2[:, 0, :], 1.0, v1t[:, R_PRE2:R_PRE2 + 8], ALU.add, ALU.mult).then_inc(S["v_aff"], 1)
            gate_row(1)

            for c in range(NLT):
                dve.wait_ge(S["a_sdy"], c + 1)
                link(v.reciprocal(ry[:, c:c + 1], sdy[:, c:c + 1]))
                for half in range(2):
                    h = slice(half * CH, (half + 1) * CH)
                    t = ctmp[:, half, :]
                    link(stt(t, B[2 * c + half][:, :], ry[:, c:c + 1], g1p[:, h], ALU.mult, ALU.mult))
                    v.tensor_tensor(x3[:, c, h], x3[:, c, h], t, ALU.add).then_inc(S["v_x1"], 1)
                dve.wait_ge(S["a_ss2"], c + 1)
                link(v.reciprocal(rs2[:, c:c + 1], sd2[:, c:c + 1]))
                if c >= 2:
                    dve.wait_ge(S["p_h2"], 2 * (c - 1))
                dve.wait_ge(S["v_x1"], 2 * c + 2)
                v.tensor_scalar(xn2[:, c % 2, :], x3[:, c, :], rs2[:, c:c + 1], None, ALU.mult).then_inc(S["v_xn2"], 1)
                if 1 <= c < 3:
                    h2_half(c - 1)
                if c == 2:
                    h2_half(2)
            h2_half(NLT - 1)
            dve.wait_ge(S["p_lg"], NLT)
            v.tensor_copy(lgt[0:E, :], B[4][0:E, :]).then_inc(S["v_lgt"], 1)
            dve.wait_ge(S["p_lgt"], 1)
            l5 = B[5][:, 0:NLT * E].rearrange("p (c e) -> p c e", c=NLT)
            link(v.tensor_reduce(mx4, l5, AX.X, ALU.max))
            v.tensor_tensor(lg, l5, mx4.unsqueeze(2).broadcast_to([P, NLT, E]), ALU.subtract).then_inc(S["v_sub"], 1)
            dve.wait_ge(S["a_exp"], 1)
            link(v.tensor_reduce(sm4, lg, AX.X, ALU.add))
            link(v.reciprocal(rc4, sm4))
            v.tensor_tensor(aft, lg, rc4.unsqueeze(2).broadcast_to([P, NLT, E]), ALU.mult).then_inc(S["v_aft"], 1)
            dve.wait_ge(S["v_aft"], 1)
            v.tensor_copy(affr, aft.rearrange("p c e -> p e c")).then_inc(S["v_slot"], 1)
            dve.wait_ge(S["p_aft"], 1)
            link(v.tensor_copy(lgt[0:E, :], B[6][0:E, :]))
            cur = lgt
            for r in range(CAP // 8):
                nxt = wka if r % 2 == 0 else wkb
                link(v.max(out=top8[0:E, :], in_=cur[0:E, :]))
                link(v.match_replace(out=nxt[0:E, :], in_to_replace=top8[0:E, :], in_values=cur[0:E, :], imm_value=-1.0))
                cur = nxt
            v.tensor_tensor(wka[0:E, :], cur[0:E, :], lgt[0:E, :], ALU.not_equal).then_inc(S["v_mk"], 1)
            dve.wait_ge(S["p_mk"], 1)
            v.tensor_copy(mkt, B[7][:, 0:NLT * E].rearrange("p (c e) -> p c e", c=NLT)).then_inc(S["v_mkt"], 1)
            dve.wait_ge(S["p_rk"], 1)
            sl = slotm.rearrange("p e c -> p c e")
            link(v.tensor_tensor(sl, B[0][:, 0:NLT * E].rearrange("p (c e) -> p c e", c=NLT), mkt, ALU.mult))
            v.tensor_scalar(slotm, slotm, -1.0, None, ALU.add).then_inc(S["v_slot"], 1)

            dve.wait_ge(S["v_slot"], 2)
            dve.wait_ge(S["g_ms"], 3)

            with dve.Fori(0, NPAIR) as j:
                v.tensor_copy(slp, slotm[:, bass.ds(2 * j, 2), :].rearrange("p e c -> p (e c)")).then_inc(S["v_sel"], 1)
                dve.wait_ge(S["v_sel"], 4 * j + 1)
                for e2 in range(2):
                    io = cst[:, C_IO:C_IO + CAP].unsqueeze(1).broadcast_to([P, NLT, CAP])
                    sl = slp[:, 4 * e2:4 * e2 + 4].unsqueeze(2).broadcast_to([P, NLT, CAP])
                    v.tensor_tensor(peq[:, :, CAP * e2:CAP * e2 + CAP], io, sl, ALU.is_equal).then_inc(S["v_sel"], 1)
                dve.wait_ge(S["v_sel"], 4 * j + 3)
                v.tensor_tensor(psel, peq, rs2.unsqueeze(2).broadcast_to([P, NLT, P]), ALU.mult)\
                    .then_inc(S["v_sel"], 1)
                dve.wait_ge(S["p_xs"], 2 * j + 1)
                for k in range(4):
                    v.tensor_scalar(xst[:, k, :], B[6][:, k * P:(k + 1) * P], aff2[:, 0, k:k + 1], aff2[:, 1, k:k + 1],
                                    ALU.mult, ALU.add).then_inc(S["v_xs"], 1)

                def hidden(st):
                    dve.wait_ge(S["a_sil"], 8 * j + st + 1)
                    if st >= 2:
                        dve.wait_ge(S["p_ht"], 8 * j + st - 1)
                    v.tensor_tensor(hid[CAP:P, st % 2, :], sil[CAP:P, st % 2, :], B[st % 2][CAP:P, :],
                                    ALU.mult).then_inc(S["v_hid"], 1)

                def turned_hidden(st):
                    dve.wait_ge(S["p_ht"], 8 * j + st + 1)
                    if st >= 2:
                        dve.wait_ge(S["p_dn"], 8 * j + st - 1)
                    v.tensor_copy(hdt[:, st % 2, :].rearrange("p (k n) -> p k n", k=4),
                                  B[2 + st % 2][:, :].rearrange("p (k n) -> p k n", k=4)[:, :, CAP:P])\
                        .then_inc(S["v_hdt"], 1)

                hidden(0)
                hidden(1)
                turned_hidden(0)
                for st in range(2, 8):
                    hidden(st)
                    turned_hidden(st - 1)
                turned_hidden(7)
                for n in range(2 * NLT):
                    c, half = divmod(n, 2)
                    dve.wait_ge(S["p_sca"], 8 * j + n + 1)
                    dst = y3[:, c, half * CH:(half + 1) * CH]
                    v.tensor_tensor(dst, dst, B[6 + half][:, :], ALU.add).then_inc(S["v_yacc"], 1)
            for c in range(NLT):
                dve.wait_ge(S["a_fsd"], c + 1)
                link(v.reciprocal(ry[:, c:c + 1], sd2[:, c:c + 1]))
                dve.wait_ge(S["v_yacc"], 8 * NPAIR)
                link(stt(y3[:, c, :], y3[:, c, :], ry[:, c:c + 1], g2p[:, :], ALU.mult, ALU.mult))
                v.tensor_tensor(y3[:, c, :], y3[:, c, :], x3[:, c, :], ALU.add).then_inc(S["v_res"], 1)


NAMES = ["x", "c", "ctx", "c_ctx", "w_mod", "b_mod", "pre_norm1", "post_norm1", "pre_norm2", "post_norm2",
         "w_in", "conv_w", "conv_b", "filt_w1", "filt_b1", "filt_w2", "filt_b2", "filt_w3", "filt_b3", "filt_w4",
         "filt_freq", "hyena_bias", "ml_gate_b", "ml_norm", "w_out", "w_router", "w_exp_gate", "w_exp_up",
         "w_exp_down"]


def kernel(**inputs):
    import concourse.bacc as bacc
    from concourse.bass_utils import run_bass_kernel_spmd

    nc = bacc.Bacc("TRN2", target_bir_lowering=False, num_devices=1)
    arrays = {n: np.ascontiguousarray(inputs[n]) for n in NAMES}
    arrays.update(shape_constants())
    A = {n: nc.dram_tensor(f"in_{n}", a.shape, mybir.dt.from_np(a.dtype), kind="ExternalInput").ap()
         for n, a in arrays.items()}
    out = nc.dram_tensor("out", (1, L, D), F32, kind="ExternalOutput").ap()
    block_kernel(nc, A, out)
    r = run_bass_kernel_spmd(nc, [{f"in_{n}": a for n, a in arrays.items()}], core_ids=[0])
    return r.results[0]["out"]
```

```python
import math
from contextlib import ExitStack

import numpy as np

import concourse.bass as bass
from concourse import mybir

F32 = mybir.dt.float32
ALU = mybir.AluOpType
ACT = mybir.ActivationFunctionType
AX = mybir.AxisListType

D, L, LC = 1024, 512, 256
P = 128
KD = D // P
NLT, NCT = L // P, LC // P
NTT = NLT + NCT
HY, DK, DV, NH = 512, 64, 128, 4
QK = NH * DK
GRID_W = 64
E, FF, CAP = 16, 2048, 64
BANDS, FEMB, FH = 16, 33, 64
EPS = 1e-6
GCAP = 15.0
NCH = HY // P
BIG = 1e30
NSLOT, SLOTF = 8, 4096
CH = 512
NKC = L // 2 // P
TWO_PI = 2.0 * math.pi
MAGIC = 12582912.0
TURN = 2 * 3.1415925

R_C, R_CC, R_PRE1, R_PRE2, R_BMOD = 0, 8, 16, 24, 32
R1_ROWS = 80
R_CW, R_CB, R_MLN, R_FB, R_FQ = 0, 36, 48, 52, 55
R2_ROWS = 56

C_ID, C_UP, C_LO, C_ONE, C_BF, C_BB, C_IO, C_TC = 0, 128, 256, 384, 512, 640, 768, 832
C_COLS = 836


def shape_constants():
    i = np.arange(P)
    cst = np.zeros((P, C_COLS), np.float32)
    cst[:, C_ID:C_ID + P] = np.eye(P)
    cst[:, C_UP:C_UP + P] = i[:, None] <= i[None, :]
    cst[:, C_LO:C_LO + P] = i[:, None] >= i[None, :]
    cst[:, C_ONE:C_ONE + P] = 1.0
    cst[:, C_BF:C_BF + P] = np.where(i[:, None] <= i[None, :], 0.0, BIG)
    cst[:, C_BB:C_BB + P] = np.where(i[:, None] >= i[None, :], 0.0, BIG)
    cst[:, C_IO:C_IO + CAP] = np.arange(CAP)[None, :]
    tpos = np.linspace(0.0, 1.0, L, dtype=np.float32)
    even_odd = np.concatenate([np.arange(0, L, 2), np.arange(1, L, 2)])
    cst[:, C_TC:C_TC + NLT] = -tpos[even_odd].reshape(NLT, P).T
    quarter = D // 4
    omega = 1.0 / (10000.0 ** (np.arange(quarter, dtype=np.float64) / quarter))

    def emb(n):
        ang = np.arange(n, dtype=np.float64)[:, None] * omega[None, :]
        return np.concatenate([np.sin(ang), np.cos(ang)], axis=-1)
    rows = L // GRID_W
    er, ec = emb(rows), emb(GRID_W)
    pe = np.concatenate([np.broadcast_to(er[:, None, :], (rows, GRID_W, D // 2)),
                         np.broadcast_to(ec[None, :, :], (rows, GRID_W, D // 2))], axis=-1)
    pe = np.ascontiguousarray(pe.reshape(L, D).astype(np.float32))
    w = 2.0 * np.pi * np.arange(L) / L
    f = np.linspace(1e-4, BANDS - 1, BANDS)
    ang = w[:, None] * f[None, :]
    zf = np.concatenate([tpos[:, None].astype(np.float64), np.cos(ang), -np.sin(ang)], axis=-1)
    zft = np.ascontiguousarray(zf[even_odd].T.astype(np.float32))
    lo, hi = math.log(1e-2) / 1.5, math.log(1e-2) / 0.3
    deltas = np.abs(np.linspace(lo, hi, HY, dtype=np.float32))
    dl = np.ascontiguousarray(np.broadcast_to(deltas[None, :], (P, HY)).astype(np.float32))
    a = (np.pi / L) * (even_odd[:, None].astype(np.float64) * (np.arange(L // 2)[None, :] + 0.5))
    fwd = np.stack([np.cos(a), np.sin(a)])
    inv = np.stack([np.cos(a).T, np.sin(a).T]) / L

    def tiles(m):
        w, rows, cols = m.shape
        return np.ascontiguousarray(
            m.reshape(w, rows // P, P, cols).transpose(2, 0, 1, 3).reshape(P, w * rows // P * cols).astype(np.float32))
    return {"cst": cst, "pos": pe, "zft": zft, "dl": dl, "dft": tiles(fwd), "idft": tiles(inv)}


def step_of(d, tile):
    if d == 0:
        return tile
    return NCT - 1 - tile if tile < NCT else NTT - 1 - (tile - NCT)


def block_kernel(nc, A, out):
    ctx = ExitStack()
    with ctx:
        def sb(name, cols, rows=P):
            return ctx.enter_context(nc.sbuf_tensor(name, [rows, cols], F32))

        def sem(name):
            return ctx.enter_context(nc.semaphore(name))

        ring = sb("ring", NSLOT * SLOTF)

        def slot(n, a=0, b=SLOTF):
            return ring[:, n * SLOTF + a:n * SLOTF + b]

        xl = sb("xl", NLT * D)
        yacc = sb("yacc", NLT * D)
        moe = sb("moe", 6144)
        fr = sb("fr", 3584)
        g2p = sb("g2p", D)
        cst = sb("cst_sb", C_COLS)
        col = sb("col", 620)

        ident = cst[:, C_ID:C_ID + P]
        ones = cst[:, C_ONE:C_ONE + P]
        x3 = xl[:, :].rearrange("p (c n) -> p c n", c=NLT)

        v1t = col[:, 0:R1_ROWS]
        v2t = col[:, 80:80 + R2_ROWS]
        aff1 = col[:, 136:168].rearrange("p (v w k) -> p v w k", v=2, w=2)
        aff2 = col[:, 168:184].rearrange("p (w k) -> p w k", w=2)
        sst = col[:, 184:190]
        std = col[:, 190:196]
        rst = col[:, 196:202]
        epsc = col[:, 202:203]
        fqt = col[0:FH, 203:204]
        slotm = col[:, 204:268].rearrange("p (e c) -> p e c", e=E)
        affr = col[:, 268:332].rearrange("p (e c) -> p e c", e=E)
        ss2 = col[:, 332:336]
        sd2 = col[:, 336:340]
        rs2 = col[:, 340:344]
        mcur = col[:, 344:408]
        mprev = col[:, 408:472]
        mend = col[:, 472:536]
        wcp = col[:, 536:560]
        slp = col[:, 560:568]
        afp = col[:, 568:576]
        sy = col[:, 576:580]
        sdy = col[:, 580:584]
        ry = col[:, 584:588]
        gb = col[:, 588:604]

        ut = slot(2, 0, 2048).rearrange("p (i t) -> p i t", i=NCH)
        brow = slot(2, 2048, 2560)
        prow = slot(2, 2560, 3072)
        g1p = slot(2, 3072, 4096)
        ht = ring[:, 3 * SLOTF:3 * SLOTF + KD * (L + LC)].rearrange("p (k t) -> p k t", k=KD)
        usp = slot(2, 0, 2048).rearrange("p (w j n) -> p w j n", w=2, j=2)
        hsum = slot(4, 0, 2048).rearrange("p (c n) -> p c n", c=NLT)
        x0t = slot(4, 2048, 4096).rearrange("p (i t) -> p i t", i=NCH)
        cprod = [fr[:, 2048:3072], moe[:, 2048:3072]]
        dft = slot(5, 0, 2048).rearrange("p (w c k) -> p w c k", w=2, c=NLT)
        cs0 = 5 * SLOTF + 3840
        cstate = ring[:, cs0:cs0 + 2064].rearrange("p (d s n) -> p d s n", d=2, s=NLT)
        ebufs = [slot(5, 2048, 3072).rearrange("p (b n) -> p b n", b=2),
                 moe[:, 2048:3072].rearrange("p (b n) -> p b n", b=2)]
        xn = slot(6).rearrange("p (c n) -> p c n", c=NLT)
        idft = slot(6, 1808, 3856).rearrange("p (w k t) -> p w k t", w=2, k=NKC)
        ksp = slot(7).rearrange("p (w k j n) -> p w k j n", w=2, k=NKC, j=2)
        zft = slot(3, 0, 512)
        fw1 = slot(3, 512, 576)
        fw2 = slot(3, 576, 640)
        fw3 = slot(3, 640, 704)
        fw4 = slot(3, 704, 1728)
        fh = slot(3, 1728, 2240)
        fa = slot(3, 2240, 2752)
        ft = slot(3, 2752, 3264)
        dlb = slot(3, 3264, 3776)
        dcy = slot(4, 0, 2048).rearrange("p (c n) -> p c n", c=NLT)
        hyb = slot(4, 2048, 2560)
        vr1 = slot(4, 2560, 2688)
        vr2 = slot(4, 2688, 2816)
        sq = slot(4, 2816, 3840)
        fws = slot(7, 0, 1024).rearrange("p (w n) -> p w n", w=2)
        hpm = yacc[:, :].rearrange("p (w c n) -> p w c n", w=2, c=NLT)
        v1 = yacc[:, 0:NTT * NH * (DV + 1)].rearrange("p (t h n) -> p t h n", t=NTT, h=NH)
        g0 = NTT * NH * (DV + 1)
        atp = yacc[:, g0:g0 + 512].rearrange("p (b n) -> p b n", b=2)
        ew = yacc[:, g0 + 512:g0 + 768].rearrange("p (w n) -> p w n", w=4)
        th = yacc[:, g0 + 768:g0 + 864].rearrange("p (d s n) -> p d s n", d=2, s=NTT)
        lf = yacc[:, g0 + 864:g0 + 912].rearrange("p (d s n) -> p d s n", d=2, s=NTT)
        aco = yacc[:, g0 + 912:g0 + 976]
        cx = moe[:, 0:NCT * D].rearrange("p (c n) -> p c n", c=NCT)
        qt = moe[:, 0:1024].rearrange("p (h t) -> p h t", h=2)
        kt = moe[:, 1024:2048].rearrange("p (h t) -> p h t", h=2)
        kk = moe[:, 2048:3584].rearrange("p (t n) -> p t n", t=NTT)
        og = moe[:, 3584:5632].rearrange("p (c n) -> p c n", c=NLT)
        kwb = [moe[:, 3584 + n * QK:3584 + (n + 1) * QK] for n in range(8)] + \
            [slot(5, 3072 + n * QK, 3072 + (n + 1) * QK) for n in range(2)]
        cpad = moe[:, 5632:5888].rearrange("p (k m) -> p k m", k=KD)
        mrow_t = moe[:, 5888:6016]
        wgate_sb = moe[:, 6016:6144].rearrange("p (k n) -> p k n", k=KD)
        us = fr[:, 0:2048].rearrange("p (c n) -> p c n", c=NLT)
        ymt = fr[:, 0:2048].rearrange("p (h t) -> p h t", h=NH)
        ctmp = fr[:, 2048:3072].rearrange("p (b n) -> p b n", b=2)
        tot = fr[:, 2048:2048 + 516].rearrange("p (b c n) -> p b c n", b=2, c=2)
        dab = fr[:, 2570:2578].rearrange("p (b c) -> p b c", b=4)
        ssq = fr[:, 2580:2596]
        mrow = fr[:, 3072:3584]
        gt = moe[:, 3584:4352]

        xst = moe[:, 0:1024].rearrange("p (k n) -> p k n", k=KD)
        sil = moe[:, 1024:2048].rearrange("p (b n) -> p b n", b=2)
        hid = moe[:, 2048:3072].rearrange("p (b n) -> p b n", b=2)
        hdt = moe[:, 3072:3584].rearrange("p (b n) -> p b n", b=2)
        ye = moe[:, 3584:4608]
        psel = moe[:, 4608:5120].rearrange("p (c n) -> p c n", c=NLT)
        pw = moe[:, 5120:5632].rearrange("p (c n) -> p c n", c=NLT)
        pwt = moe[:, 5632:6144].rearrange("p (c n) -> p c n", c=NLT)
        peq = fr[:, 0:512].rearrange("p (c n) -> p c n", c=NLT)
        y3 = yacc[:, :].rearrange("p (c n) -> p c n", c=NLT)

        B = [ctx.enter_context(nc.psum_tensor(f"B{i}", [P, 512], F32)) for i in range(8)]

        wr = slot(2, 2048, 2176).rearrange("p (k e) -> p k e", k=KD)
        wra = slot(2, 2176, 2304).rearrange("p (k e) -> p k e", k=KD)
        junk = slot(4, 0, 1024)
        x1t = yacc[:, :].rearrange("p (k t) -> p k t", k=KD)
        lgt = fr[:, 0:512]
        lg = fr[:, 512:576].rearrange("p (c e) -> p c e", c=NLT)
        mx4 = fr[:, 576:580]
        sm4 = fr[:, 580:584]
        rc4 = fr[:, 584:588]
        aft = fr[:, 592:656].rearrange("p (c e) -> p c e", c=NLT)
        wka = fr[:, 1024:1536]
        wkb = fr[:, 1536:2048]
        top8 = fr[:, 656:664]
        mkt = fr[:, 672:736].rearrange("p (c e) -> p c e", c=NLT)

        d_vec1, d_vec2, d_cst, d_filt = map(sem, ["d_vec1", "d_vec2", "d_cst", "d_filt"])
        d_taps, d_dft, d_inv = map(sem, ["d_taps", "d_dft", "d_inv"])
        d_x, d_pos, d_ctx, d_row, d_gate, d_wr = map(sem, ["d_x", "d_pos", "d_ctx", "d_row", "d_gate", "d_wr"])
        d_w = [sem(f"d_w{i}") for i in range(2)]
        d_ring = [sem(f"d_ring{i}") for i in range(NSLOT)]
        d_extra = sem("d_extra")
        d_out = sem("d_out")
        names = ["p_vt", "p_fil", "p_kf", "p_ksp", "p_w", "p_modt", "p_g1", "p_htl", "p_htc", "p_gt",
                 "p_gtr", "p_cs", "p_at", "p_cm", "p_mt", "p_hy", "p_utr", "p_qk", "p_kc", "p_ktr", "p_v",
                 "p_st", "p_o", "p_usp", "p_inv", "p_sc", "p_mb", "p_num", "p_ytr", "p_y", "p_h2", "p_lg",
                 "p_lgt", "p_aft", "p_mk", "p_rk", "p_xs", "p_gu", "p_pwt", "p_ht", "p_dn", "p_sca", "v_ch",
                 "v_vt", "v_arg", "v_hpm", "v_kf", "v_mrow", "v_aff", "v_grow", "v_xn", "v_htc", "v_cpad",
                 "v_gsum", "v_sel", "v_x", "v_ew", "v_cs", "v_at", "v_cum", "v_m", "v_mt",
                 "v_conv", "v_ksp", "v_usp", "a_hq", "v_fws", "v_kc", "v_st", "v_cx", "v_inv", "v_d", "v_sw", "v_tot", "v_hs", "v_hn", "v_x1",
                 "v_wra", "v_h2", "v_ry", "a_y0", "g_y0", "v_lgt", "v_sub", "v_aft", "v_mk", "v_mkt", "v_slot", "v_xs", "v_hid",
                 "v_hdt", "v_yacc", "v_res", "v_cp", "a_ch", "a_th", "a_fil", "a_dec", "a_ksp", "a_ss",
                 "a_std", "a_htl", "a_gt", "a_lf", "a_ew", "a_us", "a_qk", "a_ktr", "a_v", "a_o", "a_usp",
                 "a_e", "a_n2", "a_sq", "a_yt", "a_sy", "a_sdy", "a_ss2", "a_h2", "a_exp", "a_xs", "a_sil",
                 "a_pwt", "a_ye", "a_fsd", "g_ms", "g_zero", "g_kw", "g_sel", "g_cp"]
        S = {n: sem(n) for n in names}

        SLOT_OF = [3, 7, 6, 5, 0, 1, 4, 2]
        NPAIR = E // 2
        TILES = [("g", 0), ("u", 0), ("g", 1), ("u", 1), ("d", 0)]
        for q in range(2, 8):
            TILES += [("g", q), ("u", q), ("d", q - 1)]
        TILES += [("d", 7)]
        NTI = len(TILES)
        LOADS = [("m", 0, 0), ("m", 1, 1), ("m", 2, 0), ("m", 3, 1), ("i", 0, 0), ("m", 4, 1), ("i", 1, 1),
                 ("m", 5, 0), ("i", 2, 0), ("m", 6, 1), ("i", 3, 1), ("m", 7, 0), ("i", 4, 0), ("m", 8, 1),
                 ("i", 5, 1), ("m", 9, 0), ("m", 10, 0), ("m", 11, 0), ("o", 0, 0), ("o", 1, 1)]
        DONE = [("m", 0), ("m", 1), ("m", 2), ("m", 3), ("m", 4), ("i", 0), ("m", 5), ("i", 1), ("m", 6),
                ("i", 2), ("m", 7), ("i", 3), ("m", 8), ("i", 4), ("m", 9), ("m", 10), ("m", 11), ("i", 5),
                ("o", 0), ("o", 1)]

        def done_count(kind, i):
            return DONE.index((kind, i)) + 1

        w_mod, w_in, w_out = A["w_mod"][0], A["w_in"][0], A["w_out"][0]

        N_VEC1, N_VEC2 = 5, 7
        hy_bank, qk_bank, kc_bank, v_bank, o_bank, usp_bank = {}, {}, {}, {}, {}, {}
        ksp_bank, htl_bank, htc_bank = {}, {}, {}
        TAPS = [(1, 0), (0, 0), (0, 1), (0, 2), (0, 3), (1, 1), (1, 2), (1, 3)]

        def mb_bank(h, d):
            return (3 if h < 2 else 2) + d

        def score_bank(h):
            return h if h < 2 else 0

        INV_BANK = [1, 1, 1, 2]
        usq = moe[:, 3072:3584].rearrange("p (c n) -> p c n", n=DV)

        block = ctx.enter_context(nc.Block())

        @block.sync
        def _(sp):
            def rows(dst, r, src, n):
                sp.dma_start(dst[r:r + n, :], src.rearrange("(a b) -> a b", b=P)).then_inc(d_vec2, 16)
            sp.dma_start(cst[:, :], A["cst"]).then_inc(d_cst, 16)
            sp.dma_start(dlb, A["dl"]).then_inc(d_cst, 16)
            sp.wait_ge(S["g_ms"], 1)
            sp.dma_start(vr2[R_CW:R_CW + 36, :],
                         A["conv_w"][0].rearrange("w (a b) -> (w a) b", b=P)).then_inc(d_vec2, 16)
            rows(vr2, R_CB, A["conv_b"][0], 12)
            rows(vr2, R_MLN, A["ml_norm"][0], 4)
            sp.dma_start(fw3[0:FH, :], A["filt_w3"][0]).then_inc(d_taps, 16)
            sp.dma_start(fw4[0:FH, :], A["filt_w4"][0]).then_inc(d_taps, 16)
            sp.dma_start(hyb[0:1, :], A["hyena_bias"]).then_inc(d_taps, 16)
            sp.dma_start(slot(5, 0, 2048), A["dft"]).then_inc(d_dft, 16)

            def weight(n):
                kind, i, at = LOADS[n]
                before = [t[0:2] for t in LOADS[:n] if t[2] == at]
                if before:
                    sp.wait_ge(S["p_w"], done_count(*before[-1]))
                dst = slot(at)
                if kind == "m":
                    r, kp = divmod(i, 4)
                    src = w_mod[kp * 2 * P:(kp + 1) * 2 * P, r * 2048:(r + 1) * 2048]
                    dst = dst.rearrange("p (k n) -> p k n", k=2)
                elif kind == "i":
                    src, dst = w_in[:, i * CH:(i + 1) * CH], dst.rearrange("p (k n) -> p k n", k=KD)
                else:
                    src, dst = w_out[:, i * CH:(i + 1) * CH], dst.rearrange("p (k n) -> p k n", k=KD)
                sp.dma_start(dst, src.rearrange("(k p) n -> p k n", p=P)).then_inc(d_w[at], 16)

            for n in range(len(LOADS)):
                if n == 2:
                    sp.dma_start(cx, A["ctx"][0].rearrange("(c p) n -> p c n", p=P)).then_inc(d_ctx, 16)
                    sp.dma_start(x3, A["x"][0].rearrange("(c p) n -> p c n", p=P)).then_inc(d_x, 16)
                    sp.dma_start(xn, A["pos"].rearrange("(c p) n -> p c n", p=P)).then_inc(d_pos, 16)
                if n == 4:
                    sp.dma_start(wgate_sb, w_in[:, 6 * CH:6 * CH + 16].rearrange("(k p) n -> p k n", p=P))\
                        .then_inc(d_gate, 16)
                    sp.dma_start(gb, A["ml_gate_b"][0].partition_broadcast(P)).then_inc(d_gate, 16)
                if n == 6:
                    sp.wait_ge(S["p_htl"], KD)
                    sp.dma_start(slot(6, 1808, 3856), A["idft"]).then_inc(d_inv, 16)
                weight(n)

            def expert_tile(i, pair):
                kind, st = TILES[i]
                e2, q = divmod(st, 4)
                dst, loaded = slot(SLOT_OF[i % NSLOT]), d_ring[i % NSLOT]
                if i == NSLOT and isinstance(pair, int) and pair == 0:
                    dst, loaded = yacc[:, :], d_extra
                ex = 2 * pair + e2
                if kind == "d":
                    src = A["w_exp_down"][0, bass.ds(ex, 1), q * CH:(q + 1) * CH, :]
                    src = src.rearrange("o (k p) n -> p (o k) n", p=P)
                    dst = dst.rearrange("p (k n) -> p k n", k=4)
                else:
                    w = A["w_exp_gate" if kind == "g" else "w_exp_up"]
                    src = w[0, bass.ds(ex, 1), :, q * CH:(q + 1) * CH]
                    src = src.rearrange("o (k p) n -> p (o k) n", p=P)
                    dst = dst.rearrange("p (k n) -> p k n", k=KD)
                sp.dma_start(dst, src).then_inc(loaded, 16)

            def used(i, pair):
                kind, st = TILES[i]
                sp.wait_ge(S["p_dn" if kind == "d" else "p_gu"], 8 * pair + st + 1)

            sp.wait_ge(S["p_w"], done_count("i", 5))
            expert_tile(0, 0)
            sp.wait_ge(S["p_inv"], NCH)
            expert_tile(1, 0)
            sp.wait_ge(S["p_num"], 16)
            expert_tile(2, 0)
            expert_tile(3, 0)
            sp.wait_ge(S["v_grow"], 2)
            sp.dma_start(wr, A["w_router"][0].rearrange("(k p) e -> p k e", p=P)).then_inc(d_wr, 16)
            sp.wait_ge(S["p_w"], len(DONE))
            expert_tile(4, 0)
            expert_tile(5, 0)
            sp.wait_ge(S["a_ss2"], NLT)
            expert_tile(6, 0)
            sp.wait_ge(S["p_lg"], NLT)
            expert_tile(7, 0)
            expert_tile(NSLOT, 0)
            for i in range(1, NTI):
                if i != NSLOT:
                    used(i, 0)
                expert_tile((i + NSLOT) % NTI, 0 if i + NSLOT < NTI else 1)
            with sp.Fori(1, NPAIR - 1) as j:
                for i in range(NTI):
                    used(i, j)
                    expert_tile((i + NSLOT) % NTI, j if i + NSLOT < NTI else j + 1)
            for i in range(NTI - NSLOT):
                used(i, NPAIR - 1)
                expert_tile(i + NSLOT, NPAIR - 1)
            for c in (1, 2, 0, 3):
                if c:
                    sp.wait_ge(S["v_res"], c)
                else:
                    sp.wait_ge(S["g_y0"], 2)
                sp.dma_start(out[0, c * P:(c + 1) * P, :], y3[:, c, :]).then_inc(d_out, 16)
            sp.wait_ge(d_out, 16 * NLT)

        @block.gpsimd
        def _(pool):
            g = nc.gpsimd
            g.memset(vr2, 0.0).then_inc(S["g_ms"], 1)
            g.memset(brow, 0.0).then_inc(S["g_zero"], 1)
            g.memset(prow, 0.0).then_inc(S["g_zero"], 1)
            g.memset(moe[:, 5632:5888], 0.0).then_inc(S["g_zero"], 1)
            g.memset(epsc, EPS).then_inc(S["g_zero"], 1)
            for r, n, src in ((R_C, 8, A["c"][0]), (R_CC, 8, A["c_ctx"]), (R_PRE1, 8, A["pre_norm1"][0]),
                              (R_PRE2, 8, A["pre_norm2"][0]), (R_BMOD, 48, A["b_mod"][0])):
                pool.dma_start(vr1[r:r + n, :], src.rearrange("(a b) -> a b", b=P)).then_inc(d_vec1, 16)
            pool.wait_ge(S["g_zero"], 2)
            for i, (o, norm) in enumerate(((2 * D, "post_norm1"), (5 * D, "post_norm2"))):
                r = 64 * i
                pool.dma_start(brow[r:r + 33:32, :], A["b_mod"][0, o:o + D].rearrange("(a n) -> a n", a=2)).then_inc(d_row, 16)
                pool.dma_start(prow[r:r + 33:32, :], A[norm][0].rearrange("(a n) -> a n", a=2)).then_inc(d_row, 16)
            pool.wait_ge(S["a_ew"], 1)
            pool.wait_ge(S["v_kc"], NCT)
            pool.wait_ge(S["a_ktr"], 2)
            n = 0
            for st in range(NTT - 1):
                for d in range(2):
                    tile = [t for t in range(NTT) if step_of(d, t) == st][0]
                    r = 32 * d + 4 * st
                    src = kk[:, tile, :].rearrange("p (h n) -> p h n", h=NH)
                    wsb = ew[:, 2, r:r + NH].rearrange("p (h o) -> p h o", o=1).to_broadcast([P, NH, DK])
                    g.tensor_tensor(kwb[n].rearrange("p (h n) -> p h n", h=NH), src, wsb,
                                    ALU.mult).then_inc(S["g_kw"], 1)
                    n += 1
            pool.wait_ge(S["v_hn"], NLT)
            g.memset(hid[0:CAP, :, :], 0.0).then_inc(S["g_ms"], 1)

            def combination(j):
                pool.wait_ge(S["v_sel"], 4 * j + 1)
                g.tensor_copy(afp, affr[:, bass.ds(2 * j, 2), :]
                              .rearrange("p e c -> p (e c)")).then_inc(S["g_cp"], 1)
                pool.wait_ge(S["g_cp"], j + 1)
                pool.wait_ge(S["v_sel"], 4 * j + 3)
                for e2 in range(2):
                    af = afp[:, 4 * e2:4 * e2 + 4].rearrange("p (c o) -> p c o", o=1).to_broadcast([P, NLT, CAP])
                    g.tensor_tensor(pw[:, :, CAP * e2:CAP * e2 + CAP], peq[:, :, CAP * e2:CAP * e2 + CAP], af,
                                    ALU.mult).then_inc(S["g_sel"], 1)

            pool.wait_ge(S["v_slot"], 2)
            combination(0)
            pool.wait_ge(S["p_gu"], 4)
            g.memset(yacc[:, :], 0.0).then_inc(S["g_ms"], 1)
            with pool.Fori(1, NPAIR) as j:
                combination(j)
            pool.wait_ge(S["a_y0"], 1)
            g.tensor_tensor(y3[:, 0, :], y3[:, 0, :], g2p[:, :], ALU.mult).then_inc(S["g_y0"], 1)
            pool.wait_ge(S["g_y0"], 1)
            g.tensor_tensor(y3[:, 0, :], y3[:, 0, :], x3[:, 0, :], ALU.add).then_inc(S["g_y0"], 1)

        @block.tensor
        def _(pe):
            mm, tr = nc.tensor.matmul, nc.tensor.transpose
            idn = ident
            users = {}

            def take(b):
                if b in users:
                    pe.wait_ge(*users[b])

            def upper(m):
                return ident[0:m, 0:m]

            pe.wait_ge(d_cst, 32)
            pe.wait_ge(d_vec2, 16 * N_VEC2)
            tr(B[1][:, 0:R2_ROWS], vr2[0:R2_ROWS, :], upper(R2_ROWS)).then_inc(S["p_vt"], 1)
            for n, w in enumerate((fw1[0:FEMB, :], fw2[0:FH, :], fw3[0:FH, :])):
                if n == 0:
                    pe.wait_ge(d_filt, 48)
                if n == 2:
                    pe.wait_ge(d_taps, 48)
                for half in range(2):
                    if n:
                        pe.wait_ge(S["a_fil"], 2 * n + half - 1)
                    src = fh[0:FH, half * LC:(half + 1) * LC] if n else zft[0:FEMB, half * LC:(half + 1) * LC]
                    mm(B[2 + half][0:FH, (n % 2) * LC:(n % 2 + 1) * LC], w, src, start=True, stop=True).then_inc(S["p_fil"], 1)
                if n == 0:
                    pe.wait_ge(d_vec1, 16 * N_VEC1)
                    tr(B[0][:, 0:R1_ROWS], vr1[0:R1_ROWS, :], upper(R1_ROWS)).then_inc(S["p_vt"], 1)
            users[0] = users[1] = (S["v_vt"], 2)
            pe.wait_ge(S["v_fws"], 2)
            pe.wait_ge(S["a_fil"], 6)
            for n, (w, c) in enumerate(TAPS):
                b = 4 + n % 4
                if n >= 4:
                    pe.wait_ge(S["v_kf"], n - 3)
                mm(B[b][:, :], fh[0:FH, c * P:(c + 1) * P], fws[0:FH, w, :], start=True, stop=True)\
                    .then_inc(S["p_kf"], 1)
                users[b] = (S["v_kf"], n + 1)
            users[2] = users[3] = (S["a_fil"], 6)
            def weights(kind, i):
                n = [t[0:2] for t in LOADS].index((kind, i))
                at = LOADS[n][2]
                pe.wait_ge(d_w[at], 16 * sum(t[2] == at for t in LOADS[:n + 1]))
                return slot(at)

            def mod_tile(i):
                r, kp = divmod(i, 4)
                w = weights("m", i).rearrange("p (k n) -> p k n", k=2)
                if kp == 0:
                    take(2)
                for k in range(2):
                    for n in range(4):
                        x = mm(B[2][32 * n:32 * n + 32, :], cpad[:, 2 * kp + k, :], w[:, k, n * CH:(n + 1) * CH],
                               start=(kp == 0 and k == 0), stop=(kp == 3 and k == 1))
                x.then_inc(S["p_w"], 1)
                users[2] = (S["v_mrow"], r + 1)

            def mod_turn(r, b):
                pe.wait_ge(S["v_mrow"], r + 1)
                take(b)
                for q in range(4):
                    x = tr(B[b][:, q * P:(q + 1) * P], mrow[:, q * P:(q + 1) * P], idn)
                x.then_inc(S["p_modt"], 1)
                users[b] = (S["v_aff"], r + 1)

            def gate_rows(g, n0, b0):
                pe.wait_ge(S["v_grow"], g + 1)
                for h in range(2):
                    take(b0 + h)
                    row = 32 * (n0 + h)
                    mm(B[b0 + h][:, :], ident[:, row:row + 1].to_broadcast([P, P]), mrow[:, :],
                       start=True, stop=True).then_inc(S["p_g1"], 1)
                    users[b0 + h] = (S["v_cp"], 2 * g + h + 1)

            rotation = [3, 4, 5, 6, 7]

            def next_bank():
                b = rotation.pop(0)
                rotation.append(b)
                take(b)
                return b

            def spectrum(n, src, p_done, odd_used, even_used, banks):
                kc, w = divmod(n, 2)
                banks[n] = []
                for odd in (1, 0):
                    b = next_bank()
                    for c in (2 * odd, 2 * odd + 1):
                        x = mm(B[b][:, :], dft[:, w, c, kc * P:(kc + 1) * P], src(w, c), start=(c % 2 == 0), stop=(c % 2 == 1))
                    x.then_inc(p_done, 1)
                    banks[n].append(b)
                    users[b] = (odd_used if odd else even_used, n + 1)

            pe.wait_ge(S["v_cpad"], 1)
            mod_tile(0)
            mod_tile(1)

            def filter_spectrum(n):
                spectrum(n, lambda w, c: hpm[:, w, c, :], S["p_ksp"], S["a_ksp"], S["v_ksp"], ksp_bank)

            pe.wait_ge(d_dft, 16)
            pe.wait_ge(S["v_hpm"], 1)
            pe.wait_ge(S["v_kf"], TAPS.index((0, 3)) + 1)
            filter_spectrum(0)
            pe.wait_ge(S["v_kf"], len(TAPS))
            filter_spectrum(1)
            filter_spectrum(2)
            mod_tile(2)
            filter_spectrum(3)
            mod_tile(3)
            mod_turn(0, 1)
            pe.wait_ge(S["v_xn"], NTT)
            for k in range(KD):
                for lat in (1, 0):
                    b = next_bank()
                    (htl_bank if lat else htc_bank)[k] = b
                    src = xn if lat else cx
                    for c in range(NLT if lat else NCT):
                        x = tr(B[b][:, c * P:(c + 1) * P], src[:, c, k * P:(k + 1) * P], idn)
                    x.then_inc(S["p_htl" if lat else "p_htc"], 1)
                    users[b] = (S["a_htl" if lat else "v_htc"], k + 1)
            pe.wait_ge(S["a_htl"], KD)
            pe.wait_ge(S["v_htc"], KD)
            pe.wait_ge(d_gate, 32)
            take(0)
            for k in range(KD):
                mm(B[0][0:16, :], wgate_sb[:, k, :], ht[:, k, LC:], start=(k == 0), stop=(k == KD - 1))
                x = mm(B[0][32:48, 0:LC], wgate_sb[:, k, :], ht[:, k, 0:LC], start=(k == 0), stop=(k == KD - 1))
            x.then_inc(S["p_gt"], 1)
            users[0] = (S["a_gt"], 2)
            def hyena_tile(i):
                w = weights("i", i).rearrange("p (k n) -> p k n", k=KD)
                for m in range(NCH):
                    b = next_bank()
                    for k in range(KD):
                        x = mm(B[b][:, :], w[:, k, m * P:(m + 1) * P], ht[:, k, LC:], start=(k == 0), stop=(k == KD - 1))
                    x.then_inc(S["p_hy" if m < NCH - 1 else "p_w"], 1)
                    n = i * NCH + m
                    hy_bank[n] = b
                    users[b] = (S["v_conv"], n + 1)
                    if m == 1:
                        mod_tile(4 + i)

            hyena_tile(0)
            pe.wait_ge(S["a_gt"], 2)
            take(1)
            for d in range(2):
                for t in range(NTT):
                    o = (d * NTT + step_of(d, t)) * 16
                    x = tr(B[1][:, o:o + 16], gt[0:16, t * P:(t + 1) * P], upper(16))
            x.then_inc(S["p_gtr"], 1)
            users[1] = (S["v_gsum"], 2)
            hyena_tile(1)
            pe.wait_ge(S["a_lf"], 1)
            take(0)
            mm(B[0][:, 0:24], cst[:, C_UP:C_UP + P], lf[:, 0, :, :], start=True, stop=True)
            mm(B[0][:, 32:56], cst[:, C_LO:C_LO + P], lf[:, 1, :, :], start=True, stop=True)
            mm(B[0][:, 64:88], ones, lf[:, 0, :, :], start=True, stop=True)
            mm(B[0][:, 96:120], ones, lf[:, 1, :, :], start=True, stop=True).then_inc(S["p_cs"], 1)
            users[0] = (S["v_cs"], 1)
            pe.wait_ge(S["v_cs"], 1)
            take(1)
            tr(B[1][0:64, 0:P], aco, idn).then_inc(S["p_at"], 1)
            users[1] = (S["v_at"], 1)
            hyena_tile(2)
            pe.wait_ge(S["v_cum"], 1)
            take(0)
            tr(B[0][:, 0:64], atp[0:64, 1, 64:192], upper(64))
            mm(B[0][:, 64:128], mrow_t[0:64, 0:1].to_broadcast([64, P]), upper(64),
               start=True, stop=True).then_inc(S["p_cm"], 1)
            users[0] = (S["v_m"], 1)
            w = weights("i", 3).rearrange("p (k n) -> p k n", k=KD)
            for m in range(4):
                b = next_bank()
                for k in range(KD):
                    x = mm(B[b][:, :], w[:, k, m * P:(m + 1) * P], ht[:, k, LC:], start=(k == 0), stop=(k == KD - 1))
                x.then_inc(S["p_qk"], 1)
                qk_bank[m] = b
                users[b] = (S["a_qk"], m + 1)
                if m == 0:
                    pe.wait_ge(S["v_m"], 1)
                    take(1)
                    tr(B[1][0:64, 0:P], mcur, idn).then_inc(S["p_mt"], 1)
                    users[1] = (S["v_mt"], 1)
                if m == 1:
                    mod_tile(7)
            for c in range(NCT):
                b = next_bank()
                for k in range(KD):
                    x = mm(B[b][:, 0:QK], ht[:, k, c * P:(c + 1) * P], w[:, k, QK:2 * QK], start=(k == 0), stop=(k == KD - 1))
                x.then_inc(S["p_kc"] if c < NCT - 1 else S["p_w"], 1)
                kc_bank[c] = b
                users[b] = (S["v_kc"], c + 1)
            for i in range(NCH):
                pe.wait_ge(S["v_conv"], 2 * NCH + i + 1)
                take(i % 2)
                for c in range(NLT):
                    times = ut[:, i, :].rearrange("p (c t w) -> p w c t", c=2, w=2)[:, c // 2, c % 2, :]
                    x = tr(B[i % 2][:, c * P:(c + 1) * P], times, idn)
                x.then_inc(S["p_utr"], 1)
                users[i % 2] = (S["a_us"], i + 1)
            pe.wait_ge(S["a_qk"], 4)
            for g in range(2):
                take(g)
                for c in range(2):
                    for hp in range(2):
                        x = tr(B[g][:, c * QK + hp * P:c * QK + (hp + 1) * P],
                               kt[:, hp, (2 * g + c) * P:(2 * g + c + 1) * P], idn)
                x.then_inc(S["p_ktr"], 1)
                users[g] = (S["a_ktr"], g + 1)
            w = weights("i", 4).rearrange("p (k n) -> p k n", k=KD)
            for t in range(NTT):
                b = next_bank()
                for k in range(KD):
                    x = mm(B[b][:, :], ht[:, k, t * P:(t + 1) * P], w[:, k, :], start=(k == 0), stop=(k == KD - 1))
                x.then_inc(S["p_v"] if t < NTT - 1 else S["p_w"], 1)
                v_bank[t] = b
                users[b] = (S["a_v"], t + 1)
                if t == 1:
                    mod_turn(1, 1)
                if t == 3:
                    mod_tile(8)
            gate_rows(0, 0, 0)
            def states(n0, n1):
                for n in range(n0, n1):
                    st, d = divmod(n, 2)
                    tile = [t for t in range(NTT) if step_of(d, t) == st][0]
                    pe.wait_ge(S["g_kw"], n + 1)
                    if n == 0:
                        pe.wait_ge(S["a_v"], NTT)
                    take(n % 2)
                    for h in range(NH):
                        po = DK * (h % 2)
                        x = mm(B[n % 2][po:po + DK, (h // 2) * (DV + 1):(h // 2 + 1) * (DV + 1)],
                               kwb[n][:, h * DK:(h + 1) * DK], v1[:, tile, h, :], start=True, stop=True)
                    x.then_inc(S["p_st"], 1)
                    users[n % 2] = (S["v_st"], n + 1)

            def prepare(h):
                po = DK * (h % 2)
                sbank = score_bank(h)
                take(sbank)
                for c in range(NLT):
                    x = mm(B[sbank][:, c * P:(c + 1) * P], kt[po:po + DK, h // 2, c * P:(c + 1) * P],
                           qt[po:po + DK, h // 2, c * P:(c + 1) * P], start=True, stop=True)
                x.then_inc(S["p_sc"], 1)
                users[sbank] = (S["v_sw"], 2 * h + 2)
                for d in range(2):
                    mb = mb_bank(h, d)
                    take(mb)
                    for c in range(NLT):
                        r = 32 * d + 4 * step_of(d, NCT + c) + h
                        x = mm(B[mb][:, c * P:(c + 1) * P], ident[0:64, r:r + 1].to_broadcast([64, P]),
                               mrow_t[0:64, :], start=True, stop=True)
                    x.then_inc(S["p_mb"], 1)
                    users[mb] = (S["v_d"], 2 * h + d + 1)

            def product_spectrum(n):
                spectrum(n, lambda w, c: us[:, c, :], S["p_usp"], S["a_usp"], S["v_usp"], usp_bank)

            pe.wait_ge(S["a_us"], NCH)
            rotation[:] = [3, 4, 5, 6, 7]
            states(0, 4)
            product_spectrum(0)
            states(4, 8)
            product_spectrum(1)
            mod_tile(9)
            states(8, 10)
            product_spectrum(2)
            product_spectrum(3)
            rotation[:] = [6, 7, 5]
            w = weights("i", 5).rearrange("p (k n) -> p k n", k=KD)
            for c in range(NLT):
                b = next_bank()
                for k in range(KD):
                    x = mm(B[b][:, :], ht[:, k, LC + c * P:LC + (c + 1) * P], w[:, k, :], start=(k == 0), stop=(k == KD - 1))
                x.then_inc(S["p_o"] if c < NLT - 1 else S["p_w"], 1)
                o_bank[c] = b
                users[b] = (S["a_o"], c + 1)
                if c == 0:
                    pe.wait_ge(S["v_mt"], 1)
                    prepare(0)
                if c == 1:
                    mod_tile(10)
                if c == 2:
                    prepare(1)
                    mod_tile(11)
            def numerators(h):
                po = DK * (h % 2)
                for d in range(2):
                    pe.wait_ge(S["v_sw"], 2 * h + d + 1)
                    for cp in range(2):
                        n = 4 * h + 2 * d + cp
                        ba, bb = 4 + 2 * (n % 2), 5 + 2 * (n % 2)
                        take(ba)
                        take(bb)
                        for c in (2 * cp, 2 * cp + 1):
                            o = (c % 2) * (DV + 1)
                            st = step_of(d, NCT + c)
                            mm(B[bb][:, o:o + DV + 1], qt[po:po + DK, h // 2, c * P:(c + 1) * P],
                               cstate[po:po + DK, d, st - NCT, (h // 2) * (DV + 1):(h // 2 + 1) * (DV + 1)],
                               start=True, stop=True)
                            x = mm(B[ba][:, o:o + DV + 1], ebufs[h % 2][:, d, c * P:(c + 1) * P], v1[:, NCT + c, h, :],
                                   start=True, stop=True)
                        x.then_inc(S["p_num"], 1)
                        users[ba] = users[bb] = (S["v_tot"], n + 1)

            def inverse(i):
                b = INV_BANK[i]
                take(b)
                for odd in range(2):
                    t = slice(odd * LC, (odd + 1) * LC)
                    for wv in range(2):
                        for k in range(NKC):
                            x = mm(B[b][:, t], ksp[:, wv, k, odd, i * P:(i + 1) * P], idft[:, wv, k, t],
                                   start=(wv == 0 and k == 0), stop=(wv == 1 and k == NKC - 1))
                x.then_inc(S["p_inv"], 1)
                users[b] = (S["v_inv"], i + 1)

            pe.wait_ge(S["v_st"], 2 * (NTT - 1))
            numerators(0)
            pe.wait_ge(d_inv, 16)
            pe.wait_ge(S["v_cx"], NKC)
            inverse(0)
            prepare(2)
            numerators(1)
            inverse(1)
            prepare(3)
            numerators(2)
            inverse(2)
            inverse(3)
            numerators(3)

            def project(c, ks, halves=(0, 1)):
                for half in halves:
                    b = 2 * c + half
                    if ks[0] == 0:
                        take(b)
                    for k in ks:
                        lhs = x0t[:, k, c * P:(c + 1) * P] if k < NCH else ymt[:, k - NCH, c * P:(c + 1) * P]
                        x = mm(B[b][:, :], lhs, wo[half][:, k, :], start=(k == 0), stop=(k == KD - 1))
                    if ks[-1] == KD - 1:
                        x.then_inc(S["p_w" if c == NLT - 1 else "p_y"], 1)
                        users[b] = (S["v_x1"], b + 1)

            pe.wait_ge(S["v_inv"], NCH)
            wo = [weights("o", i).rearrange("p (k n) -> p k n", k=KD) for i in range(2)]
            hy_ks, ml_ks = range(NCH), range(NCH, KD)
            for c in range(NLT - 1):
                project(c, hy_ks)
            for i in range(NLT):
                pe.wait_ge(S["v_hn"], i + 1)
                b = 6 + i % 2
                take(b)
                for h in range(NH):
                    x = tr(B[b][:, h * P:(h + 1) * P], hsum[:, i, h * P:(h + 1) * P], idn)
                x.then_inc(S["p_ytr"], 1)
                users[b] = (S["a_yt"], i + 1)
            mod_turn(2, 6)
            pe.wait_ge(S["a_yt"], NLT)
            project(0, ml_ks)
            gate_rows(1, 2, 6)
            project(1, ml_ks)
            project(2, ml_ks)

            def rows_turned(c):
                pe.wait_ge(S["v_x1"], 2 * c + 2)
                for g in range(2):
                    b = 2 * (c % 2) + g
                    take(b)
                    for k in range(4):
                        x = tr(B[b][:, k * P:(k + 1) * P], x3[:, c, (4 * g + k) * P:(4 * g + k + 1) * P], idn)
                    x.then_inc(S["p_h2"], 1)
                    users[b] = (S["a_h2"] if g else S["v_h2"], c + 1)

            def logits(c):
                pe.wait_ge(S["a_h2"], c + 1)
                pe.wait_ge(S["v_h2"], c + 1)
                if c == 0:
                    take(4)
                for k in range(KD):
                    x = mm(B[4][0:E, c * P:(c + 1) * P], wra[:, k, :], x1t[:, k, c * P:(c + 1) * P],
                           start=(k == 0), stop=(k == KD - 1))
                x.then_inc(S["p_lg"], 1)

            rows_turned(0)
            rows_turned(1)
            project(3, range(KD), (0,))
            rows_turned(2)
            pe.wait_ge(S["v_wra"], 1)
            logits(0)
            logits(1)
            project(3, range(KD), (1,))
            take(5)
            for k in range(KD):
                mm(B[5][:, NLT * E:(NLT + 1) * E], aff2[:, 1, k:k + 1].to_broadcast([P, P]), wr[:, k, :],
                   start=(k == 0), stop=(k == KD - 1))
            logits(2)
            rows_turned(3)
            logits(3)
            pe.wait_ge(S["v_lgt"], 1)
            for c in range(NLT):
                x = tr(B[5][:, c * E:(c + 1) * E], lgt[0:E, c * P:(c + 1) * P], upper(E))
            x.then_inc(S["p_lgt"], 1)
            pe.wait_ge(S["v_aft"], 1)
            take(6)
            for c in range(NLT):
                x = tr(B[6][0:E, c * P:(c + 1) * P], aft[:, c, :], idn)
            x.then_inc(S["p_aft"], 1)
            pe.wait_ge(S["v_mk"], 1)
            take(7)
            for c in range(NLT):
                x = tr(B[7][:, c * E:(c + 1) * E], wka[0:E, c * P:(c + 1) * P], upper(E))
            x.then_inc(S["p_mk"], 1)
            pe.wait_ge(S["v_mkt"], 1)
            take(0)
            mm(B[0][:, 0:NLT * E], cst[:, C_UP:C_UP + P], mkt, start=True, stop=False)
            for s in range(1, NLT):
                x = mm(B[0][:, s * E:NLT * E], ones, mkt[:, 0:NLT - s, :], start=False, stop=(s == NLT - 1))
            x.then_inc(S["p_rk"], 1)
            pe.wait_ge(S["v_slot"], 2)

            pe.wait_ge(S["g_ms"], 2)
            def expert_pair(j, first):
                pe.wait_ge(S["v_sel"], 4 * j + 4)
                for g in range(2):
                    for k in range(4):
                        for c in range(NLT):
                            dk = 4 * g + k
                            x = mm(B[6 + g][:, k * P:(k + 1) * P], x3[:, c, dk * P:(dk + 1) * P], psel[:, c, :],
                                   start=(c == 0), stop=(c == NLT - 1))
                    x.then_inc(S["p_xs"], 1)

                def ring_tile(kind, st):
                    i = TILES.index((kind, st))
                    if first and i == NSLOT:
                        pe.wait_ge(d_extra, 16)
                        return yacc[:, :]
                    count = NTI // NSLOT * j + i // NSLOT + 1
                    if i % NSLOT == 0 and not (first and i == 0):
                        count = count - 1
                    pe.wait_ge(d_ring[i % NSLOT], 16 * count)
                    return slot(SLOT_OF[i % NSLOT])

                def gate_up(st):
                    e2 = st // 4
                    wg = ring_tile("g", st).rearrange("p (k n) -> p k n", k=KD)
                    wu = ring_tile("u", st).rearrange("p (k n) -> p k n", k=KD)
                    if st == 0:
                        pe.wait_ge(S["v_xs"], 4 * j + 4)
                    if st >= 2:
                        pe.wait_ge(S["v_hid"], 8 * j + st - 1)
                    for k in range(KD):
                        if st == 0 and k == 4:
                            pe.wait_ge(S["a_xs"], 4 * j + 4)
                        lhs = xst[:, k, CAP * e2:CAP * (e2 + 1)]
                        mm(B[st % 2][0:CAP, :], lhs, wg[:, k, :], start=(k == 0), stop=(k == KD - 1))
                        x = mm(B[st % 2][CAP:P, :], lhs, wu[:, k, :], start=(k == 0), stop=(k == KD - 1))
                    x.then_inc(S["p_gu"], 1)

                def down(st):
                    e2, q = divmod(st, 4)
                    pe.wait_ge(S["v_hid"], 8 * j + st + 1)
                    for k in range(4):
                        x = tr(B[2 + st % 2][:, k * P:(k + 1) * P], hid[:, st % 2, k * P:(k + 1) * P], idn)
                    x.then_inc(S["p_ht"], 1)
                    wd = ring_tile("d", st).rearrange("p (k n) -> p k n", k=4)
                    pe.wait_ge(S["v_hdt"], 8 * j + st + 1)
                    for k in range(4):
                        for half in range(2):
                            x = mm(B[4 + e2][CAP * half:CAP * (half + 1), :], hdt[:, st % 2, k * CAP:(k + 1) * CAP],
                                   wd[:, k, half * CH:(half + 1) * CH],
                                   start=(q == 0 and k == 0), stop=(q == 3 and k == 3))
                    x.then_inc(S["p_dn"], 1)

                gate_up(0)
                gate_up(1)
                pe.wait_ge(S["g_sel"], 2 * j + 2)
                for c in range(NLT):
                    x = tr(B[6][:, c * P:(c + 1) * P], pw[:, c, :], idn)
                x.then_inc(S["p_pwt"], 1)
                down(0)
                for st in range(2, 8):
                    gate_up(st)
                    down(st - 1)
                down(7)
                pe.wait_ge(S["a_pwt"], j + 1)
                pe.wait_ge(S["a_ye"], 4 * j + 4)
                for n in range(2 * NLT):
                    c, half = divmod(n, 2)
                    if n >= 2:
                        pe.wait_ge(S["v_yacc"], 8 * j + n - 1)
                    mm(B[6 + half][:, :], pwt[:, c, :], ye[:, half * CH:(half + 1) * CH],
                       start=True, stop=True).then_inc(S["p_sca"], 1)
                pe.wait_ge(S["v_yacc"], 8 * j + 8)

            expert_pair(0, True)
            with pe.Fori(1, NPAIR) as j:
                expert_pair(j, False)

        @block.scalar
        def _(act):
            a = nc.scalar
            act.dma_start(zft[0:FEMB, :], A["zft"]).then_inc(d_filt, 16)
            act.dma_start(fw1[0:FEMB, :], A["filt_w1"][0]).then_inc(d_filt, 16)
            act.wait_ge(S["g_ms"], 1)
            for n, name in enumerate(("filt_b1", "filt_b2", "filt_b3", "filt_freq")):
                act.dma_start(vr2[R_FB + n:R_FB + n + 1, 0:FH], A[name]).then_inc(d_vec2, 16)
            act.dma_start(fw2[0:FH, :], A["filt_w2"][0]).then_inc(d_filt, 16)
            done = [0]

            def link(ins):
                done[0] += 1
                ins.then_inc(S["a_ch"], 1)
                act.wait_ge(S["a_ch"], done[0])

            act.wait_ge(d_cst, 32)
            for c in range(NLT):
                a.activation(dcy[:, c, :], dlb, ACT.Exp, scale=cst[:, C_TC + c:C_TC + c + 1]).then_inc(S["a_dec"], 1)
            for n in range(6):
                act.wait_ge(S["v_arg"], n + 1)
                h = slice((n % 2) * LC, (n % 2 + 1) * LC)
                if n >= 2:
                    act.wait_ge(S["p_fil"], n + 1)
                a.activation(fh[0:FH, h], fa[0:FH, h], ACT.Sin, scale=TURN).then_inc(S["a_fil"], 1)
            act.wait_ge(S["v_vt"], 2)
            a.activation(mcur[:, 0:16], v1t[:, R_C:R_C + 16], ACT.Tanh, scale=0.5).then_inc(S["a_th"], 1)

            def odd_part(n, p_done, dst, banks, used):
                act.wait_ge(p_done, 2 * n + 1)
                a.activation(dst, B[banks[n][0]][:, :], ACT.Copy).then_inc(used, 1)

            def filter_odd(n):
                odd_part(n, S["p_ksp"], ksp[:, n % 2, n // 2, 1, :], ksp_bank, S["a_ksp"])

            def squares(t):
                if t >= NCT:
                    act.wait_ge(S["v_x"], t - NCT + 1)
                src = cx[:, t, :] if t < NCT else x3[:, t - NCT, :]
                if t:
                    act.wait_ge(S["a_ss"], t)
                a.activation(sq, src, ACT.Square, accum_out=sst[:, t:t + 1]).then_inc(S["a_ss"], 1)

            filter_odd(0)
            act.wait_ge(d_ctx, 16)
            squares(0)
            squares(1)
            filter_odd(1)
            for t in range(NCT, NTT):
                squares(t)
            filter_odd(2)
            act.wait_ge(S["a_ss"], NTT)
            act.wait_ge(S["g_zero"], 4)
            a.activation(std, sst, ACT.Sqrt, scale=1.0 / D, bias=epsc).then_inc(S["a_std"], 1)
            filter_odd(3)
            act.wait_ge(S["v_aff"], 1)
            act.wait_ge(S["v_kf"], len(TAPS))
            for k in range(KD):
                act.wait_ge(S["p_htl"], k + 1)
                a.activation(ht[:, k, LC:], B[htl_bank[k]][:, :], ACT.Identity, scale=aff1[:, 0, 0, k:k + 1],
                             bias=aff1[:, 0, 1, k:k + 1]).then_inc(S["a_htl"], 1)
            act.wait_ge(S["p_gt"], 1)
            a.activation(gt[0:16, LC:], B[0][0:16, :], ACT.Copy).then_inc(S["a_gt"], 1)
            a.activation(gt[0:16, 0:LC], B[0][32:48, 0:LC], ACT.Copy).then_inc(S["a_gt"], 1)
            act.wait_ge(S["v_gsum"], 2)
            link(a.activation(th, th, ACT.Tanh, scale=1.0 / GCAP))
            link(a.activation(lf, th[:, :, :, 4:8], ACT.Exp, scale=-GCAP))
            a.activation(lf, lf, ACT.Ln, bias=1.0).then_inc(S["a_lf"], 1)
            act.wait_ge(S["v_ew"], 1)
            a.activation(ew, ew, ACT.Exp).then_inc(S["a_ew"], 1)
            for m in range(4):
                act.wait_ge(S["p_qk"], m + 1)
                dst = (qt if m < 2 else kt)[:, m % 2, :]
                a.activation(dst, B[qk_bank[m]][:, :], ACT.Copy, scale=DK ** -0.5 if m < 2 else 1.0)\
                    .then_inc(S["a_qk"], 1)
            for i in range(NCH):
                act.wait_ge(S["p_utr"], i + 1)
                a.activation(us[:, :, i * P:(i + 1) * P], B[i % 2][:, :].rearrange("p (c n) -> p c n", c=NLT),
                             ACT.Copy).then_inc(S["a_us"], 1)
            for g in range(2):
                act.wait_ge(S["p_ktr"], g + 1)
                a.activation(kk[:, NCT + 2 * g:NCT + 2 * g + 2, :],
                             B[g][:, :].rearrange("p (c n) -> p c n", c=2), ACT.Copy).then_inc(S["a_ktr"], 1)
            for t in range(NTT):
                if t < NTT - 1:
                    act.wait_ge(S["p_v"], t + 1)
                else:
                    act.wait_ge(S["p_w"], done_count("i", 4))
                a.activation(v1[:, t, :, 0:DV], B[v_bank[t]][:, :].rearrange("p (h n) -> p h n", h=NH),
                             ACT.Copy).then_inc(S["a_v"], 1)
            def decays(h):
                for d in range(2):
                    act.wait_ge(S["v_d"], 2 * h + d + 1)
                    a.activation(ebufs[h % 2][:, d, :], ebufs[h % 2][:, d, :], ACT.Exp, scale=-1.0)\
                        .then_inc(S["a_e"], 1)

            def carried(h):
                for n in range(4 * h, 4 * h + 4):
                    d, cp = divmod(n % 4, 2)
                    act.wait_ge(S["p_num"], n + 1)
                    if n >= 2:
                        act.wait_ge(S["v_hs"], n - 1)
                    for c in (2 * cp, 2 * cp + 1):
                        o = (c % 2) * (DV + 1)
                        r = 32 * d + 4 * step_of(d, NCT + c) + h
                        a.activation(tot[:, n % 2, c % 2, :], B[5 + 2 * (n % 2)][:, o:o + DV + 1], ACT.Copy,
                                     scale=ew[:, 0, r:r + 1]).then_inc(S["a_n2"], 1)

            def head_squares(h):
                act.wait_ge(S["v_hs"], 4 * h + 4)
                if h:
                    act.wait_ge(S["a_hq"], 4 * h)
                for c in range(NLT):
                    a.activation(usq[:, c, :], hsum[:, c, h * DV:(h + 1) * DV], ACT.Square,
                                 accum_out=ssq[:, NH * c + h:NH * c + h + 1]).then_inc(S["a_hq"], 1)

            for n in range(2 * NKC):
                if n == 2:
                    act.wait_ge(S["v_cx"], 1)
                odd_part(n, S["p_usp"], usp[:, n % 2, 1, :], usp_bank, S["a_usp"])
            act.wait_ge(S["p_st"], 10)
            for c in range(NLT):
                if c < NLT - 1:
                    act.wait_ge(S["p_o"], c + 1)
                else:
                    act.wait_ge(S["p_w"], done_count("i", 5))
                a.activation(og[:, c, :], B[o_bank[c]][:, :], ACT.Tanh, scale=0.5).then_inc(S["a_o"], 1)
                if c == 1:
                    decays(0)
            decays(1)
            for h in range(NH):
                carried(h)
                head_squares(h)
                if h + 2 < NH:
                    decays(h + 2)
            act.wait_ge(S["a_hq"], NLT * NH)
            a.activation(ssq, ssq, ACT.Sqrt, scale=1.0 / DV, bias=epsc).then_inc(S["a_sq"], 1)
            for c in range(NLT):
                act.wait_ge(S["p_ytr"], c + 1)
                for h in range(NH):
                    x = a.activation(ymt[:, h, c * P:(c + 1) * P], B[6 + c % 2][:, h * P:(h + 1) * P], ACT.Copy,
                                     scale=v2t[:, R_MLN + h:R_MLN + h + 1])
                x.then_inc(S["a_yt"], 1)

            def x1_half(c):
                act.wait_ge(S["p_h2"], 2 * c + 2)
                a.activation(x1t[:, 4:8, c * P:(c + 1) * P], B[2 * (c % 2) + 1][:, :].rearrange("p (k t) -> p k t", k=4),
                             ACT.Copy).then_inc(S["a_h2"], 1)

            for c in range(NLT):
                for half in range(2):
                    if c < NLT - 1:
                        act.wait_ge(S["p_y"], 2 * c + half + 1)
                    else:
                        act.wait_ge(S["p_w"], len(DONE) - 1 + half)
                    link(a.activation(junk[:, 0:CH], B[2 * c + half][:, :], ACT.Square,
                                      accum_out=(sy if half else sst)[:, c:c + 1]))
                a.activation(sy[:, c:c + 1], sy[:, c:c + 1], ACT.Identity, bias=sst[:, c:c + 1]).then_inc(S["a_sy"], 1)
                act.wait_ge(S["a_sy"], c + 1)
                a.activation(sdy[:, c:c + 1], sy[:, c:c + 1], ACT.Sqrt, scale=1.0 / D, bias=epsc).then_inc(S["a_sdy"], 1)
                act.wait_ge(S["v_x1"], 2 * c + 2)
                link(a.activation(junk, x3[:, c, :], ACT.Square, accum_out=ss2[:, c:c + 1]))
                a.activation(sd2[:, c:c + 1], ss2[:, c:c + 1], ACT.Sqrt, scale=1.0 / D, bias=epsc).then_inc(S["a_ss2"], 1)
                if 1 <= c < 3:
                    x1_half(c - 1)
                if c == 2:
                    x1_half(2)
            x1_half(NLT - 1)
            act.wait_ge(S["v_sub"], 1)
            a.activation(lg, lg, ACT.Exp).then_inc(S["a_exp"], 1)

            with act.Fori(0, NPAIR) as j:
                act.wait_ge(S["p_xs"], 2 * j + 2)
                for k in range(4):
                    a.activation(xst[:, 4 + k, :], B[7][:, k * P:(k + 1) * P], ACT.Identity,
                                 scale=aff2[:, 0, 4 + k:5 + k], bias=aff2[:, 1, 4 + k:5 + k]).then_inc(S["a_xs"], 1)

                def silu(st):
                    act.wait_ge(S["p_gu"], 8 * j + st + 1)
                    if st >= 2:
                        act.wait_ge(S["v_hid"], 8 * j + st - 1)
                    a.activation(sil[CAP:P, st % 2, :], B[st % 2][0:CAP, :], ACT.Silu).then_inc(S["a_sil"], 1)

                def results(e2):
                    act.wait_ge(S["p_dn"], 8 * j + 4 * e2 + 4)
                    for half in range(2):
                        a.activation(ye[CAP * e2:CAP * (e2 + 1), half * CH:(half + 1) * CH],
                                     B[4 + e2][CAP * half:CAP * (half + 1), :], ACT.Copy).then_inc(S["a_ye"], 1)

                silu(0)
                silu(1)
                act.wait_ge(S["p_pwt"], j + 1)
                a.activation(pwt, B[6][:, :].rearrange("p (c n) -> p c n", c=NLT), ACT.Copy).then_inc(S["a_pwt"], 1)
                for st in range(2, 5):
                    silu(st)
                results(0)
                for st in range(5, 8):
                    silu(st)
                results(1)
            for c in range(NLT):
                act.wait_ge(S["v_yacc"], 8 * (NPAIR - 1) + 2 * c + 2)
                link(a.activation(xst[:, :, :].rearrange("p k n -> p (k n)"), y3[:, c, :], ACT.Square,
                                  accum_out=ss2[:, c:c + 1]))
                a.activation(sd2[:, c:c + 1], ss2[:, c:c + 1], ACT.Sqrt, scale=1.0 / D, bias=epsc).then_inc(S["a_fsd"], 1)
            act.wait_ge(S["v_ry"], 1)
            a.activation(y3[:, 0, :], y3[:, 0, :], ACT.Copy, scale=ry[:, 0:1]).then_inc(S["a_y0"], 1)

        @block.vector
        def _(dve):
            v = nc.vector
            done = [0]

            def link(ins):
                done[0] += 1
                ins.then_inc(S["v_ch"], 1)
                dve.wait_ge(S["v_ch"], done[0])

            def stt(out_, in0, sc, in1, op0, op1):
                return v.scalar_tensor_tensor(out=out_, in0=in0, scalar=sc, in1=in1, op0=op0, op1=op1)

            dve.wait_ge(d_taps, 48)
            v.tensor_tensor(fws[0:FH, 0, :], fw4[0:FH, 0:HY], fw4[0:FH, HY:2 * HY], ALU.add).then_inc(S["v_fws"], 1)
            v.tensor_tensor(fws[0:FH, 1, :], fw4[0:FH, 0:HY], fw4[0:FH, HY:2 * HY], ALU.subtract).then_inc(S["v_fws"], 1)
            dve.wait_ge(S["p_vt"], 1)
            v.tensor_copy(v2t, B[1][:, 0:R2_ROWS]).then_inc(S["v_vt"], 1)
            dve.wait_ge(S["v_vt"], 1)
            link(v.tensor_scalar(fqt, v2t[0:FH, R_FQ:R_FQ + 1], 1.0 / TWO_PI, None, ALU.mult))
            for n in range(6):
                h = slice((n % 2) * LC, (n % 2 + 1) * LC)
                dve.wait_ge(S["p_fil"], n + 1)
                src = B[2 + n % 2][0:FH, (n // 2 % 2) * LC:(n // 2 % 2 + 1) * LC]
                if n >= 2:
                    dve.wait_ge(S["a_fil"], n - 1)
                link(v.tensor_scalar(ft[0:FH, h], src, v2t[0:FH, R_FB + n // 2:R_FB + n // 2 + 1], fqt, ALU.add, ALU.mult))
                link(v.tensor_scalar(fa[0:FH, h], ft[0:FH, h], MAGIC, MAGIC, ALU.add, ALU.subtract))
                v.tensor_tensor(fa[0:FH, h], ft[0:FH, h], fa[0:FH, h], ALU.subtract).then_inc(S["v_arg"], 1)
                if n == 1:
                    dve.wait_ge(S["p_vt"], 2)
                    v.tensor_copy(v1t, B[0][:, 0:R1_ROWS]).then_inc(S["v_vt"], 1)
            dve.wait_ge(S["a_dec"], NLT)
            for n, (w, c) in enumerate(TAPS):
                dve.wait_ge(S["p_kf"], n + 1)
                v.tensor_tensor(hpm[:, w, c, :], B[4 + n % 4][:, :], dcy[:, c, :], ALU.mult).then_inc(S["v_kf"], 1)
                if n == 1:
                    dve.wait_ge(S["v_kf"], 2)
                    z = hpm[0:1, 0, 0, :]
                    link(v.tensor_tensor(z, z, hpm[0:1, 1, 0, :], ALU.add))
                    stt(z, z, 0.5, hyb[0:1, :], ALU.mult, ALU.add).then_inc(S["v_hpm"], 1)
            dve.wait_ge(S["a_th"], 1)
            dve.wait_ge(S["g_zero"], 3)
            link(stt(mcur[:, 16:32], mcur[:, 0:16], 1.0, v1t[:, R_C:R_C + 16], ALU.add, ALU.mult))
            v.tensor_scalar(cpad[:, :, 0:2], mcur[:, 16:32].rearrange("p (w k) -> p k w", w=2), 0.5, None,
                            ALU.mult).then_inc(S["v_cpad"], 1)
            dve.wait_ge(d_x, 16)
            dve.wait_ge(d_pos, 16)
            for c in range(NLT):
                v.tensor_tensor(x3[:, c, :], x3[:, c, :], xn[:, c, :], ALU.add).then_inc(S["v_x"], 1)
            def parts(n, p_done, lo, hi, banks, odd_used, used):
                dve.wait_ge(p_done, 2 * n + 2)
                dve.wait_ge(odd_used, n + 1)
                even = B[banks[n][1]][:, :]
                link(v.tensor_tensor(lo, even, hi, ALU.add))
                v.tensor_tensor(hi, even, hi, ALU.subtract).then_inc(used, 1)

            def filter_parts(n):
                parts(n, S["p_ksp"], ksp[:, n % 2, n // 2, 0, :], ksp[:, n % 2, n // 2, 1, :], ksp_bank, S["a_ksp"], S["v_ksp"])

            for n in range(3):
                filter_parts(n)
            dve.wait_ge(S["a_std"], 1)
            link(v.reciprocal(rst, std))
            dve.wait_ge(S["v_x"], NLT)
            for t in range(NTT):
                src = cx[:, t, :] if t < NCT else x3[:, t - NCT, :]
                dst = cx[:, t, :] if t < NCT else xn[:, t - NCT, :]
                v.tensor_scalar(dst, src, rst[:, t:t + 1], None, ALU.mult).then_inc(S["v_xn"], 1)

            def mod_rows(r):
                if r < 3:
                    dve.wait_ge(S["p_w"], done_count("m", 4 * r + 3))
                    if r:
                        dve.wait_ge(S["p_modt"], r)
                    if r == 2:
                        dve.wait_ge(S["p_g1"], 2)
                    v.tensor_copy(mrow, B[2][:, :]).then_inc(S["v_mrow"], 1)

            def turned(b, i0, w):
                return B[b][:, :].rearrange("p (q i u) -> p i q u", q=4, i=4)[:, i0:i0 + 2, :, w]

            def two(apx):
                return apx.rearrange("p (i q) -> p i q", i=2)

            filter_parts(3)
            mod_rows(0)
            dve.wait_ge(S["p_modt"], 1)
            for w in range(2):
                link(v.tensor_tensor(two(aff1[:, w, 0, :]), turned(1, 2, w), two(v1t[:, R_BMOD + 8:R_BMOD + 16]), ALU.add))
                link(stt(aff1[:, w, 0, :], aff1[:, w, 0, :], 1.0, v1t[:, R_PRE1:R_PRE1 + 8], ALU.add, ALU.mult))
                x = v.tensor_tensor(two(aff1[:, w, 1, :]), turned(1, 0, w), two(v1t[:, R_BMOD:R_BMOD + 8]), ALU.add)
                link(x) if w == 0 else x.then_inc(S["v_aff"], 1)
            dve.wait_ge(S["v_aff"], 1)
            for k in range(KD):
                dve.wait_ge(S["p_htc"], k + 1)
                v.tensor_scalar(ht[:, k, 0:LC], B[htc_bank[k]][:, 0:LC], aff1[:, 1, 0, k:k + 1],
                                aff1[:, 1, 1, k:k + 1], ALU.mult, ALU.add).then_inc(S["v_htc"], 1)

            dve.wait_ge(S["p_ksp"], 4 * NKC)
            link(v.memset(v1[:, :, :, DV:DV + 1], 1.0))
            link(v.memset(ew, 0.0))
            link(v.memset(aco, 0.0))
            link(v.memset(atp, -BIG))
            link(v.memset(mprev, 0.0))
            link(v.memset(mend, 0.0))

            def conv(n):
                i, m = divmod(n, NCH)
                if m < NCH - 1:
                    dve.wait_ge(S["p_hy"], 3 * i + m + 1)
                else:
                    dve.wait_ge(S["p_w"], done_count("i", i))
                src = B[hy_bank[n]]
                dst = (x0t[:, m, :], ut[:, m, :], ctmp[:, m % 2, :])[i]
                w = [v2t[:, R_CW + 12 * s + n:R_CW + 12 * s + n + 1] for s in range(3)]
                link(v.tensor_scalar(dst, src[:, :], w[1], v2t[:, R_CB + n:R_CB + n + 1], ALU.mult, ALU.add))
                link(stt(dst[:, 1:L], src[:, 0:L - 1], w[0], dst[:, 1:L], ALU.mult, ALU.add))
                x = stt(dst[:, 0:L - 1], src[:, 1:L], w[2], dst[:, 0:L - 1], ALU.mult, ALU.add)
                if i < 2:
                    x.then_inc(S["v_conv"], 1)
                else:
                    link(x)
                    v.tensor_tensor(ut[:, m, :], ut[:, m, :], dst, ALU.mult).then_inc(S["v_conv"], 1)

            for n in range(4):
                conv(n)
            dve.wait_ge(S["p_gtr"], 1)
            dve.wait_ge(d_gate, 32)
            for d in range(2):
                o = d * NTT * 16
                src = B[1][:, o:o + NTT * 16].rearrange("p (s n) -> p s n", s=NTT)[:, :, 8 * d:8 * d + 8]
                bias = gb[:, 8 * d:8 * d + 8].unsqueeze(1).broadcast_to([P, NTT, 8])
                v.tensor_tensor(th[:, d, :, :], src, bias, ALU.add).then_inc(S["v_gsum"], 1)
            for n in range(4, 8):
                conv(n)
            dve.wait_ge(S["p_cs"], 1)

            def packed(apx):
                return apx.rearrange("p (d n) -> p d n", d=2)[:, :, 0:24]
            link(v.tensor_copy(packed(ew[:, 1, :]), packed(B[0][:, 0:64])))
            link(v.tensor_copy(packed(ew[:, 3, :]), packed(B[0][:, 64:128])))
            for d in range(2):
                x = stt(aco[:, 32 * d:32 * d + 24], th[:, d, :, 0:4], GCAP, ew[:, 1, 32 * d:32 * d + 24]
                        .rearrange("p (s h) -> p s h", s=NTT), ALU.mult, ALU.add)
                link(x) if d == 0 else x.then_inc(S["v_cs"], 1)
            conv(8)
            dve.wait_ge(S["p_at"], 1)
            v.tensor_copy(atp[0:64, 0, 64:192], B[1][0:64, 0:P]).then_inc(S["v_at"], 1)
            dve.wait_ge(S["v_at"], 1)
            for n in range(7):
                s = 1 << n
                src, dst = atp[:, n % 2, :], atp[:, 1 - n % 2, :]
                link(v.tensor_tensor(dst[0:32, 64:192], src[0:32, 64:192], src[0:32, 64 - s:192 - s], ALU.max))
                link(v.tensor_tensor(dst[32:64, 64:192], src[32:64, 64:192], src[32:64, 64 + s:192 + s], ALU.max))
            link(v.tensor_copy(mrow_t[0:32, 0:1], atp[0:32, 1, 191:192]))
            v.tensor_copy(mrow_t[32:64, 0:1], atp[32:64, 1, 64:65]).then_inc(S["v_cum"], 1)
            for n in range(9, 12):
                conv(n)
            dve.wait_ge(S["p_cm"], 1)

            def by_dir(t, s):
                return t.rearrange("p (d n) -> p d n", d=2)[:, :, 4 * s:4 * s + 4]

            for s in range(NTT):
                link(v.tensor_tensor(by_dir(mend, s), by_dir(mprev, s), by_dir(B[0][:, 64:128], s), ALU.max))
                if s + 1 < NTT:
                    link(v.tensor_tensor(by_dir(mprev, s + 1), by_dir(mend, s), by_dir(ew[:, 3, :], s), ALU.subtract))
            v.tensor_tensor(mcur, B[0][:, 0:64], mprev, ALU.max).then_inc(S["v_m"], 1)
            dve.wait_ge(S["v_m"], 1)
            link(v.tensor_tensor(ew[:, 0, :], mprev, mcur, ALU.subtract))
            link(v.tensor_tensor(ew[:, 1, :], ew[:, 1, :], mcur, ALU.subtract))
            link(v.tensor_tensor(ew[:, 2, :], aco, mend, ALU.subtract))
            v.tensor_tensor(ew[:, 3, :], mprev, mend, ALU.subtract).then_inc(S["v_ew"], 1)
            dve.wait_ge(S["p_mt"], 1)
            v.tensor_copy(mrow_t[0:64, :], B[1][0:64, 0:P]).then_inc(S["v_mt"], 1)
            dve.wait_ge(S["a_ew"], 1)
            for p in range(2):
                q = slice(64 * p, 64 * p + 64)
                src = ew[q, 3, :].rearrange("p (d n) -> p d n", d=2)[:, :, p:24:2]
                x = v.tensor_copy(wcp[q, :].rearrange("p (d n) -> p d n", d=2), src)
                link(x)
            for c in range(NCT):
                if c < NCT - 1:
                    dve.wait_ge(S["p_kc"], c + 1)
                else:
                    dve.wait_ge(S["p_w"], done_count("i", 3))
                v.tensor_copy(kk[:, c, :], B[kc_bank[c]][:, 0:QK]).then_inc(S["v_kc"], 1)

            def gate_row(g):
                dve.wait_ge(S["p_modt"], g + 2)
                dve.wait_ge(d_row, 64)
                dve.wait_ge(S["v_mrow"], g + 2)
                link(v.tensor_tensor(mrow, mrow, brow, ALU.add))
                v.tensor_tensor(mrow, mrow, prow, ALU.mult).then_inc(S["v_grow"], 1)
                for h in range(2):
                    dve.wait_ge(S["p_g1"], 2 * g + h + 1)
                    v.tensor_copy((g1p, g2p)[g][:, h * CH:(h + 1) * CH], B[6 * g + h][:, :]).then_inc(S["v_cp"], 1)

            mod_rows(1)
            dve.wait_ge(S["p_modt"], 2)
            v.tensor_tensor(two(aff2[:, 1, :]), turned(1, 2, 0), two(v1t[:, R_BMOD + 24:R_BMOD + 32]),
                            ALU.add).then_inc(S["v_aff"], 1)
            gate_row(0)
            def states(n0, n1):
                for n in range(n0, n1):
                    st, d = divmod(n, 2)
                    dve.wait_ge(S["p_st"], n + 1)
                    if n >= 2:
                        dve.wait_ge(S["v_st"], n - 1)
                    for p in range(2):
                        o = slice(p * (DV + 1), (p + 1) * (DV + 1))
                        src = B[n % 2][:, o]
                        if st == 0:
                            x = v.tensor_copy(cstate[:, d, 0, o], src)
                        else:
                            q = d * 12 + 2 * st + p
                            x = stt(cstate[:, d, st - 1, o], cstate[:, d, max(st - 2, 0), o], wcp[:, q:q + 1], src,
                                    ALU.mult, ALU.add)
                        link(x) if p == 0 else x.then_inc(S["v_st"], 1)

            def product_parts(n):
                parts(n, S["p_usp"], usp[:, n % 2, 0, :], usp[:, n % 2, 1, :], usp_bank, S["a_usp"], S["v_usp"])

            def spectra_product(k):
                dve.wait_ge(S["v_usp"], 2 * k + 2)
                ur, ui = (usp[:, w, :, :].rearrange("p j n -> p (j n)") for w in range(2))
                kr, ki = (ksp[:, w, k, :, :].rearrange("p j n -> p (j n)") for w in range(2))
                link(v.tensor_tensor(cprod[0], ur, kr, ALU.mult))
                link(v.tensor_tensor(cprod[1], ui, ki, ALU.mult))
                link(v.tensor_tensor(kr, ui, kr, ALU.mult))
                link(v.tensor_tensor(ki, ur, ki, ALU.mult))
                link(v.tensor_tensor(ur, cprod[0], cprod[1], ALU.subtract))
                link(v.tensor_tensor(ui, kr, ki, ALU.add))
                link(v.tensor_tensor(ksp[:, :, k, 0, :], usp[:, :, 0, :], usp[:, :, 1, :], ALU.add))
                v.tensor_tensor(ksp[:, :, k, 1, :], usp[:, :, 0, :], usp[:, :, 1, :], ALU.subtract).then_inc(S["v_cx"], 1)

            states(0, 4)
            product_parts(0)
            states(4, 8)
            product_parts(1)
            states(8, 10)
            spectra_product(0)
            product_parts(2)
            product_parts(3)
            spectra_product(1)

            def weights_of(h):
                for d in range(2):
                    dve.wait_ge(S["p_mb"], 2 * h + d + 1)
                    if h >= 2:
                        dve.wait_ge(S["p_num"], 4 * (h - 2) + 2 * d + 2)
                    for c in range(NLT):
                        r = 32 * d + 4 * step_of(d, NCT + c) + h
                        x = stt(ebufs[h % 2][:, d, c * P:(c + 1) * P], B[mb_bank(h, d)][:, c * P:(c + 1) * P], aco[:, r:r + 1],
                                cst[:, (C_BF, C_BB)[d]:(C_BF, C_BB)[d] + P], ALU.subtract, ALU.max)
                    x.then_inc(S["v_d"], 1)

            def times_scores(h):
                dve.wait_ge(S["p_sc"], h + 1)
                for d in range(2):
                    dve.wait_ge(S["a_e"], 2 * h + d + 1)
                    v.tensor_tensor(ebufs[h % 2][:, d, :], ebufs[h % 2][:, d, :], B[score_bank(h)][:, :], ALU.mult).then_inc(S["v_sw"], 1)
            for h in range(2):
                weights_of(h)
                times_scores(h)
            mod_rows(2)

            def x1_half(c):
                dve.wait_ge(S["p_h2"], 2 * c + 1)
                v.tensor_copy(x1t[:, 0:4, c * P:(c + 1) * P], B[2 * (c % 2)][:, :].rearrange("p (k t) -> p k t", k=4))\
                    .then_inc(S["v_h2"], 1)

            def hyena_out(i):
                dve.wait_ge(S["p_inv"], i + 1)
                by_parity = x0t[:, i, :].rearrange("p (t w) -> p w t", w=2)
                v.tensor_tensor(by_parity, by_parity, B[INV_BANK[i]][:, :].rearrange("p (w t) -> p w t", w=2), ALU.mult)\
                    .then_inc(S["v_inv"], 1)

            def head(h):
                for n in range(4 * h, 4 * h + 4):
                    d, cp = divmod(n % 4, 2)
                    dve.wait_ge(S["a_n2"], 2 * n + 2)
                    t = tot[:, n % 2, :, :]
                    v.tensor_tensor(t, t, B[4 + 2 * (n % 2)][:, 0:2 * (DV + 1)].rearrange("p (c n) -> p c n", c=2),
                                    ALU.add).then_inc(S["v_tot"], 1)
                    dve.wait_ge(S["v_tot"], n + 1)
                    r = [32 * d + 4 * step_of(d, NCT + 2 * cp + c) + h for c in range(2)]
                    em = ew[:, 1, r[0]:r[0] + 5:4] if r[1] > r[0] else ew[:, 1, r[1]:r[1] + 5:4][:, ::-1]
                    dd = dab[:, n % 4, :].unsqueeze(2)
                    link(v.tensor_tensor(dd, t[:, :, DV:DV + 1], em.unsqueeze(2), ALU.max))
                    link(stt(dd, t[:, :, DV:DV + 1], -1.0, dd, ALU.mult, ALU.max))
                    link(v.reciprocal(dab[:, n % 4, :], dab[:, n % 4, :]))
                    rb = dab[:, n % 4, :].unsqueeze(2).broadcast_to([P, 2, DV])
                    dst = hsum[:, 2 * cp:2 * cp + 2, h * DV:(h + 1) * DV]
                    if d == 0:
                        v.tensor_tensor(dst, t[:, :, 0:DV], rb, ALU.mult).then_inc(S["v_hs"], 1)
                    else:
                        link(v.tensor_tensor(t[:, :, 0:DV], t[:, :, 0:DV], rb, ALU.mult))
                        v.tensor_tensor(dst, dst, t[:, :, 0:DV], ALU.add).then_inc(S["v_hs"], 1)

            head(0)
            hyena_out(0)
            weights_of(2)
            times_scores(2)
            head(1)
            hyena_out(1)
            weights_of(3)
            times_scores(3)
            head(2)
            hyena_out(2)
            hyena_out(3)
            head(3)
            link(v.tensor_scalar(v2t[:, R_MLN:R_MLN + NH], v2t[:, R_MLN:R_MLN + NH], 0.5, None, ALU.mult))
            dve.wait_ge(S["a_sq"], 1)
            link(v.reciprocal(ssq, ssq))
            for c in range(NLT):
                hc = hsum[:, c, :].rearrange("p (h n) -> p h n", h=NH)
                link(v.tensor_tensor(hc, hc, ssq[:, 4 * c:4 * c + 4].unsqueeze(2).broadcast_to([P, NH, DV]), ALU.mult))
                stt(hsum[:, c, :], og[:, c, :], 1.0, hsum[:, c, :], ALU.add, ALU.mult).then_inc(S["v_hn"], 1)
            dve.wait_ge(S["p_modt"], 3)
            link(v.tensor_tensor(two(aff2[:, 0, :]), turned(6, 0, 0), two(v1t[:, R_BMOD + 32:R_BMOD + 40]), ALU.add))
            stt(aff2[:, 0, :], aff2[:, 0, :], 1.0, v1t[:, R_PRE2:R_PRE2 + 8], ALU.add, ALU.mult).then_inc(S["v_aff"], 1)
            gate_row(1)

            for c in range(NLT):
                dve.wait_ge(S["a_sdy"], c + 1)
                link(v.reciprocal(ry[:, c:c + 1], sdy[:, c:c + 1]))
                for half in range(2):
                    h = slice(half * CH, (half + 1) * CH)
                    t = ctmp[:, half, :]
                    link(stt(t, B[2 * c + half][:, :], ry[:, c:c + 1], g1p[:, h], ALU.mult, ALU.mult))
                    v.tensor_tensor(x3[:, c, h], x3[:, c, h], t, ALU.add).then_inc(S["v_x1"], 1)
                dve.wait_ge(S["a_ss2"], c + 1)
                link(v.reciprocal(rs2[:, c:c + 1], sd2[:, c:c + 1]))
                if c == 0:
                    dve.wait_ge(d_wr, 16)
                    v.tensor_tensor(wra, wr, aff2[:, 0, :].unsqueeze(2).broadcast_to([P, KD, E]), ALU.mult)\
                        .then_inc(S["v_wra"], 1)
                if 1 <= c < 3:
                    x1_half(c - 1)
                if c == 2:
                    x1_half(2)
            x1_half(NLT - 1)
            dve.wait_ge(S["p_lg"], NLT)
            v.tensor_copy(lgt[0:E, :], B[4][0:E, :]).then_inc(S["v_lgt"], 1)
            dve.wait_ge(S["p_lgt"], 1)
            l5 = B[5][:, 0:NLT * E].rearrange("p (c e) -> p c e", c=NLT)
            link(v.tensor_tensor(lg, l5, rs2.unsqueeze(2).broadcast_to([P, NLT, E]), ALU.mult))
            shift = B[5][:, NLT * E:(NLT + 1) * E].unsqueeze(1).broadcast_to([P, NLT, E])
            link(v.tensor_tensor(lg, lg, shift, ALU.add))
            link(v.tensor_reduce(mx4, lg, AX.X, ALU.max))
            v.tensor_tensor(lg, lg, mx4.unsqueeze(2).broadcast_to([P, NLT, E]), ALU.subtract).then_inc(S["v_sub"], 1)
            dve.wait_ge(S["a_exp"], 1)
            link(v.tensor_reduce(sm4, lg, AX.X, ALU.add))
            link(v.reciprocal(rc4, sm4))
            v.tensor_tensor(aft, lg, rc4.unsqueeze(2).broadcast_to([P, NLT, E]), ALU.mult).then_inc(S["v_aft"], 1)
            dve.wait_ge(S["v_aft"], 1)
            v.tensor_copy(affr, aft.rearrange("p c e -> p e c")).then_inc(S["v_slot"], 1)
            dve.wait_ge(S["p_aft"], 1)
            link(v.tensor_copy(lgt[0:E, :], B[6][0:E, :]))
            cur = lgt
            for r in range(CAP // 8):
                nxt = wka if r % 2 == 0 else wkb
                link(v.max(out=top8[0:E, :], in_=cur[0:E, :]))
                link(v.match_replace(out=nxt[0:E, :], in_to_replace=top8[0:E, :], in_values=cur[0:E, :], imm_value=-1.0))
                cur = nxt
            v.tensor_tensor(wka[0:E, :], cur[0:E, :], lgt[0:E, :], ALU.not_equal).then_inc(S["v_mk"], 1)
            dve.wait_ge(S["p_mk"], 1)
            v.tensor_copy(mkt, B[7][:, 0:NLT * E].rearrange("p (c e) -> p c e", c=NLT)).then_inc(S["v_mkt"], 1)
            dve.wait_ge(S["p_rk"], 1)
            sl = slotm.rearrange("p e c -> p c e")
            link(v.tensor_tensor(sl, B[0][:, 0:NLT * E].rearrange("p (c e) -> p c e", c=NLT), mkt, ALU.mult))
            v.tensor_scalar(slotm, slotm, -1.0, None, ALU.add).then_inc(S["v_slot"], 1)

            dve.wait_ge(S["v_slot"], 2)

            with dve.Fori(0, NPAIR) as j:
                v.tensor_copy(slp, slotm[:, bass.ds(2 * j, 2), :].rearrange("p e c -> p (e c)")).then_inc(S["v_sel"], 1)
                dve.wait_ge(S["v_sel"], 4 * j + 1)
                for e2 in range(2):
                    io = cst[:, C_IO:C_IO + CAP].unsqueeze(1).broadcast_to([P, NLT, CAP])
                    sl = slp[:, 4 * e2:4 * e2 + 4].unsqueeze(2).broadcast_to([P, NLT, CAP])
                    v.tensor_tensor(peq[:, :, CAP * e2:CAP * e2 + CAP], io, sl, ALU.is_equal).then_inc(S["v_sel"], 1)
                dve.wait_ge(S["v_sel"], 4 * j + 3)
                v.tensor_tensor(psel, peq, rs2.unsqueeze(2).broadcast_to([P, NLT, P]), ALU.mult)\
                    .then_inc(S["v_sel"], 1)
                dve.wait_ge(S["p_xs"], 2 * j + 1)
                for k in range(4):
                    v.tensor_scalar(xst[:, k, :], B[6][:, k * P:(k + 1) * P], aff2[:, 0, k:k + 1], aff2[:, 1, k:k + 1],
                                    ALU.mult, ALU.add).then_inc(S["v_xs"], 1)

                def hidden(st):
                    dve.wait_ge(S["a_sil"], 8 * j + st + 1)
                    if st >= 2:
                        dve.wait_ge(S["p_ht"], 8 * j + st - 1)
                    v.tensor_tensor(hid[CAP:P, st % 2, :], sil[CAP:P, st % 2, :], B[st % 2][CAP:P, :],
                                    ALU.mult).then_inc(S["v_hid"], 1)

                def turned_hidden(st):
                    dve.wait_ge(S["p_ht"], 8 * j + st + 1)
                    if st >= 2:
                        dve.wait_ge(S["p_dn"], 8 * j + st - 1)
                    v.tensor_copy(hdt[:, st % 2, :].rearrange("p (k n) -> p k n", k=4),
                                  B[2 + st % 2][:, :].rearrange("p (k n) -> p k n", k=4)[:, :, CAP:P])\
                        .then_inc(S["v_hdt"], 1)

                hidden(0)
                hidden(1)
                turned_hidden(0)
                for st in range(2, 8):
                    hidden(st)
                    turned_hidden(st - 1)
                turned_hidden(7)
                dve.wait_ge(S["g_ms"], 3)
                for n in range(2 * NLT):
                    c, half = divmod(n, 2)
                    dve.wait_ge(S["p_sca"], 8 * j + n + 1)
                    dst = y3[:, c, half * CH:(half + 1) * CH]
                    v.tensor_tensor(dst, dst, B[6 + half][:, :], ALU.add).then_inc(S["v_yacc"], 1)
            dve.wait_ge(S["a_fsd"], 1)
            v.reciprocal(ry[:, 0:1], sd2[:, 0:1]).then_inc(S["v_ry"], 1)
            for c in range(1, NLT):
                dve.wait_ge(S["a_fsd"], c + 1)
                link(v.reciprocal(ry[:, c:c + 1], sd2[:, c:c + 1]))
                dve.wait_ge(S["v_yacc"], 8 * NPAIR)
                link(stt(y3[:, c, :], y3[:, c, :], ry[:, c:c + 1], g2p[:, :], ALU.mult, ALU.mult))
                v.tensor_tensor(y3[:, c, :], y3[:, c, :], x3[:, c, :], ALU.add).then_inc(S["v_res"], 1)


NAMES = ["x", "c", "ctx", "c_ctx", "w_mod", "b_mod", "pre_norm1", "post_norm1", "pre_norm2", "post_norm2",
         "w_in", "conv_w", "conv_b", "filt_w1", "filt_b1", "filt_w2", "filt_b2", "filt_w3", "filt_b3", "filt_w4",
         "filt_freq", "hyena_bias", "ml_gate_b", "ml_norm", "w_out", "w_router", "w_exp_gate", "w_exp_up",
         "w_exp_down"]


def kernel(**inputs):
    import concourse.bacc as bacc
    from concourse.bass_utils import run_bass_kernel_spmd

    nc = bacc.Bacc("TRN2", target_bir_lowering=False, num_devices=1)
    arrays = {n: np.ascontiguousarray(inputs[n]) for n in NAMES}
    arrays.update(shape_constants())
    A = {n: nc.dram_tensor(f"in_{n}", a.shape, mybir.dt.from_np(a.dtype), kind="ExternalInput").ap()
         for n, a in arrays.items()}
    out = nc.dram_tensor("out", (1, L, D), F32, kind="ExternalOutput").ap()
    block_kernel(nc, A, out)
    r = run_bass_kernel_spmd(nc, [{f"in_{n}": a for n, a in arrays.items()}], core_ids=[0])
    return r.results[0]["out"]
```
